# Optimizing a Trainium2 kernel written in Bass

```python
import jax, jax.numpy as jnp
from jax import lax
import numpy as np
import math

D_MODEL = 1024
BATCH = 1
SEQ = 1024
DEPTH = 1

CHUNK = 64
CONV_WIDTH = 3
CONV_DIM = D_MODEL // 2
CONV_GROUPS = 8
RET_HEADS = 4
RET_DIM = D_MODEL - CONV_DIM
RET_HEAD_DIM = RET_DIM // RET_HEADS
MIX_DIM = CONV_DIM + RET_DIM
IN_DIM = 3 * CONV_DIM + 4 * RET_DIM
D_FF = 4 * D_MODEL
ROPE_BASE = 10000.0
DECAY_OFFSET = 5.0
EPS = 1e-6
N_MOD = 6


def rms_norm(x, g):
    xf = x.astype(jnp.float32)
    y = xf * lax.rsqrt(jnp.mean(xf * xf, axis=-1, keepdims=True) + EPS)
    return (y * g.astype(jnp.float32)).astype(x.dtype)

def rotary(t, positions):
    half = t.shape[-1] // 2
    inv_freq = ROPE_BASE ** (-jnp.arange(half, dtype=jnp.float32) / half)
    ang = positions.astype(jnp.float32)[..., None] * inv_freq
    cos = jnp.cos(ang)[:, :, None, :]
    sin = jnp.sin(ang)[:, :, None, :]
    tf = t.astype(jnp.float32)
    t1, t2 = tf[..., :half], tf[..., half:]
    out = jnp.concatenate([t1 * cos - t2 * sin, t2 * cos + t1 * sin], axis=-1)
    return out.astype(t.dtype)

def short_conv_mixer(xin, b_gate, c_gate, conv_w):
    S = xin.shape[1]
    u = c_gate * xin
    up = jnp.pad(u, ((0, 0), (CONV_WIDTH - 1, 0), (0, 0)))
    y = up[:, 0:S] * conv_w[0]
    for j in range(1, CONV_WIDTH):
        y = y + up[:, j:j + S] * conv_w[j]
    return b_gate * y

def retention_mixer(q, k, v, g, positions):
    B, S, _ = q.shape
    H, dh, C = RET_HEADS, RET_HEAD_DIM, CHUNK
    NC = S // C
    dt = q.dtype
    q = rotary(q.reshape(B, S, H, dh), positions)
    k = rotary(k.reshape(B, S, H, dh), positions) * (dh ** -0.5)
    v = v.reshape(B, S, H, dh)

    def to_chunks(t):
        return t.reshape(B, NC, C, H, dh).transpose(0, 3, 1, 2, 4)

    q, k, v = to_chunks(q), to_chunks(k), to_chunks(v)

    log_gamma = jnp.log1p(-jnp.exp2(-DECAY_OFFSET - jnp.arange(H, dtype=jnp.float32)))
    idx = jnp.arange(C, dtype=jnp.float32)
    intra_dec = jnp.exp(log_gamma[:, None, None] * jnp.abs(idx[:, None] - idx[None, :]))
    q_dec = jnp.exp(log_gamma[:, None] * (idx + 1.0))
    k_dec = jnp.exp(log_gamma[:, None] * (C - 1.0 - idx))
    chunk_dec = jnp.exp(log_gamma * C)

    scores = jnp.einsum('bhncd,bhnmd->bhncm', q, k) * intra_dec[:, None].astype(dt)
    o_intra = jnp.einsum('bhncm,bhnmd->bhncd', scores, v)

    kv = jnp.einsum('bhnmd,bhnme->nbhde', k * k_dec[:, None, :, None].astype(dt), v)
    kv = kv.astype(jnp.float32)

    def step(state, kv_n):
        return state * chunk_dec[:, None, None] + kv_n, state

    _, s_prev = lax.scan(step, jnp.zeros((B, H, dh, dh), jnp.float32), kv)
    o_cross = jnp.einsum('bhncd,nbhde->bhnce',
                         q * q_dec[:, None, :, None].astype(dt), s_prev.astype(dt))

    o = (o_intra + o_cross).transpose(0, 2, 3, 1, 4).reshape(B, S, H, dh)
    of = o.astype(jnp.float32)
    of = of * lax.rsqrt(jnp.mean(of * of, axis=-1, keepdims=True) + EPS)
    o = of.astype(dt).reshape(B, S, RET_DIM)
    return jax.nn.silu(g) * o

def first_inputs(seed: int = 0) -> dict:
    key = jax.random.key(seed)
    ks = jax.random.split(key, 16)
    f32 = jnp.float32
    x = jax.random.normal(ks[0], (BATCH, SEQ, D_MODEL), f32)
    c = jax.random.normal(ks[1], (BATCH, D_MODEL), f32)
    offset = jax.random.randint(ks[2], (BATCH, 1), 0, 4096, dtype=jnp.int32)
    positions = offset + jnp.arange(SEQ, dtype=jnp.int32)[None, :]
    w_ada = jax.random.normal(ks[3], (DEPTH, D_MODEL, N_MOD * D_MODEL), f32) * (0.5 * D_MODEL ** -0.5)
    b_ada = jax.random.normal(ks[4], (DEPTH, N_MOD * D_MODEL), f32) * 0.01
    g_pre_mix = 1.0 + 0.05 * jax.random.normal(ks[5], (DEPTH, D_MODEL), f32)
    g_post_mix = 1.0 + 0.05 * jax.random.normal(ks[6], (DEPTH, D_MODEL), f32)
    w_in = jax.random.normal(ks[7], (DEPTH, D_MODEL, IN_DIM), f32) * D_MODEL ** -0.5
    conv_w = jax.random.normal(ks[8], (DEPTH, CONV_WIDTH, CONV_DIM), f32) * CONV_WIDTH ** -0.5
    w_out = jax.random.normal(ks[9], (DEPTH, MIX_DIM, D_MODEL), f32) * MIX_DIM ** -0.5
    g_pre_mlp = 1.0 + 0.05 * jax.random.normal(ks[10], (DEPTH, D_MODEL), f32)
    g_post_mlp = 1.0 + 0.05 * jax.random.normal(ks[11], (DEPTH, D_MODEL), f32)
    w_fc1 = jax.random.normal(ks[12], (DEPTH, D_MODEL, D_FF), f32) * D_MODEL ** -0.5
    w_fc2 = jax.random.normal(ks[13], (DEPTH, D_FF, D_MODEL), f32) * D_FF ** -0.5
    return {'x': x, 'c': c, 'positions': positions, 'w_ada': w_ada, 'b_ada': b_ada,
            'g_pre_mix': g_pre_mix, 'g_post_mix': g_post_mix, 'w_in': w_in,
            'conv_w': conv_w, 'w_out': w_out, 'g_pre_mlp': g_pre_mlp,
            'g_post_mlp': g_post_mlp, 'w_fc1': w_fc1, 'w_fc2': w_fc2}

def first_block(x, c, positions, w_ada, b_ada, g_pre_mix, g_post_mix, w_in, conv_w,
              w_out, g_pre_mlp, g_post_mlp, w_fc1, w_fc2):
    split_at = [CONV_DIM, 2 * CONV_DIM, 3 * CONV_DIM,
                3 * CONV_DIM + RET_DIM, 3 * CONV_DIM + 2 * RET_DIM, 3 * CONV_DIM + 3 * RET_DIM]
    for layer in range(DEPTH):
        mod = jax.nn.silu(c) @ w_ada[layer] + b_ada[layer]
        shift1, scale1, gate1, shift2, scale2, gate2 = [
            m[:, None, :] for m in jnp.split(mod, N_MOD, axis=-1)]

        h = rms_norm(x, g_pre_mix[layer]) * (1.0 + scale1) + shift1
        proj = h @ w_in[layer]
        xin, b_gate, c_gate, q, k, v, g = jnp.split(proj, split_at, axis=-1)
        y_conv = short_conv_mixer(xin, b_gate, c_gate, conv_w[layer])
        y_ret = retention_mixer(q, k, v, g, positions)
        mix = jnp.concatenate([y_conv, y_ret], axis=-1) @ w_out[layer]
        x = x + gate1 * rms_norm(mix, g_post_mix[layer])

        h = rms_norm(x, g_pre_mlp[layer]) * (1.0 + scale2) + shift2
        f = jnp.square(jax.nn.relu(h @ w_fc1[layer])) @ w_fc2[layer]
        x = x + gate2 * rms_norm(f, g_post_mlp[layer])
    return x


A_HEADS = 8
A_HEAD_DIM = 64
A_WIDTH = A_HEADS * A_HEAD_DIM
IDX_HEADS = 4
IDX_DIM = 64
TOPK_MAX = 256
B_HEADS = 8
B_NOPE_DIM = 64
B_ROPE_DIM = 32
B_QK_DIM = B_NOPE_DIM + B_ROPE_DIM
B_V_DIM = 64
B_WIDTH = B_HEADS * B_V_DIM
Q_LORA = 256
KV_LORA = 128
ROPE_THETA = 10000.0
REL_BUCKETS = 32
REL_MAX_DIST = 128
N_BRANCHES = 2
D_FF_2 = 4 * D_MODEL
Q_BLOCK = 128
NEG_INF = -1e30
IN_SIZES = (A_WIDTH, A_HEAD_DIM, A_HEAD_DIM, IDX_HEADS * IDX_DIM, IDX_DIM, IDX_HEADS,
            Q_LORA, KV_LORA, B_ROPE_DIM, N_BRANCHES * D_MODEL)
D_IN = sum(IN_SIZES)


def rmsnorm(x, g):
    xf = x.astype(jnp.float32)
    y = xf * lax.rsqrt(jnp.mean(xf * xf, axis=-1, keepdims=True) + EPS)
    return (y * g.astype(jnp.float32)).astype(x.dtype)

def split_cols(z, sizes):
    cuts = [int(c) for c in np.cumsum(sizes)[:-1]]
    return jnp.split(z, cuts, axis=-1)

def rope_tables(positions):
    inv_freq = ROPE_THETA ** (-jnp.arange(0, B_ROPE_DIM, 2, dtype=jnp.float32) / B_ROPE_DIM)
    ang = positions.astype(jnp.float32)[..., None] * inv_freq
    return jnp.cos(ang), jnp.sin(ang)

def apply_rope(x, cos, sin):
    x1, x2 = jnp.split(x, 2, axis=-1)
    cos = cos.astype(x.dtype)
    sin = sin.astype(x.dtype)
    return jnp.concatenate([x1 * cos - x2 * sin, x1 * sin + x2 * cos], axis=-1)

def rel_bucket(dist):
    max_exact = REL_BUCKETS // 2
    n = jnp.maximum(dist, 0)
    nf = jnp.maximum(n.astype(jnp.float32), 1.0)
    log_b = max_exact + (jnp.log(nf / max_exact) / math.log(REL_MAX_DIST / max_exact)
                         * (REL_BUCKETS - max_exact)).astype(jnp.int32)
    return jnp.where(n < max_exact, n, jnp.minimum(log_b, REL_BUCKETS - 1))

def take_rows(arr, idx):
    return jax.vmap(lambda a, i: a[i])(arr, idx)

def dsa_sparse_attention(q, k, v, iq, ik, iw, positions, rel_table):
    bsz, L = q.shape[0], q.shape[1]
    k_top = min(TOPK_MAX, L // 4)
    key_idx = jnp.arange(L)
    ikf = ik.astype(jnp.float32)

    def one_block(bi):
        start = bi * Q_BLOCK
        qb = lax.dynamic_slice_in_dim(q, start, Q_BLOCK, axis=1)
        iqb = lax.dynamic_slice_in_dim(iq, start, Q_BLOCK, axis=1).astype(jnp.float32)
        iwb = lax.dynamic_slice_in_dim(iw, start, Q_BLOCK, axis=1).astype(jnp.float32) * IDX_HEADS ** -0.5
        posq = lax.dynamic_slice_in_dim(positions, start, Q_BLOCK, axis=1)
        q_idx = start + jnp.arange(Q_BLOCK)
        causal = key_idx[None, :] <= q_idx[:, None]
        dots = jnp.einsum('bqhd,bsd->bqhs', iqb, ikf) * IDX_DIM ** -0.5
        score = jnp.einsum('bqh,bqhs->bqs', iwb, jax.nn.relu(dots))
        score = jnp.where(causal[None], score, -jnp.inf)
        _, sel = lax.top_k(score, k_top)
        k_sel = take_rows(k, sel)
        v_sel = take_rows(v, sel)
        bias = rel_table[rel_bucket(posq[:, :, None] - take_rows(positions, sel))]
        logits = jnp.einsum('bqhd,bqkd->bqhk', qb, k_sel).astype(jnp.float32) * A_HEAD_DIM ** -0.5
        logits = logits + jnp.swapaxes(bias, 2, 3).astype(jnp.float32)
        valid = sel <= q_idx[None, :, None]
        logits = jnp.where(valid[:, :, None, :], logits, NEG_INF)
        p = jax.nn.softmax(logits, axis=-1).astype(v.dtype)
        return jnp.einsum('bqhk,bqkd->bqhd', p, v_sel)

    out = lax.map(one_block, jnp.arange(L // Q_BLOCK))
    return jnp.moveaxis(out, 0, 1).reshape(bsz, L, A_WIDTH)

def mla_attention(q_nope, q_rope, k_nope, k_rope, v):
    bsz, L = q_nope.shape[0], q_nope.shape[1]
    key_idx = jnp.arange(L)

    def one_block(bi):
        start = bi * Q_BLOCK
        qn = lax.dynamic_slice_in_dim(q_nope, start, Q_BLOCK, axis=1)
        qr = lax.dynamic_slice_in_dim(q_rope, start, Q_BLOCK, axis=1)
        q_idx = start + jnp.arange(Q_BLOCK)
        logits = (jnp.einsum('bqhd,bshd->bhqs', qn, k_nope)
                  + jnp.einsum('bqhr,bsr->bhqs', qr, k_rope)).astype(jnp.float32) * B_QK_DIM ** -0.5
        causal = key_idx[None, :] <= q_idx[:, None]
        logits = jnp.where(causal[None, None], logits, NEG_INF)
        p = jax.nn.softmax(logits, axis=-1).astype(v.dtype)
        return jnp.einsum('bhqs,bshd->bqhd', p, v)

    out = lax.map(one_block, jnp.arange(L // Q_BLOCK))
    return jnp.moveaxis(out, 0, 1).reshape(bsz, L, B_WIDTH)

def second_inputs(seed: int = 0) -> dict:
    key = jax.random.key(seed)
    ks = jax.random.split(key, 20)
    f32 = jnp.float32

    def nrm(k, shape, scale):
        return jax.random.normal(k, shape, f32) * scale

    def gain(k, shape):
        return 1.0 + 0.02 * jax.random.normal(k, shape, f32)

    x = jax.random.normal(ks[0], (BATCH, SEQ, D_MODEL), f32)
    offset = jax.random.randint(ks[1], (BATCH, 1), 0, 4096, dtype=jnp.int32)
    positions = offset + jnp.arange(SEQ, dtype=jnp.int32)[None, :]
    return {
        "x": x,
        "positions": positions,
        "attn_norm_g": gain(ks[2], (DEPTH, D_MODEL)),
        "w_in": nrm(ks[3], (DEPTH, D_MODEL, D_IN), D_MODEL ** -0.5),
        "b_gate": nrm(ks[4], (DEPTH, N_BRANCHES * D_MODEL), 0.02),
        "q_latent_norm_g": gain(ks[5], (DEPTH, Q_LORA)),
        "kv_latent_norm_g": gain(ks[6], (DEPTH, KV_LORA)),
        "w_uq": nrm(ks[7], (DEPTH, Q_LORA, B_HEADS * B_QK_DIM), Q_LORA ** -0.5),
        "w_ukv": nrm(ks[8], (DEPTH, KV_LORA, B_HEADS * (B_NOPE_DIM + B_V_DIM)), KV_LORA ** -0.5),
        "w_branch_a": nrm(ks[9], (DEPTH, A_WIDTH, D_MODEL), A_WIDTH ** -0.5),
        "w_branch_b": nrm(ks[10], (DEPTH, B_WIDTH, D_MODEL), B_WIDTH ** -0.5),
        "w_out": nrm(ks[11], (DEPTH, D_MODEL, D_MODEL), D_MODEL ** -0.5),
        "mlp_norm_g": gain(ks[12], (DEPTH, D_MODEL)),
        "w_ff1": nrm(ks[13], (DEPTH, D_MODEL, D_FF_2), D_MODEL ** -0.5),
        "w_ff2": nrm(ks[14], (DEPTH, D_FF_2, D_MODEL), D_FF_2 ** -0.5),
        "rel_bias": nrm(ks[15], (REL_BUCKETS, A_HEADS), 0.5),
        "final_norm_g": gain(ks[16], (D_MODEL,)),
    }

def second_block(x, positions, attn_norm_g, w_in, b_gate, q_latent_norm_g, kv_latent_norm_g,
              w_uq, w_ukv, w_branch_a, w_branch_b, w_out, mlp_norm_g, w_ff1, w_ff2,
              rel_bias, final_norm_g):
    bsz, L, _ = x.shape
    cos, sin = rope_tables(positions)
    for l in range(DEPTH):
        h = rmsnorm(x, attn_norm_g[l])
        z = h @ w_in[l]
        a_q, a_k, a_v, i_q, i_k, i_w, c_q, c_kv, k_r, g = split_cols(z, IN_SIZES)
        y_a = dsa_sparse_attention(a_q.reshape(bsz, L, A_HEADS, A_HEAD_DIM), a_k, a_v,
                                   i_q.reshape(bsz, L, IDX_HEADS, IDX_DIM), i_k, i_w,
                                   positions, rel_bias)
        qb = (rmsnorm(c_q, q_latent_norm_g[l]) @ w_uq[l]).reshape(bsz, L, B_HEADS, B_QK_DIM)
        q_nope, q_rope = jnp.split(qb, [B_NOPE_DIM], axis=-1)
        q_rope = apply_rope(q_rope, cos[:, :, None], sin[:, :, None])
        kvb = (rmsnorm(c_kv, kv_latent_norm_g[l]) @ w_ukv[l]).reshape(bsz, L, B_HEADS, B_NOPE_DIM + B_V_DIM)
        k_nope, v_b = jnp.split(kvb, [B_NOPE_DIM], axis=-1)
        k_rope = apply_rope(k_r, cos, sin)
        y_b = mla_attention(q_nope, q_rope, k_nope, k_rope, v_b)
        gates = jax.nn.sigmoid((g + b_gate[l]).astype(jnp.float32)).astype(x.dtype)
        gates = gates.reshape(bsz, L, N_BRANCHES, D_MODEL)
        merged = gates[:, :, 0] * (y_a @ w_branch_a[l]) + gates[:, :, 1] * (y_b @ w_branch_b[l])
        x = x + merged @ w_out[l]
        h2 = rmsnorm(x, mlp_norm_g[l])
        x = x + jnp.square(jax.nn.relu(h2 @ w_ff1[l])) @ w_ff2[l]
    return rmsnorm(x, final_norm_g)


def setup_inputs(seed=0):
    out = dict(first_inputs(seed))
    for name, value in second_inputs(seed + 1).items():
        if name != "x":
            out[name + "_2"] = value
    return out


def reference(
    x, c, positions, w_ada, b_ada, g_pre_mix, g_post_mix, w_in, conv_w, w_out, g_pre_mlp,
    g_post_mlp, w_fc1, w_fc2, positions_2, attn_norm_g_2, w_in_2, b_gate_2, q_latent_norm_g_2,
    kv_latent_norm_g_2, w_uq_2, w_ukv_2, w_branch_a_2, w_branch_b_2, w_out_2, mlp_norm_g_2,
    w_ff1_2, w_ff2_2, rel_bias_2, final_norm_g_2,
):
    x = first_block(
        x, c, positions, w_ada, b_ada, g_pre_mix, g_post_mix, w_in, conv_w, w_out, g_pre_mlp,
        g_post_mlp, w_fc1, w_fc2,
    )
    return second_block(
        x, positions_2, attn_norm_g_2, w_in_2, b_gate_2, q_latent_norm_g_2, kv_latent_norm_g_2,
        w_uq_2, w_ukv_2, w_branch_a_2, w_branch_b_2, w_out_2, mlp_norm_g_2, w_ff1_2, w_ff2_2,
        rel_bias_2, final_norm_g_2,
    )


_drawn_inputs = setup_inputs


def setup_inputs(seed=0):
    import zlib

    import numpy as np

    out = dict(_drawn_inputs(seed))
    spreads = {}
    factors = {'b_ada': 2.948,
     'g_post_mix': 2.99,
     'g_pre_mlp': 3.041,
     'g_post_mlp': 3.231,
     'attn_norm_g_2': 6.442,
     'b_gate_2': 8.0,
     'q_latent_norm_g_2': 8.0,
     'kv_latent_norm_g_2': 8.0,
     'mlp_norm_g_2': 9.009,
     'final_norm_g_2': 7.423}
    for name, (base, spread) in spreads.items():
        noise = np.random.default_rng([zlib.crc32(name.encode()), seed]).standard_normal(out[name].shape)
        drawn = base * np.exp(spread * noise) if base else spread * noise
        out[name] = __import__('jax').numpy.asarray(drawn.astype(out[name].dtype))
    for name, factor in factors.items():
        out[name] = (out[name] * factor).astype(out[name].dtype)
    return out
```

```python
from contextlib import ExitStack

import numpy as np

import concourse.bass as bass
from concourse import mybir

F32 = mybir.dt.float32
F32R = mybir.dt.float32r
BF16 = mybir.dt.bfloat16
I32 = mybir.dt.int32
ALU = mybir.AluOpType
ACT = mybir.ActivationFunctionType
AX = mybir.AxisListType.X

P = 128
S = 1024
D = 1024
KC = D // P
NB = S // P
HALF = 512
DFF = 4 * D
EPS = 1e-6

RET_HEADS, RET_DIM, CHUNK = 4, 128, 64
CONV = 4

A_HEADS, A_DIM = 8, 64
IDX_HEADS, TOPK = 4, 256
B_HEADS, B_NOPE, B_ROPE, B_QK, B_V = 8, 64, 32, 96, 64
BUCKETS = 32
QT = P // A_HEADS
STEPQ = P // BUCKETS
NSTEP = QT // STEPQ

NEG = -1e30
HIDDEN = -3.0e38
TAKEN = -3.3e38

AQ, AK, AV, IQ, IK, IW, CQ, CKV, KR, GT = 0, 512, 576, 640, 896, 960, 964, 1220, 1348, 1380

VEC_A = [("c", 8), ("b_ada", 48), ("g_pre_mix", 8), ("g_post_mix", 8), ("g_pre_mlp", 8), ("g_post_mlp", 8),
         ("conv_w", 12)]
VEC_B = [("attn_norm_g_2", 8), ("b_gate_2", 16), ("q_latent_norm_g_2", 2), ("kv_latent_norm_g_2", 1),
         ("mlp_norm_g_2", 8), ("final_norm_g_2", 8)]


def vec_columns():
    at, n = {}, 0
    for name, k in VEC_A + VEC_B:
        at[name] = n
        n += k
    return at


VCOL = vec_columns()
NVA = sum(k for _, k in VEC_A)
NVB = sum(k for _, k in VEC_B)


def bucket_steps():
    n = np.arange(1, 4096)
    f = np.float32
    log_b = 16 + (np.log(n.astype(f) / f(16)) / f(np.log(8.0)) * f(16)).astype(np.int32)
    b = np.where(n < 16, n, np.minimum(log_b, BUCKETS - 1))
    return [-1e9] + [float(n[np.argmax(b >= k)]) for k in range(1, BUCKETS)]


def constants():
    parts = {}
    i = np.arange(P)
    parts["ident"] = np.eye(P)
    parts["ones"] = np.ones((P, 1))
    parts["eps"] = np.full((P, 1), EPS)
    half = RET_DIM // 2
    inv = np.float32(10000.0) ** (-(np.arange(half, dtype=np.float32)) / np.float32(half))
    parts["inv1"] = np.tile(inv, 2)[:, None]
    inv2 = np.float32(10000.0) ** (-np.arange(0, B_ROPE, 2, dtype=np.float32) / np.float32(B_ROPE))
    parts["inv2"] = np.tile(inv2, 8)[:, None]
    parts["sgn1"] = np.where(i < half, 1.0, -1.0)[:, None]
    parts["sgn2"] = np.where(i % B_ROPE < 16, -1.0, 1.0)[:, None]
    parts["steps"] = np.tile(np.array(bucket_steps()), STEPQ)[:, None]
    gam = 1.0 - 2.0 ** (-5.0 - np.arange(RET_HEADS))
    j = i[:, None]
    q = i[None, :]
    allowed = (j // CHUNK) <= (q // CHUNK)
    parts["decay"] = np.concatenate([np.where(allowed, g ** np.abs(j - q), 0.0) for g in gam], axis=1)
    parts["qdec"] = np.concatenate([np.tile(g ** (q + 1.0), (P, 1)) for g in gam], axis=1)
    parts["kdec"] = np.stack([g ** (P - 1.0 - i) for g in gam], axis=1)
    sel = np.zeros((P, NB, A_HEADS, QT))
    for r in range(NB):
        for t in range(QT):
            sel[r * QT + t, r, :, t] = 1.0
    parts["sel"] = sel.reshape(P, NB * P)
    rep = np.zeros((P, P))
    for t in range(STEPQ):
        for b in range(BUCKETS):
            rep[b, t * BUCKETS + b] = 1.0
            if b:
                rep[b - 1, t * BUCKETS + b] = -1.0
    parts["rep"] = rep
    reach = np.zeros((P, NSTEP, A_HEADS, QT))
    for g in range(NSTEP):
        for t in range(STEPQ):
            reach[t * BUCKETS:(t + 1) * BUCKETS, g, :, g * STEPQ + t] = 1.0
    parts["reach"] = reach.reshape(P, NSTEP * P)
    parts["tri"] = np.where(i[None, :] > i[:, None], NEG, 0.0)
    at, n = {}, 0
    for name, a in parts.items():
        at[name] = (n, a.shape[1])
        n += a.shape[1]
    return at, np.concatenate([np.asarray(a, np.float32) for a in parts.values()], axis=1).astype(np.float32)


CONST_AT, CONST = constants()
MAGIC = 1.5 * 2.0 ** 23
PI = float(np.nextafter(np.float32(np.pi), np.float32(0)))
TWO_PI = [6.28125, float(np.float32(0.0019350051879882812)), 2 * np.pi - 6.28125 - float(np.float32(0.0019350051879882812))]
GAMMA_BLOCK = [float((1.0 - 2.0 ** (-5.0 - h)) ** P) for h in range(RET_HEADS)]


def build(nc, x, positions, w_ada, w_in, w_out, w_fc1, w_fc2, positions_2, w_in_2, w_uq_2, w_ukv_2,
          w_branch_a_2, w_branch_b_2, w_out_2, w_ff1_2, w_ff2_2, rel_bias_2, vec, const, out):
    ctx = ExitStack()
    with ctx:
        def sem(name):
            return ctx.enter_context(nc.semaphore(name))

        arena_words = 53100
        arena = ctx.enter_context(nc.sbuf_tensor("arena", [P, arena_words], F32))
        base = (nc.sbuf_base - arena_words * 4 + 31) // 32 * 32
        taken = [0]

        def place(name, words, dt=F32, at=None):
            n = words * 2 if dt == BF16 else words
            start = taken[0] if at is None else at
            t = nc.alloc_sbuf_tensor_at(name, [P, n], dt, offset=base + 4 * start)
            if at is None:
                taken[0] += words
            return t

        X0 = taken[0]
        X = place("X", KC * S)
        H0 = taken[0]
        H = place("H", KC * S, F32R)
        L0 = taken[0]
        L = place("L", KC * S, F32R)
        Y0 = taken[0]
        Y = place("Y", KC * S)
        RAW = [place(f"RAW{j}", 1024) for j in range(2)]
        WHI = [place(f"WHI{j}", 1024, F32R) for j in range(2)]
        WLO = [place(f"WLO{j}", 1024, F32R) for j in range(2)]
        IDN = place("IDN", P)
        SC = place("SC", 16)
        IDB = place("IDB", P // 2, BF16)
        TRB = place("TRB", P // 2, BF16)
        VEC = place("VEC", 144)
        MOD = place("MOD", 48)
        MODA = place("MODA", 40)
        SS = place("SS", 8)
        RS = place("RS", 8)
        SILC = place("SILC", 8)
        ZERO = place("ZERO", 8)
        K0 = taken[0]
        WKW = arena_words - K0 - 16
        WK = place("WK", WKW)
        assert WKW >= 13312, WKW

        def region(name, start, words, dt=F32):
            return place(name, words, dt, at=start)

        def chunk(t, k, n=1, rows=slice(0, P)):
            return t[rows, k * S:(k + n) * S]

        XT = region("XT", Y0, 8192)
        ADA = [region(f"ADA{j}", K0 + 1024 * j, S) for j in range(4)]
        STG = region("STG", K0 + 4096, 3 * P)
        CX = region("CX", K0 + 4096, S)
        CU = region("CU", K0 + 5120, S + 2)
        CT = region("CT", K0 + 6152, S)
        SQ = [region("SQ0", K0 + 12304, S), region("SQ1", K0 + 7176, S)]
        ROT_C = region("ROT_C", K0 + 8200, S)
        ROT_S = region("ROT_S", K0 + 9224, S)
        DEC = region("DEC", K0 + 10248, 1028)
        ACC = region("ACC", K0 + 11280, S)
        R_QR, R_KR, R_VT, R_VTOK, R_G, R_KTOK, R_QD, R_SD = [region(n, X0 + 1024 * i, S) for i, n in enumerate(
            ["R_QR", "R_KR", "R_VT", "R_VTOK", "R_G", "R_KTOK", "R_QD", "R_SD"])]
        R_T, R_T2, R_ST, R_SQ, R_OG = [region(n, K0 + 1024 * i, S) for i, n in enumerate(
            ["R_T", "R_T2", "R_ST", "R_SQ", "R_OG"])]
        FH = region("FH", K0, 4 * S, F32R)
        FL = region("FL", K0 + 4096, 4 * S, F32R)
        RL = [region(f"RL{j}", K0 + 8192 + 1024 * j, S) for j in range(2)]
        FT = region("FT", K0 + 10240, S)

        AQP = region("AQP", X0, 4 * S)
        CQB = region("CQB", X0 + 4096, 2 * S)
        CKVB = region("CKVB", X0 + 6144, S)
        AVKR = region("AVKR", X0 + 7168, S)
        SCORE_AT, n = {}, 0
        for b in range(2, NB):
            SCORE_AT[b] = n
            n += P * (b + 1)
        SCO = region("SCO", Y0, n)
        MASK_AT = {b: P * b * (b + 1) // 2 for b in range(NB)}
        MB = region("MB", Y0 + n, P * 36 // 2, BF16)
        AKB = region("AKB", Y0 + 6528, S)
        TK = region("TK", Y0 + 7552, 8)
        IWTOK = region("IWTOK", Y0 + 7560, 32)
        MXS = region("MXS", Y0 + 7592, 8)
        NMX = region("NMX", Y0 + 7600, 8)
        RSUM = region("RSUM", Y0 + 7608, 8)
        RINV = region("RINV", Y0 + 7616, 8)
        DLT = region("DLT", Y0 + 7624, 8)
        IQB = region("IQB", K0, 2 * S)
        IKB = region("IKB", K0 + 2048, S)
        RT = [region(f"RT{j}", K0 + 3072 + 1024 * j, S) for j in range(2)]
        IWT = region("IWT", K0 + 5120, S)
        GST = [region(f"GST{j}", K0 + 6144 + 1024 * j, S) for j in range(2)]
        T2C = region("T2C", K0 + 8192, S)
        T2S = region("T2S", K0 + 9216, S)
        WUQ = region("WUQ", K0 + 10240, 2 * S)
        WUKV = region("WUKV", K0 + 12288, S)
        QM = region("QM", H0, 8 * S)
        KM = region("KM", L0, 8 * S)
        VM = region("VM", K0, 4 * S)
        PB = [region(f"PB{j}", K0 + 4096 + 1024 * j, S) for j in range(2)]
        PTS = [region(f"PTS{j}", K0 + 6144 + 1024 * j, S) for j in range(2)]
        OB = region("OB", K0 + 12288, S)
        YB = region("YB", X0 + 4096, 4 * S)
        VA = region("VA", Y0, NB * A_DIM)
        AQ64 = region("AQ64", H0, 8 * S)
        POSB = region("POSB", L0, S)
        STEP = [region("STEP0", L0 + 1024, 4 * S, F32R), region("STEP1", X0, 4 * S, F32R)]
        DHI = region("DHI", L0 + 5120, NSTEP * P, F32R)
        DLO = region("DLO", L0 + 5632, NSTEP * P, F32R)
        SELB = region("SELB", L0 + 6144, 512, BF16)
        THR = region("THR", L0 + 6656, 256)
        DF = region("DF", L0 + 6912, NSTEP * P)
        TAB = region("TAB", L0 + 7680, 8)
        YA = region("YA", K0 + 8192, 4 * S)
        CST = region("CST", K0 + 8192, 1664)
        GB = [region(f"GB{j}", K0 + 2048 * j, 2 * S) for j in range(4)]
        MT = region("MT", K0 + 8192, 2 * S)
        OT = [region(f"OT{j}", K0 + 1024 * j, S) for j in range(2)]

        PS = ctx.enter_context(nc.psum_tensor("PS", [P, 8 * HALF], F32))

        def bank(b, n=1, rows=slice(0, P)):
            return PS[rows, b * HALF:(b + n) * HALF]

        xs = nc.dram_tensor("x_scratch", [P, KC * S], F32).ap()
        gs = nc.dram_tensor("gate_scratch", [16, P, S], F32).ap()

        s_const = sem("const_in")
        s_x = sem("x_in")
        s_rot = sem("rotation_tables")
        s_raw = [sem(f"raw_in{j}") for j in range(2)]
        s_ada_in = [sem(f"ada_in{j}") for j in range(4)]
        s_ada = sem("ada_product_done")
        s_adaev = sem("ada_added")
        s_whi = sem("weight_high_part")
        s_zero = sem("zero_ready")
        s_w = sem("weight_split")
        s_mm = sem("product_done")
        s_eva = sem("psum_read_by_act")
        s_evv = sem("psum_read_by_dve")
        s_vt = sem("vectors_transposed")
        s_vec = sem("vectors_ready")
        s_silc = sem("silu_of_c")
        s_xt = sem("x_transposed")
        s_xc = sem("x_copied")
        s_sq = sem("squares")
        s_acc = sem("squares_added")
        s_ss = sem("row_sums_of_squares")
        s_std = sem("root_of_mean_square")
        s_rs = sem("reciprocal_root")
        s_bc = sem("reciprocal_root_spread")
        s_xn = sem("residual_added")
        s_h32 = sem("normed_scaled")
        s_hi = sem("activation_high_part")
        s_lo = sem("activation_low_part")
        s_dve = sem("dve_own")
        s_act = sem("act_own")
        s_xs = sem("x_stored")
        s_xr = sem("x_reloaded")
        s_mod = sem("modulations_ready")
        s_red = sem("angles_reduced")
        s_sin = sem("sines")
        s_rt = sem("rotated_terms")
        s_r_q, s_r_k, s_r_qd = sem("ret_q"), sem("ret_k"), sem("ret_q_decayed")
        s_r_vT, s_r_kT = sem("ret_v_transposed"), sem("ret_k_transposed")
        s_r_vtok, s_r_ktok = sem("ret_v_tokens"), sem("ret_k_tokens")
        s_r_sc, s_r_sd = sem("ret_scores"), sem("ret_scores_decayed")
        s_r_kv, s_r_st = sem("ret_block_sums"), sem("ret_states")
        s_r_o, s_r_sq, s_r_og, s_ret_y = sem("ret_out"), sem("ret_squares"), sem("ret_gated"), sem("ret_done")
        s_pos2 = sem("positions_2_in")
        s_red2, s_sin2 = sem("angles_2_reduced"), sem("sines_2")
        s_iwt, s_iw = sem("index_weights_transposed"), sem("index_weights_ready")
        s_ixp, s_rel, s_idx = sem("index_product"), sem("index_relu"), sem("index_added")
        s_diag, s_mb = sem("scores_masked"), sem("selection_mask")
        s_gs = [sem(f"gate_stored{j}") for j in range(2)]
        s_wuq = sem("up_weights_in")
        s_lacc, s_lat = sem("latent_squares"), sem("latent_normed")
        s_up, s_upa, s_upd, s_q = sem("up_product"), sem("up_read_by_act"), sem("up_read_by_dve"), sem("query_rotated")
        s_kt, s_kr, s_krd = sem("key_terms"), sem("key_rotated"), sem("key_spread")
        s_lg, s_nm, s_exp = sem("logits"), sem("row_max"), sem("probabilities")
        s_pt, s_pte, s_pv, s_oe = sem("probs_transposed"), sem("probs_t_copied"), sem("attended"), sem("attended_scaled")
        s_bt, s_bte = sem("attended_transposed"), sem("attended_t_copied")
        s_c4, s_aq, s_tp, s_tpd = sem("tables_in"), sem("queries_moved"), sem("table_products"), sem("tables_ready")
        s_step = sem("steps")
        s_g = [sem(f"gates_in{j}") for j in range(4)]
        s_fin, s_ft, s_fo, s_out = sem("final_normed"), sem("final_transposed"), sem("final_copied"), [sem(f"out_stored{j}") for j in range(2)]
        block = ctx.enter_context(nc.Block())

        ident = IDN[:, :]
        ones = SC[:, 0:1]
        eps = SC[:, 1:2]
        inv1, inv2 = SC[:, 2:3], SC[:, 3:4]
        sgn1, sgn2 = SC[:, 4:5], SC[:, 5:6]
        steps = SC[:, 6:7]

        def vcol(name, k):
            n = VCOL[name] + k
            return VEC[:, n:n + 1]


        def w_tile(w, r0, kc, c0, nc_):
            return w[r0:r0 + kc * P, c0:c0 + nc_].rearrange("(k p) n -> p k n", p=P)

        def k_n(t, kc, n):
            return t[:, 0:kc * n].rearrange("p (k n) -> p k n", k=kc)

        W_IN = []
        for j in range(CONV):
            W_IN += [("xin", j, j * P), ("c", j, 1024 + j * P), ("b", j, 512 + j * P)]
        for h in range(RET_HEADS):
            W_IN += [(n, h, 1536 + 512 * i + h * P) for i, n in enumerate(["q", "k", "v", "g"])]
        ADA_ORDER = [8 * g + i for g in (1, 0, 2, 3, 4, 5) for i in range(8)]
        ADA_FIRST = 16
        ADA_AFTER = {w: 3 if w < 10 else 2 for w in range(11)}

        OWNER = {}
        for w, (kind, _, _) in enumerate(W_IN):
            OWNER[w] = "act" if kind in ("xin", "v", "g") else "dve"
        W_OUT0 = len(W_IN)
        for w in range(W_OUT0, W_OUT0 + 8):
            OWNER[w] = "act"
        MLP1 = W_OUT0 + 8

        def reads(w):
            who = OWNER[w]
            return (s_eva if who == "act" else s_evv), sum(OWNER[v] == who for v in range(w + 1))

        def w_bank(w):
            return 4 * (w % 2)


        GROUPS = DFF // 512

        class Counts:

            def __init__(self, w, act, dve, f32, parts):
                self.w, self.act, self.dve, self.f32, self.parts = w, act, dve, f32, parts

        M1 = Counts(MLP1, sum(v == "act" for v in OWNER.values()), sum(v == "dve" for v in OWNER.values()),
                    2 * KC, 3 * KC)
        assert M1.w % 2 == 0

        def sq_buffer(n):
            return (RL if n // KC in SQUARES_IN_MLP else SQ)[n % 2]

        SQUARES_IN_MLP = (3, 6)

        for g in range(GROUPS):
            for i in range(8):
                OWNER[MLP1 + 8 * g + i] = "act" if i < 4 else "dve"

        Z0 = MLP1 + 8 * GROUPS
        Z_TILES = [("iw", IW), ("iq", IQ), ("iq", IQ + P), ("akik", AK), ("avkr", AV)]
        Z_TILES += [("aq", AQ + P * i) for i in range(4)]
        Z_TILES += [("cq", CQ), ("cq", CQ + P), ("ckv", CKV)]
        Z_GATE = len(Z_TILES)
        Z_TILES += [("gate", GT + P * i) for i in range(16)]
        BR0 = Z0 + len(Z_TILES)
        OUT0 = BR0 + 8
        MLP2 = OUT0 + 8
        for w in range(Z0, BR0):
            OWNER[w] = "act"
        for w in range(BR0, MLP2):
            OWNER[w] = "dve"
        DMAS = {Z0 + 3: 2, Z0 + 4: 4}

        def loads(w):
            return sum(DMAS.get(v, 1) for v in range(w % 2, w + 1, 2))

        M2 = Counts(MLP2, sum(v == "act" for v in OWNER.values()), sum(v == "dve" for v in OWNER.values()),
                    M1.f32 + 4 * GROUPS + 2 * KC, M1.parts + 4 * GROUPS + 4 * KC)
        assert M2.w % 2 == 0
        Z_PARTS = M1.parts + 4 * GROUPS + KC
        UPS = 17
        ATT = [(b, 2 * c + e) for c in range(4) for b in range(NB) for e in range(2)]
        ATT += [(b, r) for b in range(NB) for r in range(NB)]
        BACK = {16 * j + 15: j for j in range(4)}
        BACK.update({64 + 8 * j + 7: 4 + j for j in range(8)})
        GATED0 = sum(OWNER[v] == "dve" for v in range(BR0))

        @block.sync
        def _(sp):
            sp.dma_start(IDN[:, :], const[:, 0:P]).then_inc(s_const, 16)
            sp.dma_start(SC[:, 0:7], const[:, P:P + 7]).then_inc(s_const, 16)
            sp.dma_start(STG[0:NVA, 0:P], vec[0:NVA, :]).then_inc(s_const, 16)
            sp.dma_start(STG[0:NVB, P:2 * P], vec[NVA:NVA + NVB, :]).then_inc(s_const, 16)
            tri = CONST_AT["tri"][0]
            sp.dma_start(STG[:, 2 * P:3 * P], const[:, tri:tri + P]).then_inc(s_const, 16)
            sp.dma_start(XT[:, :].rearrange("p (b d) -> p b d", b=NB),
                         x.rearrange("(b p) d -> p b d", p=P)).then_inc(s_x, 16)
            sp.dma_start(ROT_S[:, :].bitcast(I32), positions.partition_broadcast(P)).then_inc(s_rot, 16)
            sp.dma_start(DEC[:, :], const[:, CONST_AT["decay"][0]:CONST_AT["decay"][0] + 1028]).then_inc(s_rot, 16)

            def load_ada(n):
                if n >= 4:
                    sp.wait_ge(s_ada, n - 3)
                a = ADA_ORDER[n]
                sp.dma_start(k_n(ADA[n % 4], KC, P), w_tile(w_ada, 0, KC, a * P, P)).then_inc(s_ada_in[n % 4], 16)

            def load_w(w, src, kc, n):
                if w >= 2:
                    sp.wait_ge(s_w, w - 1)
                sp.dma_start(k_n(RAW[w % 2], kc, n), src).then_inc(s_raw[w % 2], 16)

            for n in range(ADA_FIRST - 2):
                load_ada(n)
            for w in range(2):
                load_w(w, w_tile(w_in, 0, KC, W_IN[w][2], P), KC, P)
            for n in range(ADA_FIRST - 2, ADA_FIRST + 2):
                load_ada(n)
            sp.wait_ge(s_xc, KC)
            sp.dma_start(xs, X[:, :]).then_inc(s_xs, 16)
            n = ADA_FIRST + 2
            for w in range(2, len(W_IN)):
                for _ in range(ADA_AFTER.get(w - 2, 0)):
                    if n < 48:
                        load_ada(n)
                        n += 1
                load_w(w, w_tile(w_in, 0, KC, W_IN[w][2], P), KC, P)
            for i in range(8):
                load_w(W_OUT0 + i, w_tile(w_out, 0, KC, i * P, P), KC, P)
            sp.wait_ge(s_xs, 16)
            sp.wait_ge(s_ret_y, RET_HEADS)
            sp.dma_start(X[:, :], xs).then_inc(s_xr, 16)

            def mlp_loads(m, up, down):
                down_v = down.rearrange("(g k p) n -> g p k n", k=4, p=P)

                def group(g):
                    for i in range(8):
                        w = 8 * g + (m.w + i)
                        sp.wait_ge(s_w, w - 1)
                        if i < 4:
                            src = up.rearrange("(k p) n -> p k n", p=P)[:, :, bass.ds(512 * g + i * P, P)]
                            dst = k_n(RAW[i % 2], KC, P)
                        else:
                            src = down_v[bass.ds(g, 1), :, :, 256 * (i - 4):256 * (i - 3)].rearrange("o p k n -> (o p) k n")
                            dst = k_n(RAW[i % 2], 4, 256)
                        sp.dma_start(dst, src).then_inc(s_raw[i % 2], 16)

                with sp.Fori(0, GROUPS) as g:
                    group(g)

            mlp_loads(M1, w_fc1, w_fc2)

            sp.wait_ge(s_xr, 16)
            sp.wait_ge(s_xn, 2 * KC)
            sp.dma_start(xs, X[:, :]).then_inc(s_xs, 16)
            for i, (kind, c0) in enumerate(Z_TILES):
                w = Z0 + i
                sp.wait_ge(s_w, w - 1)
                dst = k_n(RAW[w % 2], KC, P)
                if kind == "akik":
                    pieces = [(0, AK, 64), (64, IK, 64)]
                elif kind == "avkr":
                    pieces = [(0, AV, 64), (64, KR, 32), (96, KR + 16, 16), (112, KR, 16)]
                else:
                    pieces = [(0, c0, P)]
                for to, c, n in pieces:
                    sp.dma_start(dst[:, :, to:to + n], w_tile(w_in_2, 0, KC, c, n)).then_inc(s_raw[w % 2], 16)
                if i == 1:
                    sp.wait_ge(s_lo, Z_PARTS)
                    sp.dma_start(T2S[:, :].bitcast(I32), positions_2.partition_broadcast(P)).then_inc(s_pos2, 16)
                    q = WUQ[:, :].rearrange("p (k h n) -> p k h n", k=2, h=B_HEADS)
                    qd = w_uq_2.rearrange("(k p) (h n) -> p k h n", p=P, n=B_QK)
                    for k in range(2):
                        sp.dma_start(q[:, k, :, 0:B_QK], qd[:, k, :, :]).then_inc(s_wuq, 16)
                        sp.dma_start(q[:, k, :, 96:112], qd[:, k, :, 80:96]).then_inc(s_wuq, 16)
                        sp.dma_start(q[:, k, :, 112:128], qd[:, k, :, 64:80]).then_inc(s_wuq, 16)
                    kv = w_ukv_2.rearrange("p (h n) -> p h n", h=B_HEADS)
                    for e in range(2):
                        sp.dma_start(WUKV[:, e * HALF:(e + 1) * HALF].rearrange("p (h n) -> p h n", h=B_HEADS),
                                     kv[:, :, 64 * e:64 * (e + 1)]).then_inc(s_wuq, 16)

            def load_branch(m):
                w = BR0 + m
                sp.wait_ge(s_w, w - 1)
                src = w_branch_b_2 if m % 2 else w_branch_a_2
                sp.dma_start(k_n(RAW[w % 2], 4, 256), w_tile(src, 0, 4, 256 * (m // 2), 256)).then_inc(s_raw[w % 2], 16)

            load_branch(0)
            load_branch(1)
            sp.wait_ge(s_kr, 1)
            for h in range(1, B_HEADS):
                sp.dma_start(KM[64:96, h * S:(h + 1) * S], KM[64:96, 0:S]).then_inc(s_krd, 16)
            sp.wait_ge(s_lg, 64)
            aq = AQ64[0:64, :].rearrange("p (i e n) -> p i e n", e=2, n=64)
            for e in range(2):
                sp.dma_start(aq[:, :, e, :], AQP[64 * e:64 * e + 64, :].rearrange("p (i n) -> p i n", n=64)).then_inc(s_aq, 16)
            sp.dma_start(POSB[:, :].bitcast(I32), positions_2.partition_broadcast(P)).then_inc(s_c4, 16)
            sp.dma_start(TAB[0:BUCKETS, :], rel_bias_2).then_inc(s_c4, 16)
            c = CONST_AT["sel"][0]
            sp.dma_start(CST[:, :], const[:, c:c + 1664]).then_inc(s_c4, 16)
            sp.wait_ge(s_pv, 128)
            for j in range(2):
                sp.wait_ge(s_gs[j], 128)

            def load_gates(m):
                if m >= 4:
                    sp.wait_ge(s_evv, GATED0 + m - 3)
                t = 8 * (m % 2) + 2 * (m // 2)
                sp.dma_start(GB[m % 4][:, :].rearrange("p (t s) -> p t s", t=2),
                             gs[t:t + 2].rearrange("t p s -> p t s")).then_inc(s_g[m % 4], 16)

            for m in range(8):
                load_gates(m)
                if m >= 2:
                    load_branch(m)
            sp.wait_ge(s_lo, Z_PARTS + KC)
            sp.wait_ge(s_xs, 32)
            sp.dma_start(X[:, :], xs).then_inc(s_xr, 16)
            for i in range(8):
                w = OUT0 + i
                sp.wait_ge(s_w, w - 1)
                sp.dma_start(k_n(RAW[w % 2], KC, P), w_tile(w_out_2, 0, KC, i * P, P)).then_inc(s_raw[w % 2], 16)
            mlp_loads(M2, w_ff1_2, w_ff2_2)
            for t in range(NB):
                sp.wait_ge(s_fo, t + 1)
                sp.dma_start(out[t * P:(t + 1) * P, :], OT[t % 2][:, :]).then_inc(s_out[t % 2], 16)
            for j in range(2):
                sp.wait_ge(s_out[j], 16 * NB // 2)

        @block.gpsimd
        def _(pool):
            def split(j, w, loads, n=1024, free=True):
                pool.wait_ge(s_raw[j], 16 * loads)
                if free:
                    pool.wait_ge(s_mm, w - 1)
                nc.gpsimd.tensor_add(WHI[j][:, 0:n], RAW[j][:, 0:n], ZERO[:, 0:1].to_broadcast([P, n])).then_inc(s_whi, 1)
                pool.wait_ge(s_whi, w + 1)
                nc.gpsimd.tensor_sub(WLO[j][:, 0:n], RAW[j][:, 0:n], WHI[j][:, 0:n].bitcast(F32)).then_inc(s_w, 1)

            nc.gpsimd.memset(ZERO[:, :], 0.0).then_inc(s_zero, 1)
            pool.wait_ge(s_zero, 1)
            for w in range(W_OUT0 + 8):
                split(w % 2, w, w // 2 + 1, free=w >= 2)

            def mlp_splits(m):
                with pool.Fori(0, GROUPS) as g:
                    for i in range(8):
                        split(i % 2, 8 * g + (m.w + i), 4 * g + loads(m.w + i))

            mlp_splits(M1)

            for i in range(len(Z_TILES)):
                w = Z0 + i
                split(w % 2, w, loads(w))
                if i == 5:
                    for b in range(2, NB):
                        pool.wait_ge(s_idx, IDX_HEADS * (b - 1))
                        a = SCORE_AT[b] + P * b
                        nc.gpsimd.affine_select(out=SCO[:, a:a + P], in_=SCO[:, a:a + P], compare_op=ALU.is_ge,
                                                fill=HIDDEN, base=0, pattern=[[-1, P]],
                                                channel_multiplier=1).then_inc(s_diag, 1)
            for w in range(BR0, MLP2):
                split(w % 2, w, loads(w))
            mlp_splits(M2)

        @block.tensor
        def _(pe):
            mm = nc.tensor.matmul

            def transpose(dst, src, n=P):
                return nc.tensor.transpose(dst, src, ident[0:n, 0:n])

            def product(w, first_of=None):
                pe.wait_ge(s_w, w + 1)
                if w >= 2:
                    pe.wait_ge(*reads(w - 2))
                hi, lo = k_n(WHI[w % 2], KC, P), k_n(WLO[w % 2], KC, P)
                b = w_bank(w)
                for k in range(KC):
                    if first_of is not None:
                        pe.wait_ge(s_lo, first_of + k + 1)
                    for n, (wt, a) in enumerate(((hi, H), (hi, L), (lo, H))):
                        for t in range(2):
                            last = mm(bank(b + t), wt[:, k, :], a[:, k * S + t * HALF:k * S + (t + 1) * HALF],
                                      start=(k == 0 and n == 0), stop=(k == KC - 1 and n == 2))
                last.then_inc(s_mm, 1)

            def sums(r, acc, b):
                for t in range(NB):
                    last = mm(bank(b)[:, t:t + 1], acc[:, t * P:(t + 1) * P], ones, start=True, stop=True)
                last.then_inc(s_ss, 1)

            def spread(r, b):
                pe.wait_ge(s_rs, r + 1)
                for t in range(NB):
                    last = mm(bank(b, 2)[:, t * P:(t + 1) * P], RS[:, t:t + 1].to_broadcast([P, P]), ident,
                              start=True, stop=True)
                last.then_inc(s_bc, 1)

            pe.wait_ge(s_const, 80)
            transpose(bank(7)[:, 0:NVA], STG[0:NVA, 0:P], NVA)
            transpose(bank(7)[:, NVA:NVA + NVB], STG[0:NVB, P:2 * P], NVB).then_inc(s_vt, 1)
            pe.wait_ge(s_x, 16)
            for k in range(KC):
                if k >= 2:
                    pe.wait_ge(s_sq, k - 1)
                for t in range(NB):
                    last = transpose(bank(2 * (k % 2), 2)[:, t * P:(t + 1) * P], XT[:, t * D + k * P:t * D + (k + 1) * P])
                last.then_inc(s_xt, 1)
            pe.wait_ge(s_acc, KC)
            pe.wait_ge(s_vec, 1)
            sums(0, ACC, 7)

            def ada(n):
                pe.wait_ge(s_ada_in[n % 4], 16 * (n // 4 + 1))
                for k in range(KC):
                    last = mm(bank(6)[:, n:n + 1], ADA[n % 4][:, k * P:(k + 1) * P], SILC[:, k:k + 1],
                              start=(k == 0), stop=(k == KC - 1))
                last.then_inc(s_ada, 1)

            pe.wait_ge(s_silc, 1)
            spread(0, 2)
            for n in range(ADA_FIRST):
                ada(n)
            n_ada = ADA_FIRST

            def ret_a(h):
                pe.wait_ge(*reads(12 + 4 * h + 2))
                if h:
                    pe.wait_ge(s_r_og, h)
                for t in range(NB):
                    last = transpose(bank(2, 2)[:, t * P:(t + 1) * P], R_VT[:, t * P:(t + 1) * P])
                last.then_inc(s_r_vT, 1)
                pe.wait_ge(s_r_k, h + 1)
                if h:
                    pe.wait_ge(s_ret_y, h)
                else:
                    pe.wait_ge(s_mod, 1)
                for t in range(NB):
                    last = transpose(bank(6, 2)[:, t * P:(t + 1) * P], R_KR[:, t * P:(t + 1) * P])
                last.then_inc(s_r_kT, 1)
                pe.wait_ge(s_r_q, h + 1)
                pe.wait_ge(s_r_vtok, h + 1)
                for t in range(NB):
                    last = mm(bank(2, 2)[:, t * P:(t + 1) * P], R_KR[:, t * P:(t + 1) * P],
                              R_QR[:, t * P:(t + 1) * P], start=True, stop=True)
                last.then_inc(s_r_sc, 1)
                pe.wait_ge(s_r_ktok, h + 1)
                for t in range(NB - 1):
                    last = mm(bank(6, 2)[:, t * P:(t + 1) * P], R_KTOK[:, t * P:(t + 1) * P],
                              R_VTOK[:, t * P:(t + 1) * P], start=True, stop=True)
                last.then_inc(s_r_kv, 1)

            def ret_b(h):
                pe.wait_ge(s_r_sd, h + 1)
                pe.wait_ge(s_r_st, h + 1)
                pe.wait_ge(s_r_qd, h + 1)
                for t in range(NB):
                    o = bank(2, 2)[:, t * P:(t + 1) * P]
                    last = mm(o, R_VTOK[:, t * P:(t + 1) * P], R_SD[:, t * P:(t + 1) * P],
                              start=True, stop=(t == 0))
                    if t:
                        last = mm(o, R_ST[:, (t - 1) * P:t * P], R_QD[:, t * P:(t + 1) * P],
                                  start=False, stop=True)
                last.then_inc(s_r_o, 1)

            def ret_c(h):
                pe.wait_ge(s_r_sq, h + 1)
                sums(1 + h, R_SQ, 6)

            for w, (kind, h, _) in enumerate(W_IN):
                product(w, 0 if w == 0 else None)
                for _ in range(ADA_AFTER.get(w, 0)):
                    if n_ada < 48:
                        ada(n_ada)
                        n_ada += 1
                if kind == "q" and h:
                    ret_b(h - 1)
                if kind == "k" and h:
                    ret_c(h - 1)
                if kind == "v" and h:
                    spread(h, 6)
                if kind == "g":
                    ret_a(h)
            ret_b(RET_HEADS - 1)
            ret_c(RET_HEADS - 1)
            spread(RET_HEADS, 6)
            for i in range(8):
                product(W_OUT0 + i, KC if i == 0 else None)

            def norm_products(r, squares):
                pe.wait_ge(s_acc, squares)
                sums(r, ACC, 6)
                spread(r, 2)

            def mlp_products(m):
                pe.wait_ge(s_eva, m.act)
                pe.wait_ge(s_evv, m.dve)

                def group(g, first):
                    for i in range(8):
                        w = 8 * g + (m.w + i)
                        pe.wait_ge(s_w, w + 1)
                        if i < 2:
                            if not first:
                                pe.wait_ge(s_evv, 4 * g + (m.dve + i - 1))
                        elif i < 6:
                            pe.wait_ge(s_eva, 4 * g + (m.act + i - 1))
                        else:
                            pe.wait_ge(s_evv, 4 * g + (m.dve + i - 5))
                        b = 4 * (i % 2)
                        if i < 4:
                            hi, lo = k_n(WHI[i % 2], KC, P), k_n(WLO[i % 2], KC, P)
                            for k in range(KC):
                                if first and i == 0:
                                    pe.wait_ge(s_lo, m.parts - KC + k + 1)
                                for n, (wt, a) in enumerate(((hi, H), (hi, L), (lo, H))):
                                    for t in range(2):
                                        last = mm(bank(b + t), wt[:, k, :], a[:, k * S + t * HALF:k * S + (t + 1) * HALF],
                                                  start=(k == 0 and n == 0), stop=(k == KC - 1 and n == 2))
                        else:
                            hi, lo = k_n(WHI[i % 2], 4, 256), k_n(WLO[i % 2], 4, 256)
                            for k in range(4):
                                if i == 4:
                                    pe.wait_ge(s_lo, 4 * g + (m.parts + k + 1))
                                for c in range(2):
                                    for n, (wt, a) in enumerate(((hi, FH), (hi, FL), (lo, FH))):
                                        for t in range(2):
                                            last = mm(bank(b + 2 * c + t), wt[:, k, c * P:(c + 1) * P],
                                                      a[:, k * S + t * HALF:k * S + (t + 1) * HALF],
                                                      start=(k == 0 and n == 0), stop=(k == 3 and n == 2))
                        last.then_inc(s_mm, 1)

                group(0, True)
                with pe.Fori(1, GROUPS) as g:
                    group(g, False)

            norm_products(5, 2 * KC)
            norm_products(6, 3 * KC)
            mlp_products(M1)
            norm_products(7, 4 * KC)
            norm_products(8, 5 * KC)

            def index_scores():
                pe.wait_ge(*reads(Z0 + 3))
                for t in range(NB):
                    last = transpose(bank(7)[:, 4 * t:4 * t + 4], IWT[0:4, t * P:(t + 1) * P], 4)
                last.then_inc(s_iwt, 1)
                m = 0
                for b in range(2, NB):
                    w = P * (b + 1)
                    for h in range(IDX_HEADS):
                        if m >= 2:
                            pe.wait_ge(s_rel, m - 1)
                        if m == 1:
                            pe.wait_ge(s_iw, 1)
                        rows = slice(64 * (h % 2), 64 * (h % 2) + 64)
                        q0 = (h // 2) * S + b * P
                        for c in range(0, w, HALF):
                            n = min(HALF, w - c)
                            last = mm(bank(2 + 4 * (m % 2), 2)[:, c:c + n], IQB[rows, q0:q0 + P], IKB[rows, c:c + n],
                                      start=True, stop=True)
                        last.then_inc(s_ixp, 1)
                        m += 1

            for i in range(len(Z_TILES)):
                product(Z0 + i, Z_PARTS - KC if i == 0 else None)
                if i == 3:
                    index_scores()

            for n, r in enumerate((9, 10)):
                pe.wait_ge(s_lacc, n + 1)
                for t in range(NB):
                    last = mm(bank(6 + n)[:, t:t + 1], (RT[0] if n == 0 else IWT)[:, t * P:(t + 1) * P], ones,
                              start=True, stop=True)
                last.then_inc(s_ss, 1)
                spread(r, 2 + 2 * n - (2 if n else 0))
            pe.wait_ge(s_wuq, 8 * 16)
            pe.wait_ge(s_eva, M2.act)
            for u in range(UPS):
                if u == 0:
                    pe.wait_ge(s_lat, 3)
                if u >= 4:
                    pe.wait_ge(s_upa, u - 3)
                    if u - 4 >= 8:
                        pe.wait_ge(s_upd, u - 11)
                b = bank(2 * (u % 4), 2)
                if u < 4:
                    wt = WUKV[:, P * u:P * (u + 1)]
                    for t in range(2):
                        last = mm(b[:, t * HALF:(t + 1) * HALF], wt, CKVB[:, t * HALF:(t + 1) * HALF], start=True, stop=True)
                elif u < 8:
                    wt = WUKV[:, HALF:]
                    for t in range(2):
                        tok = (2 * (u - 4) + t) * P
                        last = mm(b[:, t * HALF:(t + 1) * HALF], CKVB[:, tok:tok + P], wt, start=True, stop=True)
                elif u < 16:
                    for k in range(2):
                        wt = WUQ[:, k * S + (u - 8) * P:k * S + (u - 7) * P]
                        for t in range(2):
                            last = mm(b[:, t * HALF:(t + 1) * HALF], wt, CQB[:, k * S + t * HALF:k * S + (t + 1) * HALF],
                                      start=(k == 0), stop=(k == 1))
                else:
                    for t in range(NB):
                        last = transpose(b[:, t * A_DIM:(t + 1) * A_DIM], AVKR[0:64, t * P:(t + 1) * P], 64)
                last.then_inc(s_up, 1)

            def logits(n):
                b = ATT[n][0]
                w = P * (b + 1)
                dst = bank(2 * (n % 2), 2)
                if n >= 2:
                    pe.wait_ge(s_exp, n - 1)
                if n < 64:
                    h = ATT[n][1]
                    for c in range(0, w, HALF):
                        cw = min(HALF, w - c)
                        end = c + cw == w
                        last = mm(dst[:, c:c + cw], QM[0:B_QK, h * S + b * P:h * S + (b + 1) * P],
                                  KM[0:B_QK, h * S + c:h * S + c + cw], start=True, stop=not end)
                        if end:
                            last = mm(dst[:, w - P:w], IDB[:, :], TRB[:, :], start=False, stop=True)
                else:
                    i = n - 64
                    pe.wait_ge(s_step, NSTEP * (i + 1))
                    q = AQ64[0:64, i * P:(i + 1) * P]
                    for c in range(0, w, HALF):
                        cw = min(HALF, w - c)
                        mm(dst[:, c:c + cw], q, AKB[0:64, c:c + cw], start=True, stop=False)
                        mm(dst[:, c:c + cw], SELB[:, (i % NB) * P:(i % NB + 1) * P],
                           MB[:, MASK_AT[b] + c:MASK_AT[b] + c + cw], start=False, stop=False)
                        for g in range(NSTEP):
                            for part in (DHI, DLO):
                                last = mm(dst[:, c:c + cw], part[:, g * P:(g + 1) * P],
                                          STEP[i % 2][:, g * S + c:g * S + c + cw], start=False,
                                          stop=(g == NSTEP - 1 and part is DLO))
                last.then_inc(s_lg, 1)

            def probs_t(n):
                pe.wait_ge(s_exp, n + 1)
                if n:
                    pe.wait_ge(s_pte, n)
                if n // 16 >= 1 and n < 64 and n % 16 == 0:
                    pe.wait_ge(s_bte, n // 16)
                if n >= 64 and n % 8 == 0:
                    pe.wait_ge(s_bte, 4 + (n - 64) // 8)
                for t in range(ATT[n][0] + 1):
                    last = transpose(bank(4, 2)[:, t * P:(t + 1) * P], PB[n % 2][:, t * P:(t + 1) * P])
                last.then_inc(s_pt, 1)

            def attend(n):
                b = ATT[n][0]
                pe.wait_ge(s_pte, n + 1)
                if n >= 2:
                    pe.wait_ge(s_oe, n - 1)
                for t in range(b + 1):
                    if n < 64:
                        v = VM[:, t * HALF + ATT[n][1] * B_V:t * HALF + (ATT[n][1] + 1) * B_V]
                    else:
                        v = VA[:, t * A_DIM:(t + 1) * A_DIM]
                    last = mm(bank(6 + n % 2)[:, 0:64], PTS[n % 2][:, t * P:(t + 1) * P], v,
                              start=(t == 0), stop=(t == b))
                last.then_inc(s_pv, 1)

            def back(j):
                pe.wait_ge(s_oe, 16 * (j + 1) if j < 4 else 64 + 8 * (j - 3))
                pe.wait_ge(s_pte, 16 * (j + 1) if j < 4 else 64 + 8 * (j - 3))
                for t in range(NB):
                    if j < 4:
                        last = transpose(bank(4, 2)[:, t * P:(t + 1) * P], OB[:, t * P:(t + 1) * P])
                    else:
                        last = transpose(bank(4, 2)[0:64, t * P:(t + 1) * P], OB[:, t * 64:(t + 1) * 64])
                last.then_inc(s_bt, 1)

            pe.wait_ge(s_upa, UPS)
            pe.wait_ge(s_upd, 8)
            pe.wait_ge(s_q, 8)
            pe.wait_ge(s_krd, 7 * 16)
            for half in range(2):
                n0, n1 = 64 * half, 64 * half + 64
                if half:
                    pe.wait_ge(s_c4, 48)
                    pe.wait_ge(s_oe, 64)
                    mm(bank(7)[:, 0:8], CST[0:BUCKETS, 1024:1152], TAB[0:BUCKETS, :], start=True, stop=True).then_inc(s_tp, 1)
                    pe.wait_ge(s_tpd, 1)
                    pe.wait_ge(s_aq, 32)
                logits(n0)
                for n in range(n0, n1):
                    if n + 1 < n1:
                        logits(n + 1)
                    if n > n0:
                        attend(n - 1)
                        if BACK.get(n - 1) is not None:
                            back(BACK[n - 1])
                    probs_t(n)
                attend(n1 - 1)
                back(BACK[n1 - 1])

            def wide(w, a0, first_of):
                pe.wait_ge(s_w, w + 1)
                pe.wait_ge(*reads(w - 2))
                hi, lo = k_n(WHI[w % 2], 4, 256), k_n(WLO[w % 2], 4, 256)
                for k in range(4):
                    if first_of is not None:
                        pe.wait_ge(s_lo, first_of + k + 1)
                    for c in range(2):
                        for n, (wt, a) in enumerate(((hi, H), (hi, L), (lo, H))):
                            for t in range(2):
                                last = mm(bank(w_bank(w) + 2 * c + t), wt[:, k, c * P:(c + 1) * P],
                                          a[:, (a0 + k) * S + t * HALF:(a0 + k) * S + (t + 1) * HALF],
                                          start=(k == 0 and n == 0), stop=(k == 3 and n == 2))
                last.then_inc(s_mm, 1)

            pe.wait_ge(s_bte, 12)
            pe.wait_ge(s_oe, 128)
            for m in range(8):
                wide(BR0 + m, 4 * (m % 2), Z_PARTS + 4 * (m % 2) if m < 2 else None)
            for i in range(8):
                product(OUT0 + i, Z_PARTS + KC if i == 0 else None)
            norm_products(11, 6 * KC)
            mlp_products(M2)
            norm_products(12, 7 * KC)
            for t in range(NB):
                if t == 0:
                    pe.wait_ge(s_fin, KC)
                if t >= 2:
                    pe.wait_ge(s_fo, t - 1)
                for k in range(KC):
                    last = transpose(bank(4 * (t % 2), 2)[:, k * P:(k + 1) * P], X[:, k * S + t * P:k * S + (t + 1) * P])
                last.then_inc(s_ft, 1)

        @block.scalar
        def _(act):
            A = nc.scalar.activation

            def copy_out(w, dst, fn=ACT.Copy, **kw):
                act.wait_ge(s_mm, w + 1)
                return A(dst, bank(w_bank(w), 2), fn, **kw).then_inc(s_eva, 1)

            def root(r, b, n=D):
                act.wait_ge(s_ss, r + 1)
                A(SS[:, :], bank(b)[:, 0:NB], ACT.Sqrt, bias=eps, scale=1.0 / n).then_inc(s_std, 1)

            act.wait_ge(s_vt, 1)
            A(VEC[:, 0:NVA + NVB], bank(7)[:, 0:NVA + NVB], ACT.Copy).then_inc(s_vec, 1)
            act.wait_ge(s_vec, 1)
            A(SILC[:, :], VEC[:, 0:8], ACT.Silu).then_inc(s_silc, 1)
            act.wait_ge(s_red, 1)
            A(ROT_S[:, :], CT[:, :], ACT.Sin, scale=sgn1).then_inc(s_sin, 1)
            A(ROT_C[:, :], CT[:, :], ACT.Sin, scale=0.5).then_inc(s_sin, 1)
            for k in range(KC):
                act.wait_ge(s_xt, k + 1)
                A(chunk(X, k), bank(2 * (k % 2), 2), ACT.Copy).then_inc(s_xc, 1)
                if k >= 2:
                    act.wait_ge(s_acc, k - 1)
                A(SQ[k % 2][:, :], bank(2 * (k % 2), 2), ACT.Square).then_inc(s_sq, 1)
            root(0, 7)

            def high(first):
                for k in range(KC):
                    act.wait_ge(s_h32, first + k + 1)
                    A(chunk(H, k), SQ[k % 2][:, :], ACT.Copy).then_inc(s_hi, 1)

            high(0)
            for w, (kind, h, _) in enumerate(W_IN):
                if kind == "xin":
                    if h:
                        act.wait_ge(*reads(w - 2))
                    copy_out(w, CX[:, :])
                elif kind == "v":
                    copy_out(w, R_VT[:, :])
                elif kind == "g":
                    if h:
                        act.wait_ge(s_r_og, h)
                    copy_out(w, R_G[:, :], ACT.Silu)
                    act.wait_ge(s_r_vT, h + 1)
                    A(R_VTOK[:, :], bank(2, 2), ACT.Copy).then_inc(s_r_vtok, 1)
                    act.wait_ge(s_r_kT, h + 1)
                    A(R_KTOK[:, :], bank(6, 2), ACT.Copy, scale=DEC[:, 1024 + h:1025 + h]).then_inc(s_r_ktok, 1)
                    if h == RET_HEADS - 1:
                        act.wait_ge(s_mm, W_OUT0)
                        for k in range(4):
                            A(chunk(H, k), chunk(Y, k), ACT.Copy).then_inc(s_hi, 1)
                    act.wait_ge(s_r_o, h + 1)
                    A(R_SQ[:, :], bank(2, 2), ACT.Square).then_inc(s_r_sq, 1)
                    act.wait_ge(s_ss, 1 + h + 1)
                    A(SS[:, :], bank(6)[:, 0:NB], ACT.Sqrt, bias=eps, scale=1.0 / RET_DIM).then_inc(s_std, 1)
            for k in range(4, KC):
                if k == KC - 1:
                    act.wait_ge(s_ret_y, RET_HEADS)
                A(chunk(H, k), chunk(Y, k), ACT.Copy).then_inc(s_hi, 1)
            def square(n, src):
                act.wait_ge(s_acc, n - 1)
                A(sq_buffer(n)[:, :], src, ACT.Square).then_inc(s_sq, 1)

            for i in range(8):
                w = W_OUT0 + i
                if i == 0:
                    act.wait_ge(s_lo, 2 * KC)
                act.wait_ge(s_mm, w + 1)
                square(KC + i, bank(w_bank(w), 2))
                copy_out(w, chunk(Y, i))

            def residual_squares(n, first_x):
                for k in range(KC):
                    act.wait_ge(s_xn, first_x + k + 1)
                    square(n + k, chunk(X, k))

            root(5, 6)
            residual_squares(2 * KC, 0)
            root(6, 6)
            high(KC)

            def mlp_act(m):

                def group(g, first):
                    for i in range(4):
                        act.wait_ge(s_mm, 8 * g + (m.w + i + 1))
                        if not (first and i < 2):
                            act.wait_ge(s_h32, 4 * g + (m.f32 + i - 1))
                        A(RL[i % 2][:, :], bank(4 * (i % 2), 2), ACT.Relu).then_inc(s_eva, 1)
                        act.wait_ge(s_eva, 4 * g + (m.act + i + 1))
                        A(chunk(FH, i), RL[i % 2][:, :], ACT.Square).then_inc(s_hi, 1)

                group(0, True)
                with act.Fori(1, GROUPS) as g:
                    group(g, False)

            mlp_act(M1)
            for k in range(KC):
                act.wait_ge(s_evv, M1.dve + 4 * (GROUPS - 1) + k // 2 + 1)
                square(3 * KC + k, chunk(Y, k))
            root(7, 6)
            residual_squares(4 * KC, KC)
            root(8, 6)
            high(2 * KC + 4 * GROUPS)

            def read_tile(w, pieces):
                act.wait_ge(s_mm, w + 1)
                for n, (dst, rows, kw) in enumerate(pieces):
                    src = bank(w_bank(w), 2, rows)
                    if "split" in kw:
                        src = src.rearrange("p (i q) -> p i q", q=kw.pop("split"))
                    ins = A(dst, src, kw.pop("fn", ACT.Copy), **kw)
                    ins.then_inc(s_eva if n == len(pieces) - 1 else s_act, 1)

            every = slice(0, P)
            top, low_rows = slice(0, 64), slice(64, P)
            act.wait_ge(s_xs, 32)
            for i, (kind, c0) in enumerate(Z_TILES):
                w = Z0 + i
                if kind == "iw":
                    read_tile(w, [(IWT[0:4, :], slice(0, 4), {})])
                    act.wait_ge(s_red2, 1)
                    A(T2S[:, :], GST[0][:, :], ACT.Sin, scale=sgn2).then_inc(s_sin2, 1)
                    A(T2C[:, :], GST[0][:, :], ACT.Sin, scale=0.5).then_inc(s_sin2, 1)
                elif kind == "iq":
                    read_tile(w, [(chunk(IQB, (c0 - IQ) // P), every, {})])
                elif kind == "akik":
                    read_tile(w, [(AKB[0:64, :], top, {}), (IKB[64:P, :], low_rows, {}), (IKB[0:64, :], low_rows, {})])
                    m = 0
                    for b in range(2, NB):
                        n = P * (b + 1)
                        for h in range(IDX_HEADS):
                            act.wait_ge(s_ixp, m + 1)
                            if m >= 2:
                                act.wait_ge(s_idx, m - 1)
                            A(RT[m % 2][:, 0:n], bank(2 + 4 * (m % 2), 2)[:, 0:n], ACT.Relu,
                              scale=float(A_DIM) ** -0.5).then_inc(s_rel, 1)
                            m += 1
                elif kind == "avkr":
                    read_tile(w, [(AVKR[:, :], every, {})])
                elif kind == "aq":
                    c = (c0 - AQ) // P
                    read_tile(w, [(AQP[:, :].rearrange("p (i c q) -> p c i q", c=4, q=QT)[:, c], every,
                                   {"scale": float(A_DIM) ** -0.5, "split": QT})])
                elif kind == "cq":
                    read_tile(w, [(chunk(CQB, (c0 - CQ) // P), every, {})])
                elif kind == "ckv":
                    read_tile(w, [(CKVB[:, :], every, {})])
                else:
                    g = i - Z_GATE
                    if g >= 2:
                        act.wait_ge(s_gs[g % 2], 16 * (g // 2))
                    else:
                        act.wait_ge(s_sin2, 2)
                    read_tile(w, [(GST[g % 2][:, :], every, {"fn": ACT.Sigmoid, "bias": vcol("b_gate_2", g)})])
                    act.wait_ge(*reads(w))
                    act.dma_start(gs[g], GST[g % 2][:, :]).then_inc(s_gs[g % 2], 16)
            root(9, 6, 2 * P)
            root(10, 7, P)
            for u in range(UPS):
                act.wait_ge(s_up, u + 1)
                b = bank(2 * (u % 4), 2)
                if u < 4:
                    A(chunk(KM, 2 * u, rows=top), b[0:64, :], ACT.Copy).then_inc(s_act, 1)
                    A(chunk(KM, 2 * u + 1, rows=top), b[64:P, :], ACT.Copy).then_inc(s_upa, 1)
                elif u < 8:
                    A(chunk(VM, u - 4), b, ACT.Copy).then_inc(s_upa, 1)
                elif u < 16:
                    A(chunk(QM, u - 8, rows=top), b[0:64, :], ACT.Copy).then_inc(s_upa, 1)
                else:
                    act.wait_ge(s_mb, 4)
                    A(VA[:, :], b[:, 0:HALF], ACT.Copy).then_inc(s_upa, 1)

            def probs_copied(n):
                act.wait_ge(s_pt, n + 1)
                if n >= 2:
                    act.wait_ge(s_pv, n - 1)
                if n < 2:
                    for j in range(2):
                        act.wait_ge(s_gs[j], 128)
                w = P * (ATT[n][0] + 1)
                A(PTS[n % 2][:, 0:w], bank(4, 2)[:, 0:w], ACT.Copy).then_inc(s_pte, 1)

            def back_copied(j):
                act.wait_ge(s_bt, j + 1)
                if j < 4:
                    A(chunk(YB, j), bank(4, 2), ACT.Copy).then_inc(s_bte, 1)
                else:
                    b = j - 4
                    src = bank(4, 2)[0:64, :].rearrange("p (r e c q) -> p r e c q", r=NB, c=4, e=2)
                    for e in range(2):
                        dst = YA[64 * e:64 * e + 64, :].rearrange("p (c b r q) -> p b r c q", c=4, b=NB, r=NB)[:, b]
                        A(dst, src[:, :, e], ACT.Copy).then_inc(s_act if e == 0 else s_bte, 1)

            for n in range(128):
                act.wait_ge(s_nm, n + 1)
                if n >= 2:
                    act.wait_ge(s_pt, n - 1)
                    act.wait_ge(s_oe, n - 1)
                w = P * (ATT[n][0] + 1)
                A(PB[n % 2][:, 0:w], bank(2 * (n % 2), 2)[:, 0:w], ACT.Exp, bias=NMX[:, n % 2:n % 2 + 1],
                  scale=float(B_QK) ** -0.5 if n < 64 else 1.0, accum_out=RSUM[:, n % 2:n % 2 + 1]).then_inc(s_exp, 1)
                if n and n != 64:
                    probs_copied(n - 1)
                    if n - 1 in BACK:
                        back_copied(BACK[n - 1])
                if n in (63, 127):
                    probs_copied(n)
                    back_copied(BACK[n])
            act.wait_ge(s_bte, 12)
            for k in range(KC):
                A(chunk(H, k), chunk(YA, k) if k < 4 else chunk(YB, k - 4), ACT.Copy).then_inc(s_hi, 1)
            act.wait_ge(s_mm, OUT0)
            for k in range(KC):
                act.wait_ge(s_evv, reads(BR0 + 2 * (k // 2) + 1)[1])
                A(chunk(H, k), chunk(Y, k), ACT.Copy).then_inc(s_hi, 1)
            for i in range(8):
                act.wait_ge(*reads(OUT0 + i))
                square(5 * KC + i, chunk(X, i))
            root(11, 6)
            high(M2.f32 - KC)
            mlp_act(M2)
            for k in range(KC):
                act.wait_ge(s_evv, M2.dve + 4 * (GROUPS - 1) + k // 2 + 1)
                square(6 * KC + k, chunk(X, k))
            root(12, 6)
            for t in range(NB):
                act.wait_ge(s_ft, t + 1)
                if t >= 2:
                    act.wait_ge(s_out[t % 2], 16 * (t // 2))
                A(OT[t % 2][:, :], bank(4 * (t % 2), 2), ACT.Copy).then_inc(s_fo, 1)


        @block.vector
        def _(dve):
            V = nc.vector
            own = [0]

            def link(ins):
                own[0] += 1
                ins.then_inc(s_dve, 1)
                dve.wait_ge(s_dve, own[0])

            def recip(r):
                dve.wait_ge(s_std, r + 1)
                V.reciprocal(RS[:, :], SS[:, :]).then_inc(s_rs, 1)

            def low(src, k, first):
                dve.wait_ge(s_hi, first + k + 1)
                V.tensor_sub(chunk(L, k), src, chunk(H, k).bitcast(F32)).then_inc(s_lo, 1)

            def reduce_angle(t, tmp, inv):
                link(V.tensor_scalar(t, t, inv, None, ALU.mult))
                link(V.tensor_scalar(tmp, t, 1.0 / (2 * np.pi), MAGIC, ALU.mult, ALU.add))
                link(V.tensor_scalar(tmp, tmp, MAGIC, None, ALU.subtract))
                for c in TWO_PI:
                    link(V.scalar_tensor_tensor(t, tmp, -c, t, ALU.mult, ALU.add))

            dve.wait_ge(s_rot, 32)
            link(V.tensor_copy(CT[:, :], ROT_S[:, :].bitcast(I32)))
            dve.wait_ge(s_const, 80)
            link(V.tensor_copy(IDB[:, :], ident))
            link(V.tensor_copy(TRB[:, :], STG[:, 2 * P:3 * P]))
            reduce_angle(CT[:, :], SQ[1][:, :], inv1)
            V.tensor_scalar(CT[:, :], CT[:, :], PI, -PI, ALU.min, ALU.max).then_inc(s_red, 1)

            def add_square(n):
                dve.wait_ge(s_sq, n + 1)
                if n:
                    dve.wait_ge(s_acc, n)
                if n % KC == 0:
                    V.tensor_copy(ACC[:, :], sq_buffer(n)[:, :]).then_inc(s_acc, 1)
                else:
                    V.tensor_add(ACC[:, :], ACC[:, :], sq_buffer(n)[:, :]).then_inc(s_acc, 1)

            for k in range(KC):
                add_square(k)
            dve.wait_ge(s_sin, 2)
            link(V.scalar_tensor_tensor(CT[:, :], ROT_C[:, :], -2.0, ROT_C[:, :], ALU.mult, ALU.mult))
            link(V.tensor_scalar(ROT_C[:, :], CT[:, :], 1.0, None, ALU.add))
            recip(0)
            link(V.memset(CU[:, 0:2], 0.0))

            def modulation(g):
                a = ADA_ORDER[8 * g]
                n = VCOL["b_ada"] + a
                link(V.tensor_tensor(MOD[:, 8 * g:8 * g + 8], bank(6)[:, 8 * g:8 * g + 8], VEC[:, n:n + 8], ALU.add))

            def gains(name):
                return VEC[:, VCOL[name]:VCOL[name] + 8]

            dve.wait_ge(s_vec, 1)
            dve.wait_ge(s_ada, ADA_FIRST)
            modulation(0)
            modulation(1)
            link(V.scalar_tensor_tensor(MODA[:, 0:8], MOD[:, 0:8], 1.0, gains("g_pre_mix"), ALU.add, ALU.mult))

            def norm_split(r, b, scale, shift, n32, first):
                dve.wait_ge(s_bc, r + 1)
                for k in range(KC + 1):
                    if k < KC:
                        if k:
                            dve.wait_ge(s_h32, n32 + k)
                        link(V.tensor_tensor(ACC[:, :], chunk(X, k), bank(b, 2), ALU.mult))
                        if k >= 2:
                            dve.wait_ge(s_hi, first + k - 1)
                        V.tensor_scalar(SQ[k % 2][:, :], ACC[:, :], scale(k), shift(k) if shift else None, ALU.mult,
                                        ALU.add if shift else ALU.bypass).then_inc(s_h32, 1)
                    if k:
                        low(SQ[(k - 1) % 2][:, :], k - 1, first)

            dve.wait_ge(s_xc, KC)
            norm_split(0, 2, lambda k: MODA[:, k:k + 1], lambda k: MOD[:, 8 + k:9 + k], 0, 0)

            def tap(j, i):
                return vcol("conv_w", 4 * i + j)

            def rotate(w, dst, scale, done):
                src = bank(w_bank(w), 2)
                dve.wait_ge(s_mm, w + 1)
                V.scalar_tensor_tensor(R_T[:, :], src, scale, ROT_C[:, :], ALU.mult, ALU.mult).then_inc(s_rt, 1)
                for lo in (0, 64):
                    hi = 64 - lo
                    ins = V.scalar_tensor_tensor(R_T2[lo:lo + 64, :], src[hi:hi + 64, :], scale,
                                                 ROT_S[hi:hi + 64, :], ALU.mult, ALU.mult)
                    ins.then_inc(s_rt if lo == 0 else s_evv, 1)
                dve.wait_ge(s_rt, 2 * rots[0] + 2)
                dve.wait_ge(*reads(w))
                rots[0] += 1
                V.tensor_add(dst[:, :], R_T[:, :], R_T2[:, :]).then_inc(done, 1)

            rots = [0]
            blocks3 = lambda t: t.rearrange("p (b n) -> p b n", b=NB)

            def repeated(t):
                return t.rearrange("p (o n) -> p o n", o=1).broadcast_to([P, NB, P])

            def ret_finish(h):
                dve.wait_ge(s_r_o, h + 1)
                dve.wait_ge(*reads(12 + 4 * h + 3))
                dve.wait_ge(s_r_sq, h + 1)
                V.tensor_tensor(R_OG[:, :], bank(2, 2), R_G[:, :], ALU.mult).then_inc(s_r_og, 1)
                recip(1 + h)

            def ret_out(h):
                dve.wait_ge(s_bc, h + 2)
                dve.wait_ge(s_r_og, h + 1)
                V.tensor_tensor(chunk(Y, CONV + h), R_OG[:, :], bank(6, 2), ALU.mult).then_inc(s_ret_y, 1)

            for w, (kind, h, _) in enumerate(W_IN):
                if kind == "c":
                    dve.wait_ge(s_mm, w + 1)
                    dve.wait_ge(*reads(w - 1))
                    V.tensor_tensor(CU[:, 2:S + 2], bank(w_bank(w), 2), CX[:, :], ALU.mult).then_inc(s_evv, 1)
                    dve.wait_ge(*reads(w))
                    link(V.tensor_scalar(CT[:, :], CU[:, 0:S], tap(h, 0), None, ALU.mult))
                    for i in (1, 2):
                        link(V.scalar_tensor_tensor(CT[:, :], CU[:, i:i + S], tap(h, i), CT[:, :], ALU.mult, ALU.add))
                elif kind == "b":
                    dve.wait_ge(s_mm, w + 1)
                    V.tensor_tensor(chunk(Y, h), bank(w_bank(w), 2), CT[:, :], ALU.mult).then_inc(s_evv, 1)
                    if h == CONV - 1:
                        dve.wait_ge(s_ada, 48)
                        for g in range(2, 6):
                            modulation(g)
                        V.tensor_tensor(MODA[:, 8:16], MOD[:, 16:24], gains("g_post_mix"), ALU.mult)
                        V.scalar_tensor_tensor(MODA[:, 16:24], MOD[:, 32:40], 1.0, gains("g_pre_mlp"), ALU.add, ALU.mult)
                        V.tensor_tensor(MODA[:, 24:32], MOD[:, 40:48], gains("g_post_mlp"), ALU.mult).then_inc(s_mod, 1)
                elif kind == "q":
                    rotate(w, R_QR, 1.0, s_r_q)
                    dve.wait_ge(s_r_q, h + 1)
                    if h:
                        dve.wait_ge(s_r_o, h)
                    V.tensor_tensor(blocks3(R_QD[:, :]), blocks3(R_QR[:, :]), repeated(DEC[:, 512 + h * P:512 + (h + 1) * P]),
                                    ALU.mult).then_inc(s_r_qd, 1)
                elif kind == "k":
                    rotate(w, R_KR, float(RET_DIM) ** -0.5, s_r_k)
                    if h:
                        ret_finish(h - 1)
                elif kind == "v":
                    if h:
                        ret_out(h - 1)
                elif kind == "g":
                    dve.wait_ge(s_r_sc, h + 1)
                    V.tensor_tensor(blocks3(R_SD[:, :]), blocks3(bank(2, 2)), repeated(DEC[:, h * P:(h + 1) * P]),
                                    ALU.mult).then_inc(s_r_sd, 1)
                    dve.wait_ge(s_r_kv, h + 1)
                    link(V.tensor_copy(R_ST[:, 0:P], bank(6)[:, 0:P]))
                    for t in range(1, NB - 1):
                        ins = V.scalar_tensor_tensor(R_ST[:, t * P:(t + 1) * P], R_ST[:, (t - 1) * P:t * P],
                                                     GAMMA_BLOCK[h], bank(6, 2)[:, t * P:(t + 1) * P], ALU.mult, ALU.add)
                        if t < NB - 2:
                            link(ins)
                    ins.then_inc(s_r_st, 1)
            h = RET_HEADS - 1
            for k in range(4):
                low(chunk(Y, k), k, KC)
            ret_finish(h)
            for k in range(4, KC - 1):
                low(chunk(Y, k), k, KC)
            ret_out(h)
            low(chunk(Y, KC - 1), KC - 1, KC)

            for k in range(KC):
                add_square(KC + k)

            def residual(r, gain, first_x, squares):
                recip(r)
                dve.wait_ge(s_bc, r + 1)
                for k in range(KC + 1):
                    if k < KC:
                        if first_x + k:
                            dve.wait_ge(s_xn, first_x + k)
                        link(V.tensor_tensor(CT[:, :], chunk(Y, k), bank(2, 2), ALU.mult))
                        V.scalar_tensor_tensor(chunk(X, k), CT[:, :], gain(k), chunk(X, k), ALU.mult,
                                               ALU.add).then_inc(s_xn, 1)
                    if k:
                        add_square(squares + k - 1)

            dve.wait_ge(s_xr, 16)
            dve.wait_ge(s_mod, 1)
            residual(5, lambda k: MODA[:, 8 + k:9 + k], 0, 2 * KC)
            recip(6)
            norm_split(6, 2, lambda k: MODA[:, 16 + k:17 + k], lambda k: MOD[:, 24 + k:25 + k], KC, 2 * KC)

            def mlp_dve(m, acc, fresh, squares):

                def group(g, first, last):
                    for i in range(4):
                        dve.wait_ge(s_eva, 4 * g + (m.act + i + 1))
                        if not (first and i == 0):
                            dve.wait_ge(s_lo, 4 * g + (m.parts + i))
                        V.tensor_tensor(FT[:, :], RL[i % 2][:, :], RL[i % 2][:, :], ALU.mult).then_inc(s_h32, 1)
                        dve.wait_ge(s_h32, 4 * g + (m.f32 + i + 1))
                        dve.wait_ge(s_hi, 4 * g + (m.parts + i + 1))
                        V.tensor_sub(chunk(FL, i), FT[:, :], chunk(FH, i).bitcast(F32)).then_inc(s_lo, 1)
                    for c in range(4):
                        dve.wait_ge(s_mm, 8 * g + (m.w + 4 + c + 1))
                        dst = chunk(acc, 2 * c, 2)
                        if first and fresh:
                            V.tensor_copy(dst, bank(4 * (c % 2), 4)).then_inc(s_evv, 1)
                        else:
                            dve.wait_ge(s_evv, 4 * g + (m.dve + c))
                            V.tensor_tensor(dst, dst, bank(4 * (c % 2), 4), ALU.add).then_inc(s_evv, 1)
                        if last:
                            for k in (2 * c - 1, 2 * c):
                                if k >= 0:
                                    add_square(squares + k)

                group(0, True, False)
                with dve.Fori(1, GROUPS - 1) as g:
                    group(g, False, False)
                group(GROUPS - 1, False, True)
                add_square(squares + KC - 1)

            mlp_dve(M1, Y, True, 3 * KC)
            residual(7, lambda k: MODA[:, 24 + k:25 + k], KC, 4 * KC)
            recip(8)
            norm_split(8, 2, lambda k: vcol("attn_norm_g_2", k), None, 2 * KC + 4 * GROUPS, 3 * KC + 4 * GROUPS)

            dve.wait_ge(s_pos2, 16)
            link(V.tensor_copy(GST[0][:, :], T2S[:, :].bitcast(I32)))
            reduce_angle(GST[0][:, :], GST[1][:, :], inv2)
            V.tensor_scalar(GST[0][:, :], GST[0][:, :], PI, -PI, ALU.min, ALU.max).then_inc(s_red2, 1)
            dve.wait_ge(s_sin2, 2)
            link(V.scalar_tensor_tensor(GST[1][:, :], T2C[:, :], -2.0, T2C[:, :], ALU.mult, ALU.mult))
            V.tensor_scalar(T2C[:, :], GST[1][:, :], 1.0, None, ALU.add).then_inc(s_sin2, 1)
            dve.wait_ge(s_iwt, 1)
            V.tensor_scalar(IWTOK[:, :], bank(7)[:, 0:32], float(IDX_HEADS) ** -0.5, None, ALU.mult).then_inc(s_iw, 1)
            dve.wait_ge(s_iw, 1)
            m = 0
            for b in range(2, NB):
                n = P * (b + 1)
                sc = SCO[:, SCORE_AT[b]:SCORE_AT[b] + n]
                for h in range(IDX_HEADS):
                    dve.wait_ge(s_rel, m + 1)
                    iw = IWTOK[:, 4 * b + h:4 * b + h + 1]
                    if h == 0:
                        V.tensor_scalar(sc, RT[m % 2][:, 0:n], iw, None, ALU.mult).then_inc(s_idx, 1)
                    else:
                        dve.wait_ge(s_idx, m)
                        V.scalar_tensor_tensor(sc, RT[m % 2][:, 0:n], iw, sc, ALU.mult, ALU.add).then_inc(s_idx, 1)
                    m += 1
            link(V.memset(MB[:, P:2 * P], 0.0))
            V.tensor_copy(MB[:, 0:P], TRB[:, :]).then_inc(s_mb, 1)
            V.tensor_copy(MB[:, 2 * P:3 * P], TRB[:, :]).then_inc(s_mb, 1)

            def take(b):
                sc = SCO[:, SCORE_AT[b]:SCORE_AT[b] + P * (b + 1)]
                link(V.max(TK[:, :], sc))
                link(V.match_replace(sc, TK[:, :], sc, TAKEN))

            def selected(b):
                n = P * (b + 1)
                V.tensor_scalar(MB[:, MASK_AT[b]:MASK_AT[b] + n], SCO[:, SCORE_AT[b]:SCORE_AT[b] + n], TAKEN, NEG,
                                ALU.not_equal, ALU.mult).then_inc(s_mb, 1)

            dve.wait_ge(s_diag, NB - 2)
            for b in range(2, NB - 1):
                for _ in range(TOPK // 8):
                    take(b)
                selected(b)

            dve.wait_ge(*reads(Z0 + Z_GATE - 1))
            link(V.tensor_mul(RT[0][:, :], chunk(CQB, 0), chunk(CQB, 0)))
            link(V.tensor_mul(RT[1][:, :], chunk(CQB, 1), chunk(CQB, 1)))
            V.tensor_add(RT[0][:, :], RT[0][:, :], RT[1][:, :]).then_inc(s_lacc, 1)
            V.tensor_mul(IWT[:, :], CKVB[:, :], CKVB[:, :]).then_inc(s_lacc, 1)
            recip(9)
            dve.wait_ge(s_bc, 10)
            for k in range(2):
                V.scalar_tensor_tensor(chunk(CQB, k), chunk(CQB, k), vcol("q_latent_norm_g_2", k), bank(2, 2), ALU.mult,
                                       ALU.mult).then_inc(s_lat, 1)
            recip(10)
            dve.wait_ge(s_bc, 11)
            V.scalar_tensor_tensor(CKVB[:, :], CKVB[:, :], vcol("kv_latent_norm_g_2", 0), bank(2, 2), ALU.mult,
                                   ALU.mult).then_inc(s_lat, 1)
            dve.wait_ge(s_mm, BR0)
            dve.wait_ge(s_up, 8)
            dve.wait_ge(s_sin2, 3)
            V.tensor_mul(PB[0][64:96, :], AVKR[64:96, :], T2C[64:96, :]).then_inc(s_kt, 1)
            V.tensor_mul(PB[1][64:96, :], AVKR[96:P, :], T2S[96:P, :]).then_inc(s_kt, 1)
            dve.wait_ge(s_kt, 2)
            V.tensor_add(KM[64:96, 0:S], PB[0][64:96, :], PB[1][64:96, :]).then_inc(s_kr, 1)
            for h in range(B_HEADS):
                u = 8 + h
                dve.wait_ge(s_up, u + 1)
                b = bank(2 * (u % 4), 2)
                dve.wait_ge(s_kr if h == 0 else s_q, 1 if h == 0 else h)
                V.tensor_mul(PB[0][64:96, :], b[64:96, :], T2C[64:96, :]).then_inc(s_kt, 1)
                V.tensor_mul(PB[1][64:96, :], b[96:P, :], T2S[96:P, :]).then_inc(s_upd, 1)
                dve.wait_ge(s_kt, 3 + h)
                dve.wait_ge(s_upd, h + 1)
                V.tensor_add(QM[64:96, h * S:(h + 1) * S], PB[0][64:96, :], PB[1][64:96, :]).then_inc(s_q, 1)

            def scaled(n):
                dve.wait_ge(s_pv, n + 1)
                if n >= 2:
                    dve.wait_ge(s_oe, n - 1)
                rinv = RINV[:, n % 2:n % 2 + 1]
                link(V.reciprocal(rinv, RSUM[:, n % 2:n % 2 + 1]))
                if n < 64:
                    at = ATT[n][0] * P + (n % 2) * 64
                    if n % 16 == 0 and n:
                        dve.wait_ge(s_bt, n // 16)
                else:
                    at = (n % 8) * 64
                    if n % 8 == 0:
                        dve.wait_ge(s_bt, 4 + (n - 64) // 8)
                V.tensor_scalar(OB[:, at:at + 64], bank(6 + n % 2)[:, 0:64], rinv, None, ALU.mult).then_inc(s_oe, 1)

            def steps_of(i):
                w = P * (i // NB + 1)
                if i >= 2:
                    dve.wait_ge(s_lg, 64 + i - 1)
                for g in range(NSTEP):
                    V.tensor_scalar(STEP[i % 2][:, g * S:g * S + w], POSB[:, 0:w], THR[:, NSTEP * i + g:NSTEP * i + g + 1],
                                    None, ALU.is_le).then_inc(s_step, 1)

            for n in range(128):
                if n == 64:
                    scaled(62)
                    scaled(63)
                    dve.wait_ge(s_c4, 48)
                    link(V.tensor_copy(POSB[:, :], POSB[:, :].bitcast(I32)))
                    link(V.tensor_copy(SELB[:, :], CST[:, 0:1024]))
                    for t in range(STEPQ):
                        rows = slice(BUCKETS * t, BUCKETS * (t + 1))
                        link(V.tensor_scalar(THR[rows, :], POSB[rows, t:S:STEPQ], steps[rows, :], None, ALU.subtract))
                    dve.wait_ge(s_tp, 1)
                    link(V.tensor_copy(DLT[:, :], bank(7)[:, 0:8]))
                    for g in range(NSTEP):
                        at = slice(g * P, (g + 1) * P)
                        view = lambda t: t.rearrange("p (e c q) -> p e c q", e=2, q=QT)
                        link(V.tensor_tensor(view(DF[:, at]), view(CST[:, 1152 + g * P:1152 + (g + 1) * P]),
                                             DLT[:, :].rearrange("p (c e o) -> p e c o", e=2, o=1).broadcast_to([P, 2, 4, QT]),
                                             ALU.mult))
                    link(V.tensor_copy(DHI[:, :], DF[:, :]))
                    V.tensor_sub(DLO[:, :], DF[:, :], DHI[:, :].bitcast(F32)).then_inc(s_tpd, 1)
                    dve.wait_ge(s_aq, 32)
                    steps_of(0)
                if n >= 64 and n + 1 < 128:
                    steps_of(n + 1 - 64)
                dve.wait_ge(s_lg, n + 1)
                w = P * (ATT[n][0] + 1)
                link(V.reduce_max(MXS[:, n % 2:n % 2 + 1], bank(2 * (n % 2), 2)[:, 0:w], AX))
                if n >= 2:
                    dve.wait_ge(s_exp, n - 1)
                V.tensor_scalar(NMX[:, n % 2:n % 2 + 1], MXS[:, n % 2:n % 2 + 1], -(float(B_QK) ** -0.5) if n < 64 else -1.0, None,
                                ALU.mult).then_inc(s_nm, 1)
                if n < 32:
                    take(NB - 1)
                if n == 32:
                    selected(NB - 1)
                if n % 64 >= 2:
                    scaled(n - 2)
            scaled(126)
            scaled(127)
            for k in range(KC):
                low(chunk(YA, k) if k < 4 else chunk(YB, k - 4), k, Z_PARTS)
            for m in range(8):
                w = BR0 + m
                dve.wait_ge(s_mm, w + 1)
                dve.wait_ge(s_g[m % 4], 16 * (m // 4 + 1))
                dst = chunk(Y, 2 * (m // 2), 2)
                psum = bank(w_bank(w), 4)
                if m % 2 == 0:
                    V.tensor_mul(dst, psum, GB[m % 4][:, :]).then_inc(s_evv, 1)
                else:
                    link(V.tensor_mul(MT[:, :], psum, GB[m % 4][:, :]))
                    dve.wait_ge(s_evv, reads(w - 1)[1])
                    V.tensor_add(dst, dst, MT[:, :]).then_inc(s_evv, 1)
            for k in range(KC):
                low(chunk(Y, k), k, Z_PARTS + KC)
            dve.wait_ge(s_xr, 32)
            for i in range(8):
                w = OUT0 + i
                dve.wait_ge(s_mm, w + 1)
                V.tensor_add(chunk(X, i), chunk(X, i), bank(w_bank(w), 2)).then_inc(s_evv, 1)
                if i:
                    add_square(5 * KC + i - 1)
            add_square(6 * KC - 1)
            recip(11)
            norm_split(11, 2, lambda k: vcol("mlp_norm_g_2", k), None, M2.f32 - KC, M2.parts - KC)
            mlp_dve(M2, X, False, 6 * KC)
            recip(12)
            dve.wait_ge(s_bc, 13)
            for k in range(KC):
                V.scalar_tensor_tensor(chunk(X, k), chunk(X, k), vcol("final_norm_g_2", k), bank(2, 2), ALU.mult,
                                       ALU.mult).then_inc(s_fin, 1)


_MATRICES = ["w_ada", "w_in", "w_out", "w_fc1", "w_fc2", "w_in_2", "w_uq_2", "w_ukv_2", "w_branch_a_2", "w_branch_b_2",
             "w_out_2", "w_ff1_2", "w_ff2_2"]


def kernel(**inputs):
    import numpy as _np
    import concourse.bacc as _bacc
    from concourse import mybir as _mybir
    from concourse.bass_utils import run_bass_kernel_spmd as _run

    given = {name: _np.ascontiguousarray(a) for name, a in inputs.items()}
    arrays = {"x": given["x"].reshape(S, D), "positions": given["positions"].reshape(1, S)}
    for name in _MATRICES:
        arrays[name] = given[name].reshape(given[name].shape[-2:])
    arrays["positions_2"] = given["positions_2"].reshape(1, S)
    arrays["rel_bias_2"] = given["rel_bias_2"]
    arrays["vec"] = _np.concatenate([given[name].reshape(-1, P) for name, _ in VEC_A + VEC_B])
    arrays["const"] = CONST

    nc = _bacc.Bacc("TRN2", target_bir_lowering=False, num_devices=1)
    args = {n: nc.dram_tensor(n, a.shape, _mybir.dt.from_np(a.dtype), kind="ExternalInput").ap()
            for n, a in arrays.items()}
    args["out"] = nc.dram_tensor("out", (S, D), _mybir.dt.float32, kind="ExternalOutput").ap()
    build(nc, **args)
    result = _run(nc, [arrays], core_ids=[0])
    return result.results[0]["out"].reshape(1, S, D)
```

```python
from contextlib import ExitStack

import numpy as np

import concourse.bass as bass
from concourse import mybir

F32 = mybir.dt.float32
F32R = mybir.dt.float32r
BF16 = mybir.dt.bfloat16
I32 = mybir.dt.int32
ALU = mybir.AluOpType
ACT = mybir.ActivationFunctionType
AX = mybir.AxisListType.X

P = 128
S = 1024
D = 1024
KC = D // P
NB = S // P
HALF = 512
DFF = 4 * D
EPS = 1e-6

RET_HEADS, RET_DIM, CHUNK = 4, 128, 64
CONV = 4

A_HEADS, A_DIM = 8, 64
IDX_HEADS, TOPK = 4, 256
B_HEADS, B_NOPE, B_ROPE, B_QK, B_V = 8, 64, 32, 96, 64
BUCKETS = 32
QT = P // A_HEADS
STEPQ = P // BUCKETS
NSTEP = QT // STEPQ

NEG = -1e30
HIDDEN = -3.0e38

AQ, AK, AV, IQ, IK, IW, CQ, CKV, KR, GT = 0, 512, 576, 640, 896, 960, 964, 1220, 1348, 1380

VEC_A = [("c", 8), ("b_ada", 48), ("g_pre_mix", 8), ("g_post_mix", 8), ("g_pre_mlp", 8), ("g_post_mlp", 8),
         ("conv_w", 12)]
VEC_B = [("attn_norm_g_2", 8), ("b_gate_2", 16), ("q_latent_norm_g_2", 2), ("kv_latent_norm_g_2", 1),
         ("mlp_norm_g_2", 8), ("final_norm_g_2", 8)]


def vec_columns():
    at, n = {}, 0
    for name, k in VEC_A + VEC_B:
        at[name] = n
        n += k
    return at


VCOL = vec_columns()
NVA = sum(k for _, k in VEC_A)
NVB = sum(k for _, k in VEC_B)


def bucket_steps():
    n = np.arange(1, 4096)
    f = np.float32
    log_b = 16 + (np.log(n.astype(f) / f(16)) / f(np.log(8.0)) * f(16)).astype(np.int32)
    b = np.where(n < 16, n, np.minimum(log_b, BUCKETS - 1))
    return [-1e9] + [float(n[np.argmax(b >= k)]) for k in range(1, BUCKETS)]


def constants():
    parts = {}
    i = np.arange(P)
    parts["ident"] = np.eye(P)
    parts["ones"] = np.ones((P, 1))
    parts["eps"] = np.full((P, 1), EPS)
    half = RET_DIM // 2
    inv = np.float32(10000.0) ** (-(np.arange(half, dtype=np.float32)) / np.float32(half))
    parts["inv1"] = np.tile(inv, 2)[:, None]
    inv2 = np.float32(10000.0) ** (-np.arange(0, B_ROPE, 2, dtype=np.float32) / np.float32(B_ROPE))
    parts["inv2"] = np.tile(inv2, 8)[:, None]
    parts["sgn1"] = np.where(i < half, 1.0, -1.0)[:, None]
    parts["sgn2"] = np.where(i % B_ROPE < 16, -1.0, 1.0)[:, None]
    parts["steps"] = np.tile(np.array(bucket_steps()), STEPQ)[:, None]
    gam = 1.0 - 2.0 ** (-5.0 - np.arange(RET_HEADS))
    j = i[:, None]
    q = i[None, :]
    allowed = (j // CHUNK) <= (q // CHUNK)
    parts["decay"] = np.concatenate([np.where(allowed, g ** np.abs(j - q), 0.0) for g in gam], axis=1)
    parts["qdec"] = np.concatenate([np.tile(g ** (q + 1.0), (P, 1)) for g in gam], axis=1)
    parts["kdec"] = np.stack([g ** (P - 1.0 - i) for g in gam], axis=1)
    sel = np.zeros((P, NB, A_HEADS, QT))
    for r in range(NB):
        for t in range(QT):
            sel[r * QT + t, r, :, t] = 1.0
    parts["sel"] = sel.reshape(P, NB * P)
    rep = np.zeros((P, P))
    for t in range(STEPQ):
        for b in range(BUCKETS):
            rep[b, t * BUCKETS + b] = 1.0
            if b:
                rep[b - 1, t * BUCKETS + b] = -1.0
    parts["rep"] = rep
    reach = np.zeros((P, NSTEP, A_HEADS, QT))
    for g in range(NSTEP):
        for t in range(STEPQ):
            reach[t * BUCKETS:(t + 1) * BUCKETS, g, :, g * STEPQ + t] = 1.0
    parts["reach"] = reach.reshape(P, NSTEP * P)
    parts["tri"] = np.where(i[None, :] > i[:, None], NEG, 0.0)
    at, n = {}, 0
    for name, a in parts.items():
        at[name] = (n, a.shape[1])
        n += a.shape[1]
    return at, np.concatenate([np.asarray(a, np.float32) for a in parts.values()], axis=1).astype(np.float32)


CONST_AT, CONST = constants()
MAGIC = 1.5 * 2.0 ** 23
PI = float(np.nextafter(np.float32(np.pi), np.float32(0)))
TWO_PI = [6.28125, float(np.float32(0.0019350051879882812)), 2 * np.pi - 6.28125 - float(np.float32(0.0019350051879882812))]
GAMMA_BLOCK = [float((1.0 - 2.0 ** (-5.0 - h)) ** P) for h in range(RET_HEADS)]


def build(nc, x, positions, w_ada, w_in, w_out, w_fc1, w_fc2, positions_2, w_in_2, w_uq_2, w_ukv_2,
          w_branch_a_2, w_branch_b_2, w_out_2, w_ff1_2, w_ff2_2, rel_bias_2, vec, const, out):
    ctx = ExitStack()
    with ctx:
        def sem(name):
            return ctx.enter_context(nc.semaphore(name))

        arena_words = 53100
        arena = ctx.enter_context(nc.sbuf_tensor("arena", [P, arena_words], F32))
        base = (nc.sbuf_base - arena_words * 4 + 31) // 32 * 32
        taken = [0]

        def place(name, words, dt=F32, at=None):
            n = words * 2 if dt == BF16 else words
            start = taken[0] if at is None else at
            t = nc.alloc_sbuf_tensor_at(name, [P, n], dt, offset=base + 4 * start)
            if at is None:
                taken[0] += words
            return t

        X0 = taken[0]
        X = place("X", KC * S)
        H0 = taken[0]
        H = place("H", KC * S, F32R)
        L0 = taken[0]
        L = place("L", KC * S, F32R)
        Y0 = taken[0]
        Y = place("Y", KC * S)
        RAW = [place(f"RAW{j}", 1024) for j in range(2)]
        WHI = [place(f"WHI{j}", 1024, F32R) for j in range(2)]
        WLO = [place(f"WLO{j}", 1024, F32R) for j in range(2)]
        IDN = place("IDN", P)
        SC = place("SC", 16)
        IDB = place("IDB", P // 2, BF16)
        TRB = place("TRB", P // 2, BF16)
        VEC = place("VEC", 144)
        MOD = place("MOD", 48)
        MODA = place("MODA", 40)
        SS = place("SS", 8)
        RS = place("RS", 8)
        SILC = place("SILC", 8)
        ZERO = place("ZERO", 8)
        K0 = taken[0]
        WKW = arena_words - K0 - 16
        WK = place("WK", WKW)
        assert WKW >= 13312, WKW

        def region(name, start, words, dt=F32):
            return place(name, words, dt, at=start)

        def chunk(t, k, n=1, rows=slice(0, P)):
            return t[rows, k * S:(k + n) * S]

        XT = region("XT", Y0, 8192)
        ADA = [region(f"ADA{j}", K0 + 1024 * j, S) for j in range(4)]
        ADA_H = region("ADA_H", H0, KC * S)
        ADA_L = region("ADA_L", L0, 4 * S)
        MSUM = [region(f"MSUM{j}", a, S) for j, a in enumerate([L0 + 4096, L0 + 5120, Y0 + 4096, Y0 + 5120])]
        STG = region("STG", K0 + 4096, 3 * P)
        CX = region("CX", K0 + 4096, S)
        CU = region("CU", K0 + 5120, S + 2)
        CT = region("CT", K0 + 6152, S)
        SQ = [region("SQ0", K0 + 12304, S), region("SQ1", K0 + 7176, S)]
        ROT_C = region("ROT_C", K0 + 8200, S)
        ROT_S = region("ROT_S", K0 + 9224, S)
        DEC = region("DEC", K0 + 10248, 1028)
        ACC = region("ACC", K0 + 11280, S)
        R_QR, R_KR, R_VT, R_VTOK, R_G, R_KTOK, R_QD, R_SD = [region(n, X0 + 1024 * i, S) for i, n in enumerate(
            ["R_QR", "R_KR", "R_VT", "R_VTOK", "R_G", "R_KTOK", "R_QD", "R_SD"])]
        R_T, R_T2, R_ST, R_SQ, R_OG = [region(n, K0 + 1024 * i, S) for i, n in enumerate(
            ["R_T", "R_T2", "R_ST", "R_SQ", "R_OG"])]
        FH = region("FH", K0, 4 * S, F32R)
        FL = region("FL", K0 + 4096, 4 * S, F32R)
        RL = [region(f"RL{j}", K0 + 8192 + 1024 * j, S) for j in range(2)]
        FT = region("FT", K0 + 10240, S)

        AQP = region("AQP", X0, 4 * S)
        CQB = region("CQB", X0 + 4096, 2 * S)
        CKVB = region("CKVB", X0 + 6144, S)
        AVKR = region("AVKR", X0 + 7168, S)
        SCORE_AT, n = {}, 0
        for b in range(2, NB):
            SCORE_AT[b] = n
            n += P * (b + 1)
        SCO = region("SCO", Y0, n)
        MASK_AT = {b: P * b * (b + 1) // 2 for b in range(NB)}
        MB = region("MB", Y0 + n, P * 36 // 2, BF16)
        AKB = region("AKB", Y0 + 6528, S)
        KEY, FLIP, CAND, NEXT = [region(n, Y0 + 7632 + 8 * i, 8, I32) for i, n in enumerate(["KEY", "FLIP", "CAND", "NEXT"])]
        REACH = region("REACH", Y0 + 7664, 8)
        ROOM = region("ROOM", Y0 + 7672, 8)
        IWTOK = region("IWTOK", Y0 + 7560, 32)
        NMX = region("NMX", Y0 + 7600, 8)
        RSUM = region("RSUM", Y0 + 7608, 8)
        RINV = region("RINV", Y0 + 7616, 8)
        DLT = region("DLT", Y0 + 7624, 8)
        IQB = region("IQB", K0, 2 * S)
        IKB = region("IKB", K0 + 2048, S)
        RT = [region(f"RT{j}", K0 + 3072 + 1024 * j, S) for j in range(2)]
        IWT = region("IWT", K0 + 5120, S)
        GST = [region(f"GST{j}", K0 + 6144 + 1024 * j, S) for j in range(2)]
        T2C = region("T2C", K0 + 8192, S)
        T2S = region("T2S", K0 + 9216, S)
        WUQ = region("WUQ", K0 + 10240, 2 * S)
        WUKV = region("WUKV", K0 + 12288, S)
        QM = region("QM", H0, 8 * S)
        KM = region("KM", L0, 8 * S)
        VM = region("VM", K0, 4 * S)
        PB = [region(f"PB{j}", K0 + 4096 + 1024 * j, S) for j in range(2)]
        PTS = [region(f"PTS{j}", K0 + 6144 + 1024 * j, S) for j in range(2)]
        OB = region("OB", K0 + 12288, S)
        YB = region("YB", X0 + 4096, 4 * S)
        VA = region("VA", Y0, NB * A_DIM)
        AQ64 = region("AQ64", H0, 8 * S)
        POSB = region("POSB", L0, S)
        STEP = [region("STEP0", L0 + 1024, 4 * S, F32R), region("STEP1", X0, 4 * S, F32R)]
        DHI = region("DHI", L0 + 5120, NSTEP * P, F32R)
        DLO = region("DLO", L0 + 5632, NSTEP * P, F32R)
        SELB = region("SELB", L0 + 6144, 512, BF16)
        THR = region("THR", L0 + 6656, 256)
        DF = region("DF", L0 + 6912, NSTEP * P)
        TAB = region("TAB", L0 + 7680, 8)
        YA = region("YA", K0 + 8192, 4 * S)
        CST = region("CST", K0 + 8192, 1664)
        GB = [region(f"GB{j}", K0 + 2048 * j, 2 * S) for j in range(4)]
        MT = region("MT", K0 + 8192, 2 * S)
        OT = [region(f"OT{j}", K0 + 1024 * j, S) for j in range(2)]

        PS = ctx.enter_context(nc.psum_tensor("PS", [P, 8 * HALF], F32))

        def bank(b, n=1, rows=slice(0, P)):
            return PS[rows, b * HALF:(b + n) * HALF]

        xs = nc.dram_tensor("x_scratch", [P, KC * S], F32).ap()
        gs = nc.dram_tensor("gate_scratch", [16, P, S], F32).ap()

        s_const = sem("const_in")
        s_x = [sem(f"x_in{j}") for j in range(2)]
        s_dec = sem("decays_in")
        s_rot = sem("rotation_tables")
        s_raw = [sem(f"raw_in{j}") for j in range(2)]
        s_ada_in = [sem(f"ada_in{j}") for j in range(4)]
        s_ada_first = [sem(f"ada_first_in{j}") for j in range(4)]
        s_msum = sem("modulation_weights_added")
        s_ada = sem("modulation_group_summed")
        s_whi = sem("weight_high_part")
        s_zero = sem("zero_ready")
        s_w = sem("weight_split")
        s_mm = sem("product_done")
        s_eva = sem("psum_read_by_act")
        s_evv = sem("psum_read_by_dve")
        s_vt = sem("vectors_transposed")
        s_vec = sem("vectors_ready")
        s_silc = sem("silu_of_c")
        s_xt = sem("x_transposed")
        s_xc = sem("x_copied")
        s_sq = sem("squares")
        s_acc = [sem("squares_added_by_dve"), sem("squares_added_by_pool")]
        s_ss = sem("row_sums_of_squares")
        s_std = sem("root_of_mean_square")
        s_rs = sem("reciprocal_root")
        s_bc = sem("reciprocal_root_spread")
        s_xn = sem("residual_added")
        s_h32 = sem("normed_scaled")
        s_hi = sem("activation_high_part")
        s_lo = sem("activation_low_part")
        s_nlo = sem("normed_low_part")
        s_dve = sem("dve_own")
        s_act = sem("act_own")
        s_xs = sem("x_stored")
        s_xr = sem("x_reloaded")
        s_mod = sem("modulations_ready")
        s_red = sem("angles_reduced")
        s_sin = sem("sines")
        s_rt = sem("rotated_terms")
        s_r_q, s_r_k, s_r_qd = sem("ret_q"), sem("ret_k"), sem("ret_q_decayed")
        s_r_vT, s_r_kT = sem("ret_v_transposed"), sem("ret_k_transposed")
        s_r_vtok, s_r_ktok = sem("ret_v_tokens"), sem("ret_k_tokens")
        s_r_sc, s_r_sd = sem("ret_scores"), sem("ret_scores_decayed")
        s_r_kv, s_r_st = sem("ret_block_sums"), sem("ret_states")
        s_r_o, s_r_sq, s_r_og, s_ret_y = sem("ret_out"), sem("ret_squares"), sem("ret_gated"), sem("ret_done")
        s_pos2 = sem("positions_2_in")
        s_red2, s_sin2 = sem("angles_2_reduced"), sem("sines_2")
        s_iwt, s_iw = sem("index_weights_transposed"), sem("index_weights_ready")
        s_ixp, s_rel, s_idx = sem("index_product"), sem("index_relu"), sem("index_added")
        s_diag, s_mb = sem("scores_masked"), sem("selection_mask")
        s_gs = [sem(f"gate_stored{j}") for j in range(2)]
        s_wuq = sem("up_weights_in")
        s_lacc, s_lat = sem("latent_squares"), sem("latent_normed")
        s_up, s_upa, s_upd, s_q = sem("up_product"), sem("up_read_by_act"), sem("up_read_by_dve"), sem("query_rotated")
        s_kt, s_kr, s_krd = sem("key_terms"), sem("key_rotated"), sem("key_spread")
        s_lg, s_nm, s_exp, s_ri = sem("logits"), sem("row_max"), sem("probabilities"), sem("probability_sum_inverse")
        s_pt, s_pte, s_pv, s_oe = sem("probs_transposed"), sem("probs_t_copied"), sem("attended"), sem("attended_scaled")
        s_bt, s_bte = sem("attended_transposed"), sem("attended_t_copied")
        s_c4, s_aq, s_tp, s_tpd = sem("tables_in"), sem("queries_moved"), sem("table_products"), sem("tables_ready")
        s_step = sem("steps")
        s_g = [sem(f"gates_in{j}") for j in range(4)]
        s_fin, s_ft, s_fo, s_out = sem("final_normed"), sem("final_transposed"), sem("final_copied"), [sem(f"out_stored{j}") for j in range(2)]
        block = ctx.enter_context(nc.Block())

        ident = IDN[:, :]
        ones = SC[:, 0:1]
        eps = SC[:, 1:2]
        inv1, inv2 = SC[:, 2:3], SC[:, 3:4]
        sgn1, sgn2 = SC[:, 4:5], SC[:, 5:6]
        steps = SC[:, 6:7]

        def vcol(name, k):
            n = VCOL[name] + k
            return VEC[:, n:n + 1]


        def w_tile(w, r0, kc, c0, nc_):
            return w[r0:r0 + kc * P, c0:c0 + nc_].rearrange("(k p) n -> p k n", p=P)

        def k_n(t, kc, n):
            return t[:, 0:kc * n].rearrange("p (k n) -> p k n", k=kc)

        W_IN = []
        for j in range(CONV):
            W_IN += [("xin", j, j * P), ("c", j, 1024 + j * P), ("b", j, 512 + j * P)]
        for h in range(RET_HEADS):
            W_IN += [(n, h, 1536 + 512 * i + h * P) for i, n in enumerate(["q", "k", "v", "g"])]
        ADA_GROUPS = (1, 0, 2, 3, 4, 5)
        ADA_STEPS = KC * len(ADA_GROUPS)
        ADA_EARLY = 2 * KC
        ADA_PER_TILE = 3
        ADA_SUMMED_AFTER = {4: 2, 7: 3, 9: 4, 12: 5}

        OWNER = {}
        for w, (kind, _, _) in enumerate(W_IN):
            OWNER[w] = "act" if kind in ("xin", "v", "g") else "dve"
        W_OUT0 = len(W_IN)
        for w in range(W_OUT0, W_OUT0 + 8):
            OWNER[w] = "act"
        MLP1 = W_OUT0 + 8

        def reads(w):
            who = OWNER[w]
            return (s_eva if who == "act" else s_evv), sum(OWNER[v] == who for v in range(w + 1))

        def w_bank(w):
            return 4 * (w % 2)


        GROUPS = DFF // 512

        class Counts:

            def __init__(self, w, act, dve, f32, hi, lo, nlo):
                self.w, self.act, self.dve, self.f32, self.hi, self.lo, self.nlo = w, act, dve, f32, hi, lo, nlo

        M1 = Counts(MLP1, sum(v == "act" for v in OWNER.values()), sum(v == "dve" for v in OWNER.values()),
                    2 * KC, 3 * KC, KC, 2 * KC)
        assert M1.w % 2 == 0

        def sq_buffer(n):
            return (RL if n // KC in SQUARES_IN_MLP else SQ)[n % 2]

        SQUARES_IN_MLP = (3, 6)
        SQUARES_BY_POOL = (0, 2, 4)

        def added(n):
            by_pool = n // KC in SQUARES_BY_POOL
            return s_acc[by_pool], sum((v // KC in SQUARES_BY_POOL) == by_pool for v in range(n + 1))

        for g in range(GROUPS):
            for i in range(8):
                OWNER[MLP1 + 8 * g + i] = "act" if i < 4 else "dve"

        Z0 = MLP1 + 8 * GROUPS
        Z_TILES = [("iw", IW), ("iq", IQ), ("iq", IQ + P), ("akik", AK), ("avkr", AV)]
        Z_TILES += [("aq", AQ + P * i) for i in range(4)]
        Z_TILES += [("cq", CQ), ("cq", CQ + P), ("ckv", CKV)]
        Z_GATE = len(Z_TILES)
        LATENT_SUMS = Z_GATE + 13
        Z_TILES += [("gate", GT + P * i) for i in range(16)]
        BR0 = Z0 + len(Z_TILES)
        OUT0 = BR0 + 8
        MLP2 = OUT0 + 8
        for w in range(Z0, BR0):
            OWNER[w] = "act"
        for w in range(BR0, MLP2):
            OWNER[w] = "dve"
        DMAS = {Z0 + 3: 2, Z0 + 4: 4}

        def loads(w):
            return sum(DMAS.get(v, 1) for v in range(w % 2, w + 1, 2))

        M2 = Counts(MLP2, sum(v == "act" for v in OWNER.values()), sum(v == "dve" for v in OWNER.values()),
                    M1.f32 + 4 * GROUPS + 2 * KC, M1.hi + 4 * GROUPS + 4 * KC, M1.lo + 4 * GROUPS + 2 * KC, 4 * KC)
        assert M2.w % 2 == 0
        Z_LO = M1.lo + 4 * GROUPS
        UPS = 17
        ATT = [(b, 2 * c + e) for c in range(4) for b in range(NB) for e in range(2)]
        ATT += [(b, r) for b in range(NB) for r in range(NB)]
        BACK = {16 * j + 15: j for j in range(4)}
        BACK.update({64 + 8 * j + 7: 4 + j for j in range(8)})
        GATED0 = sum(OWNER[v] == "dve" for v in range(BR0))

        @block.sync
        def _(sp):
            sp.dma_start(IDN[:, :], const[:, 0:P]).then_inc(s_const, 16)
            sp.dma_start(SC[:, 0:7], const[:, P:P + 7]).then_inc(s_const, 16)
            sp.dma_start(STG[0:NVA, 0:P], vec[0:NVA, :]).then_inc(s_const, 16)
            sp.dma_start(STG[0:NVB, P:2 * P], vec[NVA:NVA + NVB, :]).then_inc(s_const, 16)
            tri = CONST_AT["tri"][0]
            sp.dma_start(STG[:, 2 * P:3 * P], const[:, tri:tri + P]).then_inc(s_const, 16)
            sp.dma_start(ROT_S[:, :].bitcast(I32), positions.partition_broadcast(P)).then_inc(s_rot, 16)
            for j in range(2):
                sp.dma_start(XT[:, :].rearrange("p (b d) -> p b d", b=NB)[:, :, j * HALF:(j + 1) * HALF],
                             x.rearrange("(b p) d -> p b d", p=P)[:, :, j * HALF:(j + 1) * HALF]).then_inc(s_x[j], 16)
            def load_ada(n):
                sp.wait_ge(s_msum, n - 3)
                k, c = n % KC, D * ADA_GROUPS[n // KC]
                sp.dma_start(ADA[n % 4][:, :], w_ada[k * P:(k + 1) * P, c:c + D]).then_inc(s_ada_in[n % 4], 16)

            def load_w(w, src, kc, n):
                if w >= 2:
                    sp.wait_ge(s_w, w - 1)
                sp.dma_start(k_n(RAW[w % 2], kc, n), src).then_inc(s_raw[w % 2], 16)

            for j in range(4):
                to = [ADA_H[:, 0:4 * S], ADA_H[:, 4 * S:8 * S], ADA_L[:, :], WK[:, 0:4 * S]][j]
                sp.dma_start(to.rearrange("p (k n) -> p k n", k=4),
                             w_tile(w_ada, HALF * (j % 2), 4, D * ADA_GROUPS[j // 2], D)).then_inc(s_ada_first[j], 16)
                if j == 1:
                    load_w(0, w_tile(w_in, 0, KC, W_IN[0][2], P), KC, P)
            load_w(1, w_tile(w_in, 0, KC, W_IN[1][2], P), KC, P)
            sp.dma_start(DEC[:, :], const[:, CONST_AT["decay"][0]:CONST_AT["decay"][0] + 1028]).then_inc(s_dec, 16)
            sp.wait_ge(s_xc, KC)
            sp.dma_start(xs, X[:, :]).then_inc(s_xs, 16)
            n = ADA_EARLY
            for _ in range(4):
                load_ada(n)
                n += 1
            for w in range(2, len(W_IN)):
                load_w(w, w_tile(w_in, 0, KC, W_IN[w][2], P), KC, P)
                for _ in range(ADA_PER_TILE):
                    if w >= 3 and n < ADA_STEPS:
                        load_ada(n)
                        n += 1
            for i in range(8):
                load_w(W_OUT0 + i, w_tile(w_out, 0, KC, i * P, P), KC, P)
            sp.wait_ge(s_xs, 16)
            sp.wait_ge(s_ret_y, RET_HEADS)
            sp.dma_start(X[:, :], xs).then_inc(s_xr, 16)

            def mlp_loads(m, up, down):
                down_v = down.rearrange("(g k p) n -> g p k n", k=4, p=P)

                def group(g):
                    for i in range(8):
                        w = 8 * g + (m.w + i)
                        sp.wait_ge(s_w, w - 1)
                        if i < 4:
                            src = up.rearrange("(k p) n -> p k n", p=P)[:, :, bass.ds(512 * g + i * P, P)]
                            dst = k_n(RAW[i % 2], KC, P)
                        else:
                            src = down_v[bass.ds(g, 1), :, :, 256 * (i - 4):256 * (i - 3)].rearrange("o p k n -> (o p) k n")
                            dst = k_n(RAW[i % 2], 4, 256)
                        sp.dma_start(dst, src).then_inc(s_raw[i % 2], 16)

                with sp.Fori(0, GROUPS) as g:
                    group(g)

            mlp_loads(M1, w_fc1, w_fc2)

            for i, (kind, c0) in enumerate(Z_TILES):
                w = Z0 + i
                sp.wait_ge(s_w, w - 1)
                dst = k_n(RAW[w % 2], KC, P)
                if kind == "akik":
                    pieces = [(0, AK, 64), (64, IK, 64)]
                elif kind == "avkr":
                    pieces = [(0, AV, 64), (64, KR, 32), (96, KR + 16, 16), (112, KR, 16)]
                else:
                    pieces = [(0, c0, P)]
                for to, c, n in pieces:
                    sp.dma_start(dst[:, :, to:to + n], w_tile(w_in_2, 0, KC, c, n)).then_inc(s_raw[w % 2], 16)
                if i == 2:
                    sp.wait_ge(s_xr, 16)
                    sp.wait_ge(s_xn, 2 * KC)
                    sp.dma_start(xs, X[:, :]).then_inc(s_xs, 16)
                    sp.wait_ge(s_nlo, 3 * KC)
                    sp.dma_start(T2S[:, :].bitcast(I32), positions_2.partition_broadcast(P)).then_inc(s_pos2, 16)
                    q = WUQ[:, :].rearrange("p (k h n) -> p k h n", k=2, h=B_HEADS)
                    qd = w_uq_2.rearrange("(k p) (h n) -> p k h n", p=P, n=B_QK)
                    for k in range(2):
                        sp.dma_start(q[:, k, :, 0:B_QK], qd[:, k, :, :]).then_inc(s_wuq, 16)
                        sp.dma_start(q[:, k, :, 96:112], qd[:, k, :, 80:96]).then_inc(s_wuq, 16)
                        sp.dma_start(q[:, k, :, 112:128], qd[:, k, :, 64:80]).then_inc(s_wuq, 16)
                    kv = w_ukv_2.rearrange("p (h n) -> p h n", h=B_HEADS)
                    for e in range(2):
                        sp.dma_start(WUKV[:, e * HALF:(e + 1) * HALF].rearrange("p (h n) -> p h n", h=B_HEADS),
                                     kv[:, :, 64 * e:64 * (e + 1)]).then_inc(s_wuq, 16)

            def load_branch(m):
                w = BR0 + m
                sp.wait_ge(s_w, w - 1)
                src = w_branch_b_2 if m % 2 else w_branch_a_2
                sp.dma_start(k_n(RAW[w % 2], 4, 256), w_tile(src, 0, 4, 256 * (m // 2), 256)).then_inc(s_raw[w % 2], 16)

            load_branch(0)
            load_branch(1)
            sp.wait_ge(s_kr, 1)
            for h in range(1, B_HEADS):
                sp.dma_start(KM[64:96, h * S:(h + 1) * S], KM[64:96, 0:S]).then_inc(s_krd, 16)
            sp.wait_ge(s_lg, 64)
            aq = AQ64[0:64, :].rearrange("p (i e n) -> p i e n", e=2, n=64)
            for e in range(2):
                sp.dma_start(aq[:, :, e, :], AQP[64 * e:64 * e + 64, :].rearrange("p (i n) -> p i n", n=64)).then_inc(s_aq, 16)
            sp.dma_start(POSB[:, :].bitcast(I32), positions_2.partition_broadcast(P)).then_inc(s_c4, 16)
            sp.dma_start(TAB[0:BUCKETS, :], rel_bias_2).then_inc(s_c4, 16)
            c = CONST_AT["sel"][0]
            sp.dma_start(CST[:, :], const[:, c:c + 1664]).then_inc(s_c4, 16)
            sp.wait_ge(s_pv, 128)
            for j in range(2):
                sp.wait_ge(s_gs[j], 128)

            def load_gates(m):
                if m >= 4:
                    sp.wait_ge(s_evv, GATED0 + m - 3)
                t = 8 * (m % 2) + 2 * (m // 2)
                sp.dma_start(GB[m % 4][:, :].rearrange("p (t s) -> p t s", t=2),
                             gs[t:t + 2].rearrange("t p s -> p t s")).then_inc(s_g[m % 4], 16)

            for m in range(8):
                load_gates(m)
                if m >= 2:
                    load_branch(m)
            sp.wait_ge(s_lo, Z_LO + KC)
            sp.wait_ge(s_xs, 32)
            sp.dma_start(X[:, :], xs).then_inc(s_xr, 16)
            for i in range(8):
                w = OUT0 + i
                sp.wait_ge(s_w, w - 1)
                sp.dma_start(k_n(RAW[w % 2], KC, P), w_tile(w_out_2, 0, KC, i * P, P)).then_inc(s_raw[w % 2], 16)
            mlp_loads(M2, w_ff1_2, w_ff2_2)
            for t in range(NB):
                sp.wait_ge(s_fo, t + 1)
                sp.dma_start(out[t * P:(t + 1) * P, :], OT[t % 2][:, :]).then_inc(s_out[t % 2], 16)
            for j in range(2):
                sp.wait_ge(s_out[j], 16 * NB // 2)

        @block.gpsimd
        def _(pool):
            def split(j, w, loads, n=1024, free=True):
                pool.wait_ge(s_raw[j], 16 * loads)
                if free:
                    pool.wait_ge(s_mm, w - 1)
                nc.gpsimd.tensor_add(WHI[j][:, 0:n], RAW[j][:, 0:n], ZERO[:, 0:1].to_broadcast([P, n])).then_inc(s_whi, 1)
                pool.wait_ge(s_whi, w + 1)
                nc.gpsimd.tensor_sub(WLO[j][:, 0:n], RAW[j][:, 0:n], WHI[j][:, 0:n].bitcast(F32)).then_inc(s_w, 1)

            nc.gpsimd.memset(ZERO[:, :], 0.0).then_inc(s_zero, 1)
            pool.wait_ge(s_zero, 1)

            def add_squares(first):
                for k in range(KC):
                    n = first + k
                    pool.wait_ge(s_sq, n + 1)
                    if n:
                        pool.wait_ge(*added(n - 1))
                    buf = sq_buffer(n)[:, :]
                    other = ZERO[:, 0:1].to_broadcast([P, S]) if k == 0 else ACC[:, :]
                    nc.gpsimd.tensor_add(ACC[:, :], buf, other).then_inc(s_acc[1], 1)

            def normed_low(i, first):
                for k in range(KC):
                    pool.wait_ge(s_hi, first + k + 1)
                    nc.gpsimd.tensor_sub(chunk(L, k), SQ[k % 2][:, :], chunk(H, k).bitcast(F32)).then_inc(s_nlo, 1)

            for w in range(W_OUT0 + 8):
                if w == 0:
                    add_squares(0)
                split(w % 2, w, w // 2 + 1, free=w >= 2)
                if w == 1:
                    normed_low(0, 0)

            def mlp_splits(m, before, i_norm):

                def group(g, first):
                    for i in range(8):
                        split(i % 2, 8 * g + (m.w + i), 4 * g + loads(m.w + i))
                        if first and i == 1:
                            before()
                            normed_low(i_norm, m.hi - KC)

                group(0, True)
                with pool.Fori(1, GROUPS) as g:
                    group(g, False)

            mlp_splits(M1, lambda: add_squares(2 * KC), 1)

            for i in range(len(Z_TILES)):
                w = Z0 + i
                split(w % 2, w, loads(w))
                if i == 1:
                    add_squares(4 * KC)
                    normed_low(2, M1.hi + 4 * GROUPS)
                if i == 5:
                    for b in range(2, NB):
                        pool.wait_ge(s_idx, IDX_HEADS * (b - 1))
                        a = SCORE_AT[b] + P * b
                        nc.gpsimd.affine_select(out=SCO[:, a:a + P], in_=SCO[:, a:a + P], compare_op=ALU.is_ge,
                                                fill=HIDDEN, base=0, pattern=[[-1, P]],
                                                channel_multiplier=1).then_inc(s_diag, 1)
            for w in range(BR0, MLP2):
                split(w % 2, w, loads(w))
            mlp_splits(M2, lambda: None, 3)

        @block.tensor
        def _(pe):
            mm = nc.tensor.matmul

            def transpose(dst, src, n=P):
                return nc.tensor.transpose(dst, src, ident[0:n, 0:n])

            def product(w, first_of=None):
                pe.wait_ge(s_w, w + 1)
                if w >= 2:
                    pe.wait_ge(*reads(w - 2))
                hi, lo = k_n(WHI[w % 2], KC, P), k_n(WLO[w % 2], KC, P)
                b = w_bank(w)
                for k in range(KC):
                    if first_of is not None:
                        pe.wait_ge(first_of[0], first_of[1] + k + 1)
                    for n, (wt, a) in enumerate(((hi, H), (hi, L), (lo, H))):
                        for t in range(2):
                            last = mm(bank(b + t), wt[:, k, :], a[:, k * S + t * HALF:k * S + (t + 1) * HALF],
                                      start=(k == 0 and n == 0), stop=(k == KC - 1 and n == 2))
                last.then_inc(s_mm, 1)

            def sums(r, acc, b):
                for t in range(NB):
                    last = mm(bank(b)[:, t:t + 1], acc[:, t * P:(t + 1) * P], ones, start=True, stop=True)
                last.then_inc(s_ss, 1)

            def spread(r, b):
                pe.wait_ge(s_rs, r + 1)
                for t in range(NB):
                    last = mm(bank(b, 2)[:, t * P:(t + 1) * P], RS[:, t:t + 1].to_broadcast([P, P]), ident,
                              start=True, stop=True)
                last.then_inc(s_bc, 1)

            pe.wait_ge(s_const, 80)
            transpose(bank(7)[:, 0:NVA], STG[0:NVA, 0:P], NVA)
            transpose(bank(7)[:, NVA:NVA + NVB], STG[0:NVB, P:2 * P], NVB).then_inc(s_vt, 1)
            for k in range(KC):
                if k % 4 == 0:
                    pe.wait_ge(s_x[k // 4], 16)
                if k >= 2:
                    pe.wait_ge(s_sq, k - 1)
                for t in range(NB):
                    last = transpose(bank(2 * (k % 2), 2)[:, t * P:(t + 1) * P], XT[:, t * D + k * P:t * D + (k + 1) * P])
                last.then_inc(s_xt, 1)
            pe.wait_ge(*added(KC - 1))
            pe.wait_ge(s_vec, 1)
            sums(0, ACC, 7)

            def ada(g):
                pe.wait_ge(s_msum, KC * (g + 1))
                for i in range(8):
                    last = mm(bank(6)[:, 8 * g + i:8 * g + i + 1], MSUM[g if g < 2 else 2 + g % 2][:, i * P:(i + 1) * P],
                              ones, start=True, stop=True)
                last.then_inc(s_ada, 1)

            spread(0, 2)
            ada(0)
            ada(1)

            def ret_a(h):
                pe.wait_ge(*reads(12 + 4 * h + 2))
                if h:
                    pe.wait_ge(s_r_og, h)
                for t in range(NB):
                    last = transpose(bank(2, 2)[:, t * P:(t + 1) * P], R_VT[:, t * P:(t + 1) * P])
                last.then_inc(s_r_vT, 1)
                pe.wait_ge(s_r_k, h + 1)
                if h:
                    pe.wait_ge(s_ret_y, h)
                else:
                    pe.wait_ge(s_mod, 1)
                for t in range(NB):
                    last = transpose(bank(6, 2)[:, t * P:(t + 1) * P], R_KR[:, t * P:(t + 1) * P])
                last.then_inc(s_r_kT, 1)
                pe.wait_ge(s_r_q, h + 1)
                pe.wait_ge(s_r_vtok, h + 1)
                for t in range(NB):
                    last = mm(bank(2, 2)[:, t * P:(t + 1) * P], R_KR[:, t * P:(t + 1) * P],
                              R_QR[:, t * P:(t + 1) * P], start=True, stop=True)
                last.then_inc(s_r_sc, 1)
                pe.wait_ge(s_r_ktok, h + 1)
                for t in range(NB - 1):
                    last = mm(bank(6, 2)[:, t * P:(t + 1) * P], R_KTOK[:, t * P:(t + 1) * P],
                              R_VTOK[:, t * P:(t + 1) * P], start=True, stop=True)
                last.then_inc(s_r_kv, 1)

            def ret_b(h):
                pe.wait_ge(s_r_sd, h + 1)
                pe.wait_ge(s_r_st, h + 1)
                pe.wait_ge(s_r_qd, h + 1)
                for t in range(NB):
                    o = bank(2, 2)[:, t * P:(t + 1) * P]
                    last = mm(o, R_VTOK[:, t * P:(t + 1) * P], R_SD[:, t * P:(t + 1) * P],
                              start=True, stop=(t == 0))
                    if t:
                        last = mm(o, R_ST[:, (t - 1) * P:t * P], R_QD[:, t * P:(t + 1) * P],
                                  start=False, stop=True)
                last.then_inc(s_r_o, 1)

            def ret_c(h):
                pe.wait_ge(s_r_sq, h + 1)
                sums(1 + h, R_SQ, 6)

            for w, (kind, h, _) in enumerate(W_IN):
                product(w, (s_nlo, 0) if w == 0 else None)
                if w in ADA_SUMMED_AFTER:
                    ada(ADA_SUMMED_AFTER[w])
                if kind == "q" and h:
                    ret_b(h - 1)
                if kind == "k" and h:
                    ret_c(h - 1)
                if kind == "v" and h:
                    spread(h, 6)
                if kind == "g":
                    ret_a(h)
            ret_b(RET_HEADS - 1)
            ret_c(RET_HEADS - 1)
            spread(RET_HEADS, 6)
            for i in range(8):
                product(W_OUT0 + i, (s_lo, 0) if i == 0 else None)

            def norm_products(r, squares):
                pe.wait_ge(*added(squares - 1))
                sums(r, ACC, 6)
                spread(r, 2)

            def mlp_products(m):
                pe.wait_ge(s_eva, m.act)
                pe.wait_ge(s_evv, m.dve)

                def group(g, first):
                    for i in range(8):
                        w = 8 * g + (m.w + i)
                        pe.wait_ge(s_w, w + 1)
                        if i < 2:
                            if not first:
                                pe.wait_ge(s_evv, 4 * g + (m.dve + i - 1))
                        elif i < 6:
                            pe.wait_ge(s_eva, 4 * g + (m.act + i - 1))
                        else:
                            pe.wait_ge(s_evv, 4 * g + (m.dve + i - 5))
                        b = 4 * (i % 2)
                        if i < 4:
                            hi, lo = k_n(WHI[i % 2], KC, P), k_n(WLO[i % 2], KC, P)
                            for k in range(KC):
                                if first and i == 0:
                                    pe.wait_ge(s_nlo, m.nlo - KC + k + 1)
                                for n, (wt, a) in enumerate(((hi, H), (hi, L), (lo, H))):
                                    for t in range(2):
                                        last = mm(bank(b + t), wt[:, k, :], a[:, k * S + t * HALF:k * S + (t + 1) * HALF],
                                                  start=(k == 0 and n == 0), stop=(k == KC - 1 and n == 2))
                        else:
                            hi, lo = k_n(WHI[i % 2], 4, 256), k_n(WLO[i % 2], 4, 256)
                            for k in range(4):
                                if i == 4:
                                    pe.wait_ge(s_lo, 4 * g + (m.lo + k + 1))
                                for c in range(2):
                                    for n, (wt, a) in enumerate(((hi, FH), (hi, FL), (lo, FH))):
                                        for t in range(2):
                                            last = mm(bank(b + 2 * c + t), wt[:, k, c * P:(c + 1) * P],
                                                      a[:, k * S + t * HALF:k * S + (t + 1) * HALF],
                                                      start=(k == 0 and n == 0), stop=(k == 3 and n == 2))
                        last.then_inc(s_mm, 1)

                group(0, True)
                with pe.Fori(1, GROUPS) as g:
                    group(g, False)

            norm_products(5, 2 * KC)
            norm_products(6, 3 * KC)
            mlp_products(M1)
            norm_products(7, 4 * KC)
            norm_products(8, 5 * KC)

            def index_scores():
                pe.wait_ge(*reads(Z0 + 3))
                for t in range(NB):
                    last = transpose(bank(7)[:, 4 * t:4 * t + 4], IWT[0:4, t * P:(t + 1) * P], 4)
                last.then_inc(s_iwt, 1)
                m = 0
                for b in range(2, NB):
                    w = P * (b + 1)
                    for h in range(IDX_HEADS):
                        if m >= 2:
                            pe.wait_ge(s_rel, m - 1)
                        if m == 1:
                            pe.wait_ge(s_iw, 1)
                        rows = slice(64 * (h % 2), 64 * (h % 2) + 64)
                        q0 = (h // 2) * S + b * P
                        for c in range(0, w, HALF):
                            n = min(HALF, w - c)
                            last = mm(bank(2 + 4 * (m % 2), 2)[:, c:c + n], IQB[rows, q0:q0 + P], IKB[rows, c:c + n],
                                      start=True, stop=True)
                        last.then_inc(s_ixp, 1)
                        m += 1

            for i in range(len(Z_TILES)):
                product(Z0 + i, (s_nlo, 2 * KC) if i == 0 else None)
                if i == 3:
                    index_scores()
                if i == LATENT_SUMS:
                    for n in range(2):
                        pe.wait_ge(s_lacc, n + 1)
                        for t in range(NB):
                            last = mm(bank(6 + n)[:, t:t + 1], (RT[0] if n == 0 else IWT)[:, t * P:(t + 1) * P], ones,
                                      start=True, stop=True)
                        last.then_inc(s_ss, 1)
                if i == LATENT_SUMS + 1:
                    spread(9, 2)
                    spread(10, 6)

            pe.wait_ge(s_wuq, 8 * 16)
            pe.wait_ge(s_eva, M2.act)
            for u in range(UPS):
                if u == 0:
                    pe.wait_ge(s_lat, 3)
                if u >= 4:
                    pe.wait_ge(s_upa, u - 3)
                    if u - 4 >= 8:
                        pe.wait_ge(s_upd, u - 11)
                b = bank(2 * (u % 4), 2)
                if u < 4:
                    wt = WUKV[:, P * u:P * (u + 1)]
                    for t in range(2):
                        last = mm(b[:, t * HALF:(t + 1) * HALF], wt, CKVB[:, t * HALF:(t + 1) * HALF], start=True, stop=True)
                elif u < 8:
                    wt = WUKV[:, HALF:]
                    for t in range(2):
                        tok = (2 * (u - 4) + t) * P
                        last = mm(b[:, t * HALF:(t + 1) * HALF], CKVB[:, tok:tok + P], wt, start=True, stop=True)
                elif u < 16:
                    for k in range(2):
                        wt = WUQ[:, k * S + (u - 8) * P:k * S + (u - 7) * P]
                        for t in range(2):
                            last = mm(b[:, t * HALF:(t + 1) * HALF], wt, CQB[:, k * S + t * HALF:k * S + (t + 1) * HALF],
                                      start=(k == 0), stop=(k == 1))
                else:
                    for t in range(NB):
                        last = transpose(b[:, t * A_DIM:(t + 1) * A_DIM], AVKR[0:64, t * P:(t + 1) * P], 64)
                last.then_inc(s_up, 1)

            def logits(n):
                b = ATT[n][0]
                w = P * (b + 1)
                dst = bank(2 * (n % 2), 2)
                if n >= 2:
                    pe.wait_ge(s_exp, n - 1)
                if n < 64:
                    h = ATT[n][1]
                    for c in range(0, w, HALF):
                        cw = min(HALF, w - c)
                        end = c + cw == w
                        last = mm(dst[:, c:c + cw], QM[0:B_QK, h * S + b * P:h * S + (b + 1) * P],
                                  KM[0:B_QK, h * S + c:h * S + c + cw], start=True, stop=not end)
                        if end:
                            last = mm(dst[:, w - P:w], IDB[:, :], TRB[:, :], start=False, stop=True)
                else:
                    i = n - 64
                    pe.wait_ge(s_step, NSTEP * (i + 1))
                    q = AQ64[0:64, i * P:(i + 1) * P]
                    for c in range(0, w, HALF):
                        cw = min(HALF, w - c)
                        mm(dst[:, c:c + cw], q, AKB[0:64, c:c + cw], start=True, stop=False)
                        mm(dst[:, c:c + cw], SELB[:, (i % NB) * P:(i % NB + 1) * P],
                           MB[:, MASK_AT[b] + c:MASK_AT[b] + c + cw], start=False, stop=False)
                        for g in range(NSTEP):
                            for part in (DHI, DLO):
                                last = mm(dst[:, c:c + cw], part[:, g * P:(g + 1) * P],
                                          STEP[i % 2][:, g * S + c:g * S + c + cw], start=False,
                                          stop=(g == NSTEP - 1 and part is DLO))
                last.then_inc(s_lg, 1)

            def probs_t(n):
                pe.wait_ge(s_exp, n + 1)
                if n:
                    pe.wait_ge(s_pte, n)
                backs = sum(m <= n - 3 for m in BACK)
                if backs:
                    pe.wait_ge(s_bte, backs)
                for t in range(ATT[n][0] + 1):
                    last = transpose(bank(4, 2)[:, t * P:(t + 1) * P], PB[n % 2][:, t * P:(t + 1) * P])
                last.then_inc(s_pt, 1)

            def attend(n):
                b = ATT[n][0]
                pe.wait_ge(s_pte, n + 1)
                if n >= 2:
                    pe.wait_ge(s_oe, n - 1)
                for t in range(b + 1):
                    if n < 64:
                        v = VM[:, t * HALF + ATT[n][1] * B_V:t * HALF + (ATT[n][1] + 1) * B_V]
                    else:
                        v = VA[:, t * A_DIM:(t + 1) * A_DIM]
                    last = mm(bank(6 + n % 2)[:, 0:64], PTS[n % 2][:, t * P:(t + 1) * P], v,
                              start=(t == 0), stop=(t == b))
                last.then_inc(s_pv, 1)

            def back(j):
                last_tile = 16 * j + 15 if j < 4 else 64 + 8 * (j - 4) + 7
                pe.wait_ge(s_oe, last_tile + 1)
                pe.wait_ge(s_pte, min(last_tile + 3, 64 if j < 4 else 128))
                for t in range(NB):
                    if j < 4:
                        last = transpose(bank(4, 2)[:, t * P:(t + 1) * P], OB[:, t * P:(t + 1) * P])
                    else:
                        last = transpose(bank(4, 2)[0:64, t * P:(t + 1) * P], OB[:, t * 64:(t + 1) * 64])
                last.then_inc(s_bt, 1)

            pe.wait_ge(s_upa, UPS)
            pe.wait_ge(s_upd, 8)
            pe.wait_ge(s_q, 8)
            pe.wait_ge(s_krd, 7 * 16)
            for half in range(2):
                n0, n1 = 64 * half, 64 * half + 64
                if half:
                    pe.wait_ge(s_c4, 48)
                    pe.wait_ge(s_oe, 64)
                    mm(bank(7)[:, 0:8], CST[0:BUCKETS, 1024:1152], TAB[0:BUCKETS, :], start=True, stop=True).then_inc(s_tp, 1)
                    pe.wait_ge(s_tpd, 1)
                    pe.wait_ge(s_aq, 32)
                logits(n0)
                for n in range(n0, n1 + 3):
                    if n + 1 < n1:
                        logits(n + 1)
                    if n0 <= n - 2 < n1:
                        attend(n - 2)
                    if n - 3 >= n0 and n - 3 in BACK:
                        back(BACK[n - 3])
                    if n < n1:
                        probs_t(n)

            def wide(w, a0, first_of):
                pe.wait_ge(s_w, w + 1)
                pe.wait_ge(*reads(w - 2))
                hi, lo = k_n(WHI[w % 2], 4, 256), k_n(WLO[w % 2], 4, 256)
                for k in range(4):
                    if first_of is not None:
                        pe.wait_ge(s_lo, first_of + k + 1)
                    for c in range(2):
                        for n, (wt, a) in enumerate(((hi, H), (hi, L), (lo, H))):
                            for t in range(2):
                                last = mm(bank(w_bank(w) + 2 * c + t), wt[:, k, c * P:(c + 1) * P],
                                          a[:, (a0 + k) * S + t * HALF:(a0 + k) * S + (t + 1) * HALF],
                                          start=(k == 0 and n == 0), stop=(k == 3 and n == 2))
                last.then_inc(s_mm, 1)

            pe.wait_ge(s_bte, 12)
            pe.wait_ge(s_oe, 128)
            for m in range(8):
                wide(BR0 + m, 4 * (m % 2), Z_LO + 4 * (m % 2) if m < 2 else None)
            for i in range(8):
                product(OUT0 + i, (s_lo, Z_LO + KC) if i == 0 else None)
            norm_products(11, 6 * KC)
            mlp_products(M2)
            norm_products(12, 7 * KC)
            for t in range(NB):
                if t == 0:
                    pe.wait_ge(s_fin, KC)
                if t >= 2:
                    pe.wait_ge(s_fo, t - 1)
                for k in range(KC):
                    last = transpose(bank(4 * (t % 2), 2)[:, k * P:(k + 1) * P], X[:, k * S + t * P:k * S + (t + 1) * P])
                last.then_inc(s_ft, 1)

        @block.scalar
        def _(act):
            A = nc.scalar.activation

            def copy_out(w, dst, fn=ACT.Copy, **kw):
                act.wait_ge(s_mm, w + 1)
                return A(dst, bank(w_bank(w), 2), fn, **kw).then_inc(s_eva, 1)

            def root(r, b, n=D):
                act.wait_ge(s_ss, r + 1)
                if r:
                    act.wait_ge(s_rs, r)
                A(SS[:, :], bank(b)[:, 0:NB], ACT.Sqrt, bias=eps, scale=1.0 / n).then_inc(s_std, 1)

            act.wait_ge(s_vt, 1)
            A(VEC[:, 0:NVA + NVB], bank(7)[:, 0:NVA + NVB], ACT.Copy).then_inc(s_vec, 1)
            act.wait_ge(s_vec, 1)
            A(SILC[:, :], VEC[:, 0:8], ACT.Silu).then_inc(s_silc, 1)
            for k in range(KC):
                act.wait_ge(s_xt, k + 1)
                A(chunk(X, k), bank(2 * (k % 2), 2), ACT.Copy).then_inc(s_xc, 1)
                if k >= 2:
                    act.wait_ge(*added(k - 2))
                A(SQ[k % 2][:, :], bank(2 * (k % 2), 2), ACT.Square).then_inc(s_sq, 1)
            act.wait_ge(s_red, 1)
            A(ROT_S[:, :], CT[:, :], ACT.Sin, scale=sgn1).then_inc(s_sin, 1)
            A(ROT_C[:, :], CT[:, :], ACT.Sin, scale=0.5).then_inc(s_sin, 1)
            root(0, 7)

            def high(first):
                for k in range(KC):
                    act.wait_ge(s_h32, first + k + 1)
                    A(chunk(H, k), SQ[k % 2][:, :], ACT.Copy).then_inc(s_hi, 1)

            high(0)
            for w, (kind, h, _) in enumerate(W_IN):
                if kind == "xin":
                    if h:
                        act.wait_ge(*reads(w - 2))
                    copy_out(w, CX[:, :])
                elif kind == "v":
                    copy_out(w, R_VT[:, :])
                elif kind == "g":
                    if h:
                        act.wait_ge(s_r_og, h)
                    copy_out(w, R_G[:, :], ACT.Silu)
                    act.wait_ge(s_r_vT, h + 1)
                    A(R_VTOK[:, :], bank(2, 2), ACT.Copy).then_inc(s_r_vtok, 1)
                    act.wait_ge(s_r_kT, h + 1)
                    act.wait_ge(s_dec, 16)
                    A(R_KTOK[:, :], bank(6, 2), ACT.Copy, scale=DEC[:, 1024 + h:1025 + h]).then_inc(s_r_ktok, 1)
                    if h == RET_HEADS - 1:
                        act.wait_ge(s_mm, W_OUT0)
                        for k in range(4):
                            A(chunk(H, k), chunk(Y, k), ACT.Copy).then_inc(s_hi, 1)
                    act.wait_ge(s_r_o, h + 1)
                    A(R_SQ[:, :], bank(2, 2), ACT.Square).then_inc(s_r_sq, 1)
                    act.wait_ge(s_ss, 1 + h + 1)
                    A(SS[:, :], bank(6)[:, 0:NB], ACT.Sqrt, bias=eps, scale=1.0 / RET_DIM).then_inc(s_std, 1)
            for k in range(4, KC):
                if k == KC - 1:
                    act.wait_ge(s_ret_y, RET_HEADS)
                A(chunk(H, k), chunk(Y, k), ACT.Copy).then_inc(s_hi, 1)
            def square(n, src):
                act.wait_ge(*added(n - 2))
                A(sq_buffer(n)[:, :], src, ACT.Square).then_inc(s_sq, 1)

            for i in range(8):
                w = W_OUT0 + i
                if i == 0:
                    act.wait_ge(s_lo, KC)
                act.wait_ge(s_mm, w + 1)
                square(KC + i, bank(w_bank(w), 2))
                copy_out(w, chunk(Y, i))

            def residual_squares(n, first_x):
                for k in range(KC):
                    act.wait_ge(s_xn, first_x + k + 1)
                    square(n + k, chunk(X, k))

            root(5, 6)
            residual_squares(2 * KC, 0)
            root(6, 6)
            high(KC)

            def mlp_act(m):

                def group(g, first):
                    for i in range(4):
                        act.wait_ge(s_mm, 8 * g + (m.w + i + 1))
                        if not (first and i < 2):
                            act.wait_ge(s_h32, 4 * g + (m.f32 + i - 1))
                        A(RL[i % 2][:, :], bank(4 * (i % 2), 2), ACT.Relu).then_inc(s_eva, 1)
                        act.wait_ge(s_eva, 4 * g + (m.act + i + 1))
                        A(chunk(FH, i), RL[i % 2][:, :], ACT.Square).then_inc(s_hi, 1)

                group(0, True)
                with act.Fori(1, GROUPS) as g:
                    group(g, False)

            mlp_act(M1)
            for k in range(KC):
                act.wait_ge(s_evv, M1.dve + 4 * (GROUPS - 1) + k // 2 + 1)
                square(3 * KC + k, chunk(Y, k))
            root(7, 6)
            residual_squares(4 * KC, KC)
            root(8, 6)
            high(2 * KC + 4 * GROUPS)

            def read_tile(w, pieces):
                act.wait_ge(s_mm, w + 1)
                for n, (dst, rows, kw) in enumerate(pieces):
                    src = bank(w_bank(w), 2, rows)
                    if "split" in kw:
                        src = src.rearrange("p (i q) -> p i q", q=kw.pop("split"))
                    ins = A(dst, src, kw.pop("fn", ACT.Copy), **kw)
                    ins.then_inc(s_eva if n == len(pieces) - 1 else s_act, 1)

            every = slice(0, P)
            top, low_rows = slice(0, 64), slice(64, P)
            act.wait_ge(s_xs, 32)
            for i, (kind, c0) in enumerate(Z_TILES):
                w = Z0 + i
                if kind == "iw":
                    read_tile(w, [(IWT[0:4, :], slice(0, 4), {})])
                elif kind == "iq":
                    read_tile(w, [(chunk(IQB, (c0 - IQ) // P), every, {})])
                elif kind == "akik":
                    read_tile(w, [(AKB[0:64, :], top, {}), (IKB[64:P, :], low_rows, {}), (IKB[0:64, :], low_rows, {})])
                    m = 0
                    for b in range(2, NB):
                        n = P * (b + 1)
                        for h in range(IDX_HEADS):
                            act.wait_ge(s_ixp, m + 1)
                            if m >= 2:
                                act.wait_ge(s_idx, m - 1)
                            A(RT[m % 2][:, 0:n], bank(2 + 4 * (m % 2), 2)[:, 0:n], ACT.Relu,
                              scale=float(A_DIM) ** -0.5).then_inc(s_rel, 1)
                            m += 1
                elif kind == "avkr":
                    read_tile(w, [(AVKR[:, :], every, {})])
                    act.wait_ge(s_red2, 1)
                    A(T2S[:, :], GST[0][:, :], ACT.Sin, scale=sgn2).then_inc(s_sin2, 1)
                    A(T2C[:, :], GST[0][:, :], ACT.Sin, scale=0.5).then_inc(s_sin2, 1)
                elif kind == "aq":
                    c = (c0 - AQ) // P
                    read_tile(w, [(AQP[:, :].rearrange("p (i c q) -> p c i q", c=4, q=QT)[:, c], every,
                                   {"scale": float(A_DIM) ** -0.5, "split": QT})])
                elif kind == "cq":
                    read_tile(w, [(chunk(CQB, (c0 - CQ) // P), every, {})])
                elif kind == "ckv":
                    read_tile(w, [(CKVB[:, :], every, {})])
                else:
                    g = i - Z_GATE
                    if g >= 2:
                        act.wait_ge(s_gs[g % 2], 16 * (g // 2))
                    else:
                        act.wait_ge(s_sin2, 3)
                    read_tile(w, [(GST[g % 2][:, :], every, {"fn": ACT.Sigmoid, "bias": vcol("b_gate_2", g)})])
                    act.wait_ge(*reads(w))
                    act.dma_start(gs[g], GST[g % 2][:, :]).then_inc(s_gs[g % 2], 16)
                    if i == LATENT_SUMS:
                        root(9, 6, 2 * P)
                        root(10, 7, P)
            for u in range(UPS):
                act.wait_ge(s_up, u + 1)
                b = bank(2 * (u % 4), 2)
                if u < 4:
                    A(chunk(KM, 2 * u, rows=top), b[0:64, :], ACT.Copy).then_inc(s_act, 1)
                    A(chunk(KM, 2 * u + 1, rows=top), b[64:P, :], ACT.Copy).then_inc(s_upa, 1)
                elif u < 8:
                    A(chunk(VM, u - 4), b, ACT.Copy).then_inc(s_upa, 1)
                elif u < 16:
                    A(chunk(QM, u - 8, rows=top), b[0:64, :], ACT.Copy, scale=float(B_QK) ** -0.5).then_inc(s_upa, 1)
                else:
                    act.wait_ge(s_mb, NB)
                    A(VA[:, :], b[:, 0:HALF], ACT.Copy).then_inc(s_upa, 1)

            def probs_copied(n):
                act.wait_ge(s_pt, n + 1)
                if n >= 2:
                    act.wait_ge(s_pv, n - 1)
                if n < 2:
                    for j in range(2):
                        act.wait_ge(s_gs[j], 128)
                w = P * (ATT[n][0] + 1)
                A(PTS[n % 2][:, 0:w], bank(4, 2)[:, 0:w], ACT.Copy).then_inc(s_pte, 1)

            def back_copied(j):
                act.wait_ge(s_bt, j + 1)
                if j < 4:
                    A(chunk(YB, j), bank(4, 2), ACT.Copy).then_inc(s_bte, 1)
                else:
                    b = j - 4
                    src = bank(4, 2)[0:64, :].rearrange("p (r e c q) -> p r e c q", r=NB, c=4, e=2)
                    for e in range(2):
                        dst = YA[64 * e:64 * e + 64, :].rearrange("p (c b r q) -> p b r c q", c=4, b=NB, r=NB)[:, b]
                        A(dst, src[:, :, e], ACT.Copy).then_inc(s_act if e == 0 else s_bte, 1)

            def scaled(n):
                act.wait_ge(s_pv, n + 1)
                act.wait_ge(s_ri, n + 1)
                at = ATT[n][0] * P + (n % 2) * 64 if n < 64 else (n % 8) * 64
                A(OB[:, at:at + 64], bank(6 + n % 2)[:, 0:64], ACT.Copy, scale=RINV[:, n % 4:n % 4 + 1]).then_inc(s_oe, 1)

            for n0 in (0, 64):
                n1 = n0 + 64
                for n in range(n0, n1 + 4):
                    if n < n1:
                        act.wait_ge(s_nm, n + 1)
                        if n >= 2:
                            act.wait_ge(s_pt, n - 1)
                        if n >= 4:
                            act.wait_ge(s_ri, n - 3)
                        w = P * (ATT[n][0] + 1)
                        A(PB[n % 2][:, 0:w], bank(2 * (n % 2), 2)[:, 0:w], ACT.Exp, bias=NMX[:, n % 2:n % 2 + 1],
                          accum_out=RSUM[:, n % 4:n % 4 + 1]).then_inc(s_exp, 1)
                    if n - 4 >= n0 and n - 4 in BACK:
                        back_copied(BACK[n - 4])
                    if n0 <= n - 1 < n1:
                        probs_copied(n - 1)
                    if n0 <= n - 3 < n1:
                        scaled(n - 3)
            act.wait_ge(s_bte, 12)
            for k in range(KC):
                A(chunk(H, k), chunk(YA, k) if k < 4 else chunk(YB, k - 4), ACT.Copy).then_inc(s_hi, 1)
            act.wait_ge(s_mm, OUT0)
            for k in range(KC):
                act.wait_ge(s_evv, reads(BR0 + 2 * (k // 2) + 1)[1])
                A(chunk(H, k), chunk(Y, k), ACT.Copy).then_inc(s_hi, 1)
            for i in range(8):
                act.wait_ge(*reads(OUT0 + i))
                square(5 * KC + i, chunk(X, i))
            root(11, 6)
            high(M2.f32 - KC)
            mlp_act(M2)
            for k in range(KC):
                act.wait_ge(s_evv, M2.dve + 4 * (GROUPS - 1) + k // 2 + 1)
                square(6 * KC + k, chunk(X, k))
            root(12, 6)
            for t in range(NB):
                act.wait_ge(s_ft, t + 1)
                if t >= 2:
                    act.wait_ge(s_out[t % 2], 16 * (t // 2))
                A(OT[t % 2][:, :], bank(4 * (t % 2), 2), ACT.Copy).then_inc(s_fo, 1)


        @block.vector
        def _(dve):
            V = nc.vector
            own = [0]

            def link(ins):
                own[0] += 1
                ins.then_inc(s_dve, 1)
                dve.wait_ge(s_dve, own[0])

            def recip(r):
                dve.wait_ge(s_std, r + 1)
                V.reciprocal(RS[:, :], SS[:, :]).then_inc(s_rs, 1)

            def low(src, k, first):
                dve.wait_ge(s_hi, first + k + 1)
                V.tensor_sub(chunk(L, k), src, chunk(H, k).bitcast(F32)).then_inc(s_lo, 1)

            def reduce_angle(t, tmp, inv):
                link(V.tensor_scalar(t, t, inv, None, ALU.mult))
                link(V.tensor_scalar(tmp, t, 1.0 / (2 * np.pi), MAGIC, ALU.mult, ALU.add))
                link(V.tensor_scalar(tmp, tmp, MAGIC, None, ALU.subtract))
                for c in TWO_PI:
                    link(V.scalar_tensor_tensor(t, tmp, -c, t, ALU.mult, ALU.add))

            dve.wait_ge(s_rot, 16)
            link(V.tensor_copy(CT[:, :], ROT_S[:, :].bitcast(I32)))
            dve.wait_ge(s_const, 80)
            link(V.tensor_copy(IDB[:, :], ident))
            link(V.tensor_copy(TRB[:, :], STG[:, 2 * P:3 * P]))
            reduce_angle(CT[:, :], ROT_C[:, :], inv1)
            V.tensor_scalar(CT[:, :], CT[:, :], PI, -PI, ALU.min, ALU.max).then_inc(s_red, 1)

            def add_square(n):
                dve.wait_ge(s_sq, n + 1)
                dve.wait_ge(*added(n - 1))
                if n % KC == 0:
                    V.tensor_copy(ACC[:, :], sq_buffer(n)[:, :]).then_inc(s_acc[0], 1)
                else:
                    V.tensor_add(ACC[:, :], ACC[:, :], sq_buffer(n)[:, :]).then_inc(s_acc[0], 1)

            def weigh(n):
                g, k = n // KC, n % KC
                if n < ADA_EARLY:
                    dve.wait_ge(s_ada_first[n // 4], 16)
                    src = [ADA_H, ADA_H, ADA_L, WK][n // 4][:, (n % 8 if g == 0 else n % 4) * S:][:, 0:S]
                else:
                    dve.wait_ge(s_ada_in[n % 4], 16 * ((n - ADA_EARLY) // 4 + 1))
                    src = ADA[n % 4][:, :]
                if n:
                    dve.wait_ge(s_msum, n)
                to = MSUM[g if g < 2 else 2 + g % 2][:, :]
                if k == 0:
                    if g >= 4:
                        dve.wait_ge(s_ada, g - 1)
                    V.tensor_scalar(to, src, SILC[:, k:k + 1], None, ALU.mult).then_inc(s_msum, 1)
                else:
                    V.scalar_tensor_tensor(to, src, SILC[:, k:k + 1], to, ALU.mult, ALU.add).then_inc(s_msum, 1)

            dve.wait_ge(s_silc, 1)
            for n in range(ADA_EARLY):
                weigh(n)
            dve.wait_ge(s_sin, 2)
            link(V.scalar_tensor_tensor(CT[:, :], ROT_C[:, :], -2.0, ROT_C[:, :], ALU.mult, ALU.mult))
            link(V.tensor_scalar(ROT_C[:, :], CT[:, :], 1.0, None, ALU.add))
            recip(0)
            link(V.memset(CU[:, 0:2], 0.0))

            def modulation(g):
                a = 8 * ADA_GROUPS[g]
                n = VCOL["b_ada"] + a
                link(V.tensor_tensor(MOD[:, 8 * g:8 * g + 8], bank(6)[:, 8 * g:8 * g + 8], VEC[:, n:n + 8], ALU.add))

            def gains(name):
                return VEC[:, VCOL[name]:VCOL[name] + 8]

            dve.wait_ge(s_vec, 1)
            dve.wait_ge(s_ada, 2)
            modulation(0)
            modulation(1)
            link(V.scalar_tensor_tensor(MODA[:, 0:8], MOD[:, 0:8], 1.0, gains("g_pre_mix"), ALU.add, ALU.mult))

            def norm_split(r, b, scale, shift, n32, first, i):
                dve.wait_ge(s_bc, r + 1)
                for k in range(KC):
                    if shift:
                        if k:
                            dve.wait_ge(s_h32, n32 + k)
                        link(V.tensor_tensor(ACC[:, :], chunk(X, k), bank(b, 2), ALU.mult))
                    if k >= 2:
                        dve.wait_ge(s_hi, first + k - 1)
                        dve.wait_ge(s_nlo, KC * i + k - 1)
                    if shift:
                        V.tensor_scalar(SQ[k % 2][:, :], ACC[:, :], scale(k), shift(k), ALU.mult, ALU.add).then_inc(s_h32, 1)
                    else:
                        V.scalar_tensor_tensor(SQ[k % 2][:, :], chunk(X, k), scale(k), bank(b, 2), ALU.mult,
                                               ALU.mult).then_inc(s_h32, 1)

            dve.wait_ge(s_xc, KC)
            norm_split(0, 2, lambda k: MODA[:, k:k + 1], lambda k: MOD[:, 8 + k:9 + k], 0, 0, 0)

            def tap(j, i):
                return vcol("conv_w", 4 * i + j)

            def rotate(w, dst, scale, done):
                src = bank(w_bank(w), 2)
                dve.wait_ge(s_mm, w + 1)
                V.scalar_tensor_tensor(R_T[:, :], src, scale, ROT_C[:, :], ALU.mult, ALU.mult).then_inc(s_rt, 1)
                for lo in (0, 64):
                    hi = 64 - lo
                    ins = V.scalar_tensor_tensor(R_T2[lo:lo + 64, :], src[hi:hi + 64, :], scale,
                                                 ROT_S[hi:hi + 64, :], ALU.mult, ALU.mult)
                    ins.then_inc(s_rt if lo == 0 else s_evv, 1)
                dve.wait_ge(s_rt, 2 * rots[0] + 2)
                dve.wait_ge(*reads(w))
                rots[0] += 1
                V.tensor_add(dst[:, :], R_T[:, :], R_T2[:, :]).then_inc(done, 1)

            rots = [0]
            blocks3 = lambda t: t.rearrange("p (b n) -> p b n", b=NB)

            def repeated(t):
                return t.rearrange("p (o n) -> p o n", o=1).broadcast_to([P, NB, P])

            def ret_finish(h):
                dve.wait_ge(s_r_o, h + 1)
                dve.wait_ge(*reads(12 + 4 * h + 3))
                dve.wait_ge(s_r_sq, h + 1)
                V.tensor_tensor(R_OG[:, :], bank(2, 2), R_G[:, :], ALU.mult).then_inc(s_r_og, 1)
                recip(1 + h)

            def ret_out(h):
                dve.wait_ge(s_bc, h + 2)
                dve.wait_ge(s_r_og, h + 1)
                V.tensor_tensor(chunk(Y, CONV + h), R_OG[:, :], bank(6, 2), ALU.mult).then_inc(s_ret_y, 1)

            n_ada = ADA_EARLY
            for w, (kind, h, _) in enumerate(W_IN):
                if kind == "c":
                    dve.wait_ge(s_mm, w + 1)
                    dve.wait_ge(*reads(w - 1))
                    V.tensor_tensor(CU[:, 2:S + 2], bank(w_bank(w), 2), CX[:, :], ALU.mult).then_inc(s_evv, 1)
                    dve.wait_ge(*reads(w))
                    link(V.tensor_scalar(CT[:, :], CU[:, 0:S], tap(h, 0), None, ALU.mult))
                    for i in (1, 2):
                        link(V.scalar_tensor_tensor(CT[:, :], CU[:, i:i + S], tap(h, i), CT[:, :], ALU.mult, ALU.add))
                elif kind == "b":
                    dve.wait_ge(s_mm, w + 1)
                    V.tensor_tensor(chunk(Y, h), bank(w_bank(w), 2), CT[:, :], ALU.mult).then_inc(s_evv, 1)
                elif kind == "q":
                    rotate(w, R_QR, 1.0, s_r_q)
                    dve.wait_ge(s_r_q, h + 1)
                    dve.wait_ge(s_dec, 16)
                    if h:
                        dve.wait_ge(s_r_o, h)
                    V.tensor_tensor(blocks3(R_QD[:, :]), blocks3(R_QR[:, :]), repeated(DEC[:, 512 + h * P:512 + (h + 1) * P]),
                                    ALU.mult).then_inc(s_r_qd, 1)
                elif kind == "k":
                    rotate(w, R_KR, float(RET_DIM) ** -0.5, s_r_k)
                    if h:
                        ret_finish(h - 1)
                elif kind == "v":
                    if h:
                        ret_out(h - 1)
                elif kind == "g":
                    dve.wait_ge(s_r_sc, h + 1)
                    V.tensor_tensor(blocks3(R_SD[:, :]), blocks3(bank(2, 2)), repeated(DEC[:, h * P:(h + 1) * P]),
                                    ALU.mult).then_inc(s_r_sd, 1)
                    dve.wait_ge(s_r_kv, h + 1)
                    link(V.tensor_copy(R_ST[:, 0:P], bank(6)[:, 0:P]))
                    for t in range(1, NB - 1):
                        ins = V.scalar_tensor_tensor(R_ST[:, t * P:(t + 1) * P], R_ST[:, (t - 1) * P:t * P],
                                                     GAMMA_BLOCK[h], bank(6, 2)[:, t * P:(t + 1) * P], ALU.mult, ALU.add)
                        if t < NB - 2:
                            link(ins)
                    ins.then_inc(s_r_st, 1)
                for _ in range(ADA_PER_TILE):
                    if n_ada < ADA_STEPS:
                        weigh(n_ada)
                        n_ada += 1
                if kind == "k" and h == 0:
                    dve.wait_ge(s_ada, 6)
                    for g in range(2, 6):
                        modulation(g)
                    V.tensor_tensor(MODA[:, 8:16], MOD[:, 16:24], gains("g_post_mix"), ALU.mult)
                    V.scalar_tensor_tensor(MODA[:, 16:24], MOD[:, 32:40], 1.0, gains("g_pre_mlp"), ALU.add, ALU.mult)
                    V.tensor_tensor(MODA[:, 24:32], MOD[:, 40:48], gains("g_post_mlp"), ALU.mult).then_inc(s_mod, 1)
            h = RET_HEADS - 1
            for k in range(4):
                low(chunk(Y, k), k, KC)
            ret_finish(h)
            for k in range(4, KC - 1):
                low(chunk(Y, k), k, KC)
            ret_out(h)
            low(chunk(Y, KC - 1), KC - 1, KC)

            for k in range(KC):
                add_square(KC + k)

            def residual(r, gain, first_x):
                recip(r)
                dve.wait_ge(s_bc, r + 1)
                for k in range(KC):
                    if first_x + k:
                        dve.wait_ge(s_xn, first_x + k)
                    link(V.tensor_tensor(CT[:, :], chunk(Y, k), bank(2, 2), ALU.mult))
                    V.scalar_tensor_tensor(chunk(X, k), CT[:, :], gain(k), chunk(X, k), ALU.mult,
                                           ALU.add).then_inc(s_xn, 1)

            dve.wait_ge(s_xr, 16)
            dve.wait_ge(s_mod, 1)
            residual(5, lambda k: MODA[:, 8 + k:9 + k], 0)
            recip(6)
            norm_split(6, 2, lambda k: MODA[:, 16 + k:17 + k], lambda k: MOD[:, 24 + k:25 + k], KC, 2 * KC, 1)

            def mlp_dve(m, acc, fresh, squares):

                def group(g, first, last):
                    for i in range(4):
                        dve.wait_ge(s_eva, 4 * g + (m.act + i + 1))
                        if not (first and i == 0):
                            dve.wait_ge(s_lo, 4 * g + (m.lo + i))
                        V.tensor_tensor(FT[:, :], RL[i % 2][:, :], RL[i % 2][:, :], ALU.mult).then_inc(s_h32, 1)
                        dve.wait_ge(s_h32, 4 * g + (m.f32 + i + 1))
                        dve.wait_ge(s_hi, 4 * g + (m.hi + i + 1))
                        V.tensor_sub(chunk(FL, i), FT[:, :], chunk(FH, i).bitcast(F32)).then_inc(s_lo, 1)
                    for c in range(4):
                        dve.wait_ge(s_mm, 8 * g + (m.w + 4 + c + 1))
                        dst = chunk(acc, 2 * c, 2)
                        if first and fresh:
                            V.tensor_copy(dst, bank(4 * (c % 2), 4)).then_inc(s_evv, 1)
                        else:
                            dve.wait_ge(s_evv, 4 * g + (m.dve + c))
                            V.tensor_tensor(dst, dst, bank(4 * (c % 2), 4), ALU.add).then_inc(s_evv, 1)
                        if last:
                            for k in (2 * c - 1, 2 * c):
                                if k >= 0:
                                    add_square(squares + k)

                group(0, True, False)
                with dve.Fori(1, GROUPS - 1) as g:
                    group(g, False, False)
                group(GROUPS - 1, False, True)
                add_square(squares + KC - 1)

            mlp_dve(M1, Y, True, 3 * KC)
            residual(7, lambda k: MODA[:, 24 + k:25 + k], KC)
            recip(8)
            norm_split(8, 2, lambda k: vcol("attn_norm_g_2", k), None, 2 * KC + 4 * GROUPS, M1.hi + 4 * GROUPS, 2)

            dve.wait_ge(s_pos2, 16)
            link(V.tensor_copy(GST[0][:, :], T2S[:, :].bitcast(I32)))
            reduce_angle(GST[0][:, :], GST[1][:, :], inv2)
            V.tensor_scalar(GST[0][:, :], GST[0][:, :], PI, -PI, ALU.min, ALU.max).then_inc(s_red2, 1)
            dve.wait_ge(s_iwt, 1)
            V.tensor_scalar(IWTOK[:, :], bank(7)[:, 0:32], float(IDX_HEADS) ** -0.5, None, ALU.mult).then_inc(s_iw, 1)
            dve.wait_ge(s_iw, 1)
            m = 0
            for b in range(2, NB):
                n = P * (b + 1)
                sc = SCO[:, SCORE_AT[b]:SCORE_AT[b] + n]
                for h in range(IDX_HEADS):
                    dve.wait_ge(s_rel, m + 1)
                    iw = IWTOK[:, 4 * b + h:4 * b + h + 1]
                    if h == 0:
                        V.tensor_scalar(sc, RT[m % 2][:, 0:n], iw, None, ALU.mult).then_inc(s_idx, 1)
                    else:
                        dve.wait_ge(s_idx, m)
                        V.scalar_tensor_tensor(sc, RT[m % 2][:, 0:n], iw, sc, ALU.mult, ALU.add).then_inc(s_idx, 1)
                    m += 1
            dve.wait_ge(s_sin2, 2)
            link(V.scalar_tensor_tensor(GST[1][:, :], T2C[:, :], -2.0, T2C[:, :], ALU.mult, ALU.mult))
            V.tensor_scalar(T2C[:, :], GST[1][:, :], 1.0, None, ALU.add).then_inc(s_sin2, 1)
            link(V.memset(MB[:, P:2 * P], 0.0))
            V.tensor_copy(MB[:, 0:P], TRB[:, :]).then_inc(s_mb, 1)
            V.tensor_copy(MB[:, 2 * P:3 * P], TRB[:, :]).then_inc(s_mb, 1)

            selecting = range(2, NB)
            every = slice(0, NB - 2)

            def scores(b):
                return SCO[:, SCORE_AT[b]:SCORE_AT[b] + P * (b + 1)]

            def mask(b):
                return MB[:, MASK_AT[b]:MASK_AT[b] + P * (b + 1)]

            def count(op):
                for b in selecting:
                    own[0] += 1
                    V.tensor_scalar(mask(b), scores(b), CAND[:, b - 2:b - 1].bitcast(F32), 0.0, op, ALU.add,
                                    accum_out=REACH[:, b - 2:b - 1]).then_inc(s_dve, 1)
                dve.wait_ge(s_dve, own[0])

            dve.wait_ge(s_diag, NB - 2)
            link(V.memset(KEY[:, :], 0))
            link(V.memset(CAND[:, :], 0))
            count(ALU.is_ge)
            link(V.tensor_scalar(FLIP[:, every], REACH[:, every], TOPK - 0.5, -1.0, ALU.is_lt, ALU.mult))
            for bit in range(30, -1, -1):
                link(V.scalar_tensor_tensor(CAND[:, every], KEY[:, every], 1 << bit, FLIP[:, every], ALU.bitwise_or,
                                            ALU.bitwise_xor))
                count(ALU.is_ge)
                link(V.tensor_scalar(NEXT[:, every], REACH[:, every], TOPK - 0.5, float(1 << bit), ALU.is_ge, ALU.mult))
                link(V.tensor_tensor(KEY[:, every], KEY[:, every], NEXT[:, every], ALU.bitwise_or))
            link(V.tensor_tensor(CAND[:, every], KEY[:, every], FLIP[:, every], ALU.bitwise_xor))
            count(ALU.is_gt)
            link(V.tensor_scalar(ROOM[:, every], REACH[:, every], -1.0, float(TOPK), ALU.mult, ALU.add))
            for b in selecting:
                n = P * (b + 1)
                least, room = CAND[:, b - 2:b - 1].bitcast(F32), ROOM[:, b - 2:b - 1]
                equal, chosen = RT[0][:, 0:n], RT[1][:, 0:n]
                link(V.tensor_scalar(equal, scores(b), least, None, ALU.is_equal))
                link(V.tensor_tensor_scan(chosen, ones.to_broadcast([P, n]), equal, 0.0, ALU.mult, ALU.add))
                link(V.scalar_tensor_tensor(chosen, chosen, room, equal, ALU.is_le, ALU.mult))
                link(V.scalar_tensor_tensor(chosen, scores(b), least, chosen, ALU.is_gt, ALU.add))
                V.tensor_scalar(mask(b), chosen, -1.0, -NEG, ALU.add, ALU.mult).then_inc(s_mb, 1)

            dve.wait_ge(*reads(Z0 + Z_GATE - 1))
            link(V.tensor_mul(RT[0][:, :], chunk(CQB, 0), chunk(CQB, 0)))
            link(V.tensor_mul(RT[1][:, :], chunk(CQB, 1), chunk(CQB, 1)))
            V.tensor_add(RT[0][:, :], RT[0][:, :], RT[1][:, :]).then_inc(s_lacc, 1)
            V.tensor_mul(IWT[:, :], CKVB[:, :], CKVB[:, :]).then_inc(s_lacc, 1)
            recip(9)
            dve.wait_ge(s_bc, 10)
            for k in range(2):
                V.scalar_tensor_tensor(chunk(CQB, k), chunk(CQB, k), vcol("q_latent_norm_g_2", k), bank(2, 2), ALU.mult,
                                       ALU.mult).then_inc(s_lat, 1)
            recip(10)
            dve.wait_ge(s_bc, 11)
            V.scalar_tensor_tensor(CKVB[:, :], CKVB[:, :], vcol("kv_latent_norm_g_2", 0), bank(6, 2), ALU.mult,
                                   ALU.mult).then_inc(s_lat, 1)
            dve.wait_ge(s_mm, BR0)
            dve.wait_ge(s_up, 8)
            dve.wait_ge(s_sin2, 3)
            V.tensor_mul(PB[0][64:96, :], AVKR[64:96, :], T2C[64:96, :]).then_inc(s_kt, 1)
            V.tensor_mul(PB[1][64:96, :], AVKR[96:P, :], T2S[96:P, :]).then_inc(s_kt, 1)
            dve.wait_ge(s_kt, 2)
            V.tensor_add(KM[64:96, 0:S], PB[0][64:96, :], PB[1][64:96, :]).then_inc(s_kr, 1)
            for h in range(B_HEADS):
                u = 8 + h
                dve.wait_ge(s_up, u + 1)
                b = bank(2 * (u % 4), 2)
                dve.wait_ge(s_kr if h == 0 else s_q, 1 if h == 0 else h)
                scale = float(B_QK) ** -0.5
                V.scalar_tensor_tensor(PB[0][64:96, :], b[64:96, :], scale, T2C[64:96, :], ALU.mult, ALU.mult).then_inc(s_kt, 1)
                V.scalar_tensor_tensor(PB[1][64:96, :], b[96:P, :], scale, T2S[96:P, :], ALU.mult, ALU.mult).then_inc(s_upd, 1)
                dve.wait_ge(s_kt, 3 + h)
                dve.wait_ge(s_upd, h + 1)
                V.tensor_add(QM[64:96, h * S:(h + 1) * S], PB[0][64:96, :], PB[1][64:96, :]).then_inc(s_q, 1)

            def inverse_sum(n):
                dve.wait_ge(s_exp, n + 1)
                if n >= 4:
                    dve.wait_ge(s_oe, n - 3)
                V.reciprocal(RINV[:, n % 4:n % 4 + 1], RSUM[:, n % 4:n % 4 + 1]).then_inc(s_ri, 1)

            def steps_of(i):
                w = P * (i // NB + 1)
                if i >= 2:
                    dve.wait_ge(s_lg, 64 + i - 1)
                for g in range(NSTEP):
                    V.tensor_scalar(STEP[i % 2][:, g * S:g * S + w], POSB[:, 0:w], THR[:, NSTEP * i + g:NSTEP * i + g + 1],
                                    None, ALU.is_le).then_inc(s_step, 1)

            for n in range(128):
                if n == 64:
                    inverse_sum(63)
                    dve.wait_ge(s_c4, 48)
                    link(V.tensor_copy(POSB[:, :], POSB[:, :].bitcast(I32)))
                    link(V.tensor_copy(SELB[:, :], CST[:, 0:1024]))
                    for t in range(STEPQ):
                        rows = slice(BUCKETS * t, BUCKETS * (t + 1))
                        link(V.tensor_scalar(THR[rows, :], POSB[rows, t:S:STEPQ], steps[rows, :], None, ALU.subtract))
                    dve.wait_ge(s_tp, 1)
                    link(V.tensor_copy(DLT[:, :], bank(7)[:, 0:8]))
                    for g in range(NSTEP):
                        at = slice(g * P, (g + 1) * P)
                        view = lambda t: t.rearrange("p (e c q) -> p e c q", e=2, q=QT)
                        link(V.tensor_tensor(view(DF[:, at]), view(CST[:, 1152 + g * P:1152 + (g + 1) * P]),
                                             DLT[:, :].rearrange("p (c e o) -> p e c o", e=2, o=1).broadcast_to([P, 2, 4, QT]),
                                             ALU.mult))
                    link(V.tensor_copy(DHI[:, :], DF[:, :]))
                    V.tensor_sub(DLO[:, :], DF[:, :], DHI[:, :].bitcast(F32)).then_inc(s_tpd, 1)
                    dve.wait_ge(s_aq, 32)
                    steps_of(0)
                if n >= 64 and n + 1 < 128:
                    steps_of(n + 1 - 64)
                dve.wait_ge(s_lg, n + 1)
                w = P * (ATT[n][0] + 1)
                if n >= 2:
                    dve.wait_ge(s_exp, n - 1)
                V.reduce_max(NMX[:, n % 2:n % 2 + 1], bank(2 * (n % 2), 2)[:, 0:w], AX, negate=True).then_inc(s_nm, 1)
                if n % 64:
                    inverse_sum(n - 1)
            inverse_sum(127)
            for k in range(KC):
                low(chunk(YA, k) if k < 4 else chunk(YB, k - 4), k, M2.hi - 3 * KC)
            for m in range(8):
                w = BR0 + m
                dve.wait_ge(s_mm, w + 1)
                dve.wait_ge(s_g[m % 4], 16 * (m // 4 + 1))
                dst = chunk(Y, 2 * (m // 2), 2)
                psum = bank(w_bank(w), 4)
                if m % 2 == 0:
                    V.tensor_mul(dst, psum, GB[m % 4][:, :]).then_inc(s_evv, 1)
                else:
                    link(V.tensor_mul(MT[:, :], psum, GB[m % 4][:, :]))
                    dve.wait_ge(s_evv, reads(w - 1)[1])
                    V.tensor_add(dst, dst, MT[:, :]).then_inc(s_evv, 1)
            for k in range(KC):
                low(chunk(Y, k), k, M2.hi - 2 * KC)
            dve.wait_ge(s_xr, 32)
            for i in range(8):
                w = OUT0 + i
                dve.wait_ge(s_mm, w + 1)
                V.tensor_add(chunk(X, i), chunk(X, i), bank(w_bank(w), 2)).then_inc(s_evv, 1)
                if i:
                    add_square(5 * KC + i - 1)
            add_square(6 * KC - 1)
            recip(11)
            norm_split(11, 2, lambda k: vcol("mlp_norm_g_2", k), None, M2.f32 - KC, M2.hi - KC, 3)
            mlp_dve(M2, X, False, 6 * KC)
            recip(12)
            dve.wait_ge(s_bc, 13)
            for k in range(KC):
                V.scalar_tensor_tensor(chunk(X, k), chunk(X, k), vcol("final_norm_g_2", k), bank(2, 2), ALU.mult,
                                       ALU.mult).then_inc(s_fin, 1)


_MATRICES = ["w_ada", "w_in", "w_out", "w_fc1", "w_fc2", "w_in_2", "w_uq_2", "w_ukv_2", "w_branch_a_2", "w_branch_b_2",
             "w_out_2", "w_ff1_2", "w_ff2_2"]


def kernel(**inputs):
    import numpy as _np
    import concourse.bacc as _bacc
    from concourse import mybir as _mybir
    from concourse.bass_utils import run_bass_kernel_spmd as _run

    given = {name: _np.ascontiguousarray(a) for name, a in inputs.items()}
    arrays = {"x": given["x"].reshape(S, D), "positions": given["positions"].reshape(1, S)}
    for name in _MATRICES:
        arrays[name] = given[name].reshape(given[name].shape[-2:])
    arrays["positions_2"] = given["positions_2"].reshape(1, S)
    arrays["rel_bias_2"] = given["rel_bias_2"]
    arrays["vec"] = _np.concatenate([given[name].reshape(-1, P) for name, _ in VEC_A + VEC_B])
    arrays["const"] = CONST

    nc = _bacc.Bacc("TRN2", target_bir_lowering=False, num_devices=1)
    args = {n: nc.dram_tensor(n, a.shape, _mybir.dt.from_np(a.dtype), kind="ExternalInput").ap()
            for n, a in arrays.items()}
    args["out"] = nc.dram_tensor("out", (S, D), _mybir.dt.float32, kind="ExternalOutput").ap()
    build(nc, **args)
    result = _run(nc, [arrays], core_ids=[0])
    return result.results[0]["out"].reshape(1, S, D)
```

```python
from contextlib import ExitStack

import numpy as np

import concourse.bass as bass
from concourse import mybir

F32 = mybir.dt.float32
F32R = mybir.dt.float32r
BF16 = mybir.dt.bfloat16
I32 = mybir.dt.int32
ALU = mybir.AluOpType
ACT = mybir.ActivationFunctionType
AX = mybir.AxisListType.X

P = 128
S = 1024
D = 1024
KC = D // P
NB = S // P
HALF = 512
DFF = 4 * D
EPS = 1e-6

RET_HEADS, RET_DIM, CHUNK = 4, 128, 64
CONV = 4

A_HEADS, A_DIM = 8, 64
IDX_HEADS, TOPK = 4, 256
B_HEADS, B_NOPE, B_ROPE, B_QK, B_V = 8, 64, 32, 96, 64
BUCKETS = 32
QT = P // A_HEADS
STEPQ = P // BUCKETS
NSTEP = QT // STEPQ

NEG = -1e30
HIDDEN = -3.0e38

AQ, AK, AV, IQ, IK, IW, CQ, CKV, KR, GT = 0, 512, 576, 640, 896, 960, 964, 1220, 1348, 1380

VEC_A = [("c", 8), ("b_ada", 48), ("g_pre_mix", 8), ("g_post_mix", 8), ("g_pre_mlp", 8), ("g_post_mlp", 8),
         ("conv_w", 12)]
VEC_B = [("attn_norm_g_2", 8), ("b_gate_2", 16), ("q_latent_norm_g_2", 2), ("kv_latent_norm_g_2", 1),
         ("mlp_norm_g_2", 8), ("final_norm_g_2", 8)]


def vec_columns():
    at, n = {}, 0
    for name, k in VEC_A + VEC_B:
        at[name] = n
        n += k
    return at


VCOL = vec_columns()
NVA = sum(k for _, k in VEC_A)
NVB = sum(k for _, k in VEC_B)


def bucket_steps():
    n = np.arange(1, 4096)
    f = np.float32
    log_b = 16 + (np.log(n.astype(f) / f(16)) / f(np.log(8.0)) * f(16)).astype(np.int32)
    b = np.where(n < 16, n, np.minimum(log_b, BUCKETS - 1))
    return [-1e9] + [float(n[np.argmax(b >= k)]) for k in range(1, BUCKETS)]


def constants():
    parts = {}
    i = np.arange(P)
    parts["ident"] = np.eye(P)
    parts["ones"] = np.ones((P, 1))
    parts["eps"] = np.full((P, 1), EPS)
    half = RET_DIM // 2
    inv = np.float32(10000.0) ** (-(np.arange(half, dtype=np.float32)) / np.float32(half))
    parts["inv1"] = np.tile(inv, 2)[:, None]
    inv2 = np.float32(10000.0) ** (-np.arange(0, B_ROPE, 2, dtype=np.float32) / np.float32(B_ROPE))
    parts["inv2"] = np.tile(inv2, 8)[:, None]
    parts["sgn1"] = np.where(i < half, 1.0, -1.0)[:, None]
    parts["sgn2"] = np.where(i % B_ROPE < 16, -1.0, 1.0)[:, None]
    parts["steps"] = np.tile(np.array(bucket_steps()), STEPQ)[:, None]
    gam = 1.0 - 2.0 ** (-5.0 - np.arange(RET_HEADS))
    j = i[:, None]
    q = i[None, :]
    allowed = (j // CHUNK) <= (q // CHUNK)
    parts["decay"] = np.concatenate([np.where(allowed, g ** np.abs(j - q), 0.0) for g in gam], axis=1)
    parts["qdec"] = np.concatenate([np.tile(g ** (q + 1.0), (P, 1)) for g in gam], axis=1)
    parts["kdec"] = np.stack([g ** (P - 1.0 - i) for g in gam], axis=1)
    sel = np.zeros((P, NB, A_HEADS, QT))
    for r in range(NB):
        for t in range(QT):
            sel[r * QT + t, r, :, t] = 1.0
    parts["sel"] = sel.reshape(P, NB * P)
    rep = np.zeros((P, P))
    for t in range(STEPQ):
        for b in range(BUCKETS):
            rep[b, t * BUCKETS + b] = 1.0
            if b:
                rep[b - 1, t * BUCKETS + b] = -1.0
    parts["rep"] = rep
    reach = np.zeros((P, NSTEP, A_HEADS, QT))
    for g in range(NSTEP):
        for t in range(STEPQ):
            reach[t * BUCKETS:(t + 1) * BUCKETS, g, :, g * STEPQ + t] = 1.0
    parts["reach"] = reach.reshape(P, NSTEP * P)
    parts["tri"] = np.where(i[None, :] > i[:, None], NEG, 0.0)
    at, n = {}, 0
    for name, a in parts.items():
        at[name] = (n, a.shape[1])
        n += a.shape[1]
    return at, np.concatenate([np.asarray(a, np.float32) for a in parts.values()], axis=1).astype(np.float32)


CONST_AT, CONST = constants()
MAGIC = 1.5 * 2.0 ** 23
PI = float(np.nextafter(np.float32(np.pi), np.float32(0)))
TWO_PI = [6.28125, float(np.float32(0.0019350051879882812)), 2 * np.pi - 6.28125 - float(np.float32(0.0019350051879882812))]
GAMMA_BLOCK = [float((1.0 - 2.0 ** (-5.0 - h)) ** P) for h in range(RET_HEADS)]


def build(nc, x, positions, w_ada, w_in, w_out, w_fc1, w_fc2, positions_2, w_in_2, w_uq_2, w_ukv_2,
          w_branch_a_2, w_branch_b_2, w_out_2, w_ff1_2, w_ff2_2, rel_bias_2, vec, const, out):
    ctx = ExitStack()
    with ctx:
        def sem(name):
            return ctx.enter_context(nc.semaphore(name))

        arena_words = 53100
        arena = ctx.enter_context(nc.sbuf_tensor("arena", [P, arena_words], F32))
        base = (nc.sbuf_base - arena_words * 4 + 31) // 32 * 32
        taken = [0]

        def place(name, words, dt=F32, at=None):
            n = words * 2 if dt == BF16 else words
            start = taken[0] if at is None else at
            t = nc.alloc_sbuf_tensor_at(name, [P, n], dt, offset=base + 4 * start)
            if at is None:
                taken[0] += words
            return t

        X0 = taken[0]
        X = place("X", KC * S)
        H0 = taken[0]
        H = place("H", KC * S, F32R)
        L0 = taken[0]
        L = place("L", KC * S, F32R)
        Y0 = taken[0]
        Y = place("Y", KC * S)
        RAW = [place(f"RAW{j}", 1024) for j in range(2)]
        WHI = [place(f"WHI{j}", 1024, F32R) for j in range(2)]
        WLO = [place(f"WLO{j}", 1024, F32R) for j in range(2)]
        IDN = place("IDN", P)
        SC = place("SC", 16)
        IDB = place("IDB", P // 2, BF16)
        TRB = place("TRB", P // 2, BF16)
        VEC = place("VEC", 144)
        MOD = place("MOD", 48)
        MODA = place("MODA", 40)
        SS = place("SS", 8)
        RS = place("RS", 8)
        SILC = place("SILC", 8)
        ZERO = place("ZERO", 8)
        K0 = taken[0]
        WKW = arena_words - K0 - 16
        WK = place("WK", WKW)
        assert WKW >= 13312, WKW

        def region(name, start, words, dt=F32):
            return place(name, words, dt, at=start)

        def chunk(t, k, n=1, rows=slice(0, P)):
            return t[rows, k * S:(k + n) * S]

        XT = region("XT", Y0, 8192)
        ADA = [region(f"ADA{j}", K0 + 1024 * j, S) for j in range(4)]
        ADA_H = region("ADA_H", H0, KC * S)
        ADA_L = region("ADA_L", L0, 4 * S)
        MSUM = [region(f"MSUM{j}", a, S) for j, a in enumerate([L0 + 4096, L0 + 5120, Y0 + 4096, Y0 + 5120])]
        STG = region("STG", K0 + 4096, 3 * P)
        CX = region("CX", K0 + 4096, S)
        CU = region("CU", K0 + 5120, S + 2)
        CT = region("CT", K0 + 6152, S)
        SQ = [region("SQ0", K0 + 12304, S), region("SQ1", K0 + 7176, S)]
        ROT_C = region("ROT_C", K0 + 8200, S)
        ROT_S = region("ROT_S", K0 + 9224, S)
        DEC = region("DEC", K0 + 10248, 1028)
        ACC = region("ACC", K0 + 11280, S)
        R_QR, R_KR, R_VT, R_VTOK, R_G, R_KTOK, R_QD, R_SD = [region(n, X0 + 1024 * i, S) for i, n in enumerate(
            ["R_QR", "R_KR", "R_VT", "R_VTOK", "R_G", "R_KTOK", "R_QD", "R_SD"])]
        R_T, R_T2, R_ST, R_SQ, R_OG = [region(n, K0 + 1024 * i, S) for i, n in enumerate(
            ["R_T", "R_T2", "R_ST", "R_SQ", "R_OG"])]
        FH = region("FH", K0, 4 * S, F32R)
        FL = region("FL", K0 + 4096, 4 * S, F32R)
        RL = [region(f"RL{j}", K0 + 8192 + 1024 * j, S) for j in range(2)]
        FT = region("FT", K0 + 10240, S)

        AQP = region("AQP", X0, 4 * S)
        CQB = region("CQB", X0 + 4096, 2 * S)
        CKVB = region("CKVB", X0 + 6144, S)
        AVKR = region("AVKR", X0 + 7168, S)
        SCORE_AT, n = {}, 0
        for b in range(2, NB):
            SCORE_AT[b] = n
            n += P * (b + 1)
        SCO = region("SCO", Y0, n)
        MASK_AT = {b: P * b * (b + 1) // 2 for b in range(NB)}
        MB = region("MB", Y0 + n, P * 36 // 2, BF16)
        AKB = region("AKB", Y0 + 6528, S)
        KEY, FLIP, CAND, NEXT = [region(n, Y0 + 7632 + 8 * i, 8, I32) for i, n in enumerate(["KEY", "FLIP", "CAND", "NEXT"])]
        REACH = region("REACH", Y0 + 7664, 8)
        ROOM = region("ROOM", Y0 + 7672, 8)
        IWTOK = region("IWTOK", Y0 + 7560, 32)
        NMX = region("NMX", Y0 + 7600, 8)
        RSUM = region("RSUM", Y0 + 7608, 8)
        RINV = region("RINV", Y0 + 7616, 8)
        IQB = region("IQB", K0, 2 * S)
        IKB = region("IKB", K0 + 2048, S)
        RT = [region(f"RT{j}", K0 + 3072 + 1024 * j, S) for j in range(2)]
        IWT = region("IWT", K0 + 5120, S)
        GST = [region(f"GST{j}", K0 + 6144 + 1024 * j, S) for j in range(2)]
        T2C = region("T2C", K0 + 8192, S)
        T2S = region("T2S", K0 + 9216, S)
        WUQ = region("WUQ", K0 + 10240, 2 * S)
        WUKV = region("WUKV", K0 + 12288, S)
        QM = region("QM", H0, 8 * S)
        KM = region("KM", L0, 8 * S)
        VM = region("VM", K0, 4 * S)
        PB = [region(f"PB{j}", K0 + 4096 + 1024 * j, S) for j in range(2)]
        PTS = [region(f"PTS{j}", K0 + 6144 + 1024 * j, S) for j in range(2)]
        OB = region("OB", K0 + 12288, S)
        YB = region("YB", X0 + 4096, 4 * S)
        VA = region("VA", Y0, NB * A_DIM)
        AQH = region("AQH", K0 + 8192, 4 * S, F32R)
        QS = region("QS", H0, 8 * S, F32R)
        KHH = region("KHH", L0, S, F32R)
        KLO = region("KLO", L0 + 5120, S, F32R)
        POSB = region("POSB", Y0 + 512, S)
        STEP = [region("STEP0", L0 + 1024, 4 * S, F32R), region("STEP1", X0, 4 * S, F32R)]
        DHI = region("DHI", Y0 + 1536, NSTEP * P, F32R)
        DLO = region("DLO", Y0 + 2048, NSTEP * P, F32R)
        SELB = region("SELB", Y0 + 2560, 512, BF16)
        THR = region("THR", Y0 + 3072, 256)
        DF = region("DF", Y0 + 3328, NSTEP * P)
        YA = region("YA", K0 + 8192, 4 * S)
        SEL = region("SEL", K0 + 8192, NB * P)
        REACHED = region("REACHED", K0 + 9216, NSTEP * P)
        REP = region("REP", K0 + 13328, P)
        TAB = region("TAB", K0 + 13456, 8)
        DLT = region("DLT", K0 + 13464, 8)
        GB = [region(f"GB{j}", K0 + 2048 * j, 2 * S) for j in range(4)]
        MT = region("MT", K0 + 8192, 2 * S)
        A2H = region("A2H", Y0, 8 * S, F32R)
        A2L = region("A2L", K0, 8 * S, F32R)
        F2H = region("F2H", L0, 4 * S, F32R)
        F2L = region("F2L", L0 + 4096, 4 * S, F32R)
        F2SUM = region("F2SUM", H0, 8 * S)
        RS2 = region("RS2", K0 + 12304, S)
        XG = region("XG", Y0, 8 * S)
        OT = [region(f"OT{j}", K0 + 1024 * j, S) for j in range(4)]

        PS = ctx.enter_context(nc.psum_tensor("PS", [P, 8 * HALF], F32))

        def bank(b, n=1, rows=slice(0, P)):
            return PS[rows, b * HALF:(b + n) * HALF]

        xs = nc.dram_tensor("x_scratch", [P, KC * S], F32).ap()
        gs = nc.dram_tensor("gate_scratch", [16, P, S], F32).ap()

        s_const = sem("const_in")
        s_x = [sem(f"x_in{j}") for j in range(2)]
        s_dec = sem("decays_in")
        s_rot = sem("rotation_tables")
        s_raw = [sem(f"raw_in{j}") for j in range(2)]
        s_ada_in = [sem(f"ada_in{j}") for j in range(4)]
        s_ada_first = [sem(f"ada_first_in{j}") for j in range(4)]
        s_msum = sem("modulation_weights_added")
        s_ada = sem("modulation_group_summed")
        s_whi = sem("weight_high_part")
        s_zero = sem("zero_ready")
        s_w = sem("weight_split")
        s_mm = sem("product_done")
        s_eva = sem("psum_read_by_act")
        s_evv = sem("psum_read_by_dve")
        s_vt = sem("vectors_transposed")
        s_vec = sem("vectors_ready")
        s_silc = sem("silu_of_c")
        s_xt = sem("x_transposed")
        s_xc = sem("x_copied")
        s_sq = sem("squares")
        s_acc = [sem("squares_added_by_dve"), sem("squares_added_by_pool")]
        s_ss = sem("row_sums_of_squares")
        s_std = sem("root_of_mean_square")
        s_rs = sem("reciprocal_root")
        s_bc = sem("reciprocal_root_spread")
        s_yn, s_xn = sem("branch_normed"), sem("residual_added")
        a_yn, a_xn, a_sq, a_acc, a_ss, a_std, a_rs, a_bc, a_h32, a_hi, a_nlo = [sem(f"first_half_{n}") for n in [
            "branch_normed", "residual_added", "squares", "squares_added", "row_sums", "root", "reciprocal_root",
            "reciprocal_root_spread", "normed_scaled", "high_part", "low_part"]]
        s_h32 = sem("normed_scaled")
        s_hi = sem("activation_high_part")
        s_lo = sem("activation_low_part")
        s_nlo = sem("normed_low_part")
        s_dve = sem("dve_own")
        s_act = sem("act_own")
        s_xs = sem("x_stored")
        s_xr = sem("x_reloaded")
        s_mod = sem("modulations_ready")
        s_red = sem("angles_reduced")
        s_sin = sem("sines")
        s_rt = sem("rotated_terms")
        s_r_q, s_r_k, s_r_qd = sem("ret_q"), sem("ret_k"), sem("ret_q_decayed")
        s_r_vT, s_r_kT = sem("ret_v_transposed"), sem("ret_k_transposed")
        s_r_vtok, s_r_ktok = sem("ret_v_tokens"), sem("ret_k_tokens")
        s_r_sc, s_r_sd = sem("ret_scores"), sem("ret_scores_decayed")
        s_r_kv, s_r_st = sem("ret_block_sums"), sem("ret_states")
        s_r_o, s_r_sq, s_r_og, s_ret_y = sem("ret_out"), sem("ret_squares"), sem("ret_gated"), sem("ret_done")
        s_pos2 = sem("positions_2_in")
        s_red2, s_sin2 = sem("angles_2_reduced"), sem("sines_2")
        s_iwt, s_iw = sem("index_weights_transposed"), sem("index_weights_ready")
        s_ixp, s_rel, s_idx = sem("index_product"), sem("index_relu"), sem("index_added")
        s_diag, s_mb = sem("scores_masked"), sem("selection_mask")
        s_gs = [sem(f"gate_stored{j}") for j in range(2)]
        s_wuq = sem("up_weights_in")
        s_lacc, s_lat = sem("latent_squares"), sem("latent_normed")
        s_up, s_upa, s_upd, s_q = sem("up_product"), sem("up_read_by_act"), sem("up_read_by_dve"), sem("query_rotated")
        s_kt, s_kr, s_krd = sem("key_terms"), sem("key_rotated"), sem("key_spread")
        s_lg, s_nm, s_exp, s_ri = sem("logits"), sem("row_max"), sem("probabilities"), sem("probability_sum_inverse")
        s_pt, s_pte, s_pv, s_oe = sem("probs_transposed"), sem("probs_t_copied"), sem("attended"), sem("attended_scaled")
        s_bt, s_bte = sem("attended_transposed"), sem("attended_t_copied")
        s_aqh, s_kparts = sem("query_high_parts"), sem("shared_keys_split")
        s_aq2 = sem("last_queries_moved")
        s_c4, s_aq, s_tpd = sem("tables_in"), sem("queries_moved"), sem("tables_ready")
        s_tab, s_tp = sem("bias_table_in"), sem("bias_steps_product")
        s_step = sem("steps")
        s_g = [sem(f"gates_in{j}") for j in range(4)]
        s_rs2, s_f2, s_x2 = sem("squared_reciprocal_root"), sem("down_sum_scaled"), sem("last_residual_added")
        s_fin, s_ft = sem("final_scaled"), sem("final_transposed")
        s_fo = [sem("final_copied_by_act"), sem("final_copied_by_dve")]
        s_out = [sem(f"out_stored{j}") for j in range(4)]
        block = ctx.enter_context(nc.Block())

        ident = IDN[:, :]
        ones = SC[:, 0:1]
        eps = SC[:, 1:2]
        inv1, inv2 = SC[:, 2:3], SC[:, 3:4]
        sgn1, sgn2 = SC[:, 4:5], SC[:, 5:6]
        steps = SC[:, 6:7]

        def vcol(name, k):
            n = VCOL[name] + k
            return VEC[:, n:n + 1]


        def w_tile(w, r0, kc, c0, nc_):
            return w[r0:r0 + kc * P, c0:c0 + nc_].rearrange("(k p) n -> p k n", p=P)

        def k_n(t, kc, n):
            return t[:, 0:kc * n].rearrange("p (k n) -> p k n", k=kc)

        W_IN = []
        for j in range(CONV):
            W_IN += [("xin", j, j * P), ("c", j, 1024 + j * P), ("b", j, 512 + j * P)]
        for h in range(RET_HEADS):
            W_IN += [(n, h, 1536 + 512 * i + h * P) for i, n in enumerate(["q", "k", "v", "g"])]
        ADA_GROUPS = (1, 0, 2, 3, 4, 5)
        ADA_STEPS = KC * len(ADA_GROUPS)
        ADA_EARLY = 2 * KC
        ADA_PER_TILE = 3
        ADA_SUMMED_AFTER = {4: 2, 7: 3, 9: 4, 12: 5}

        OWNER = {}
        for w, (kind, _, _) in enumerate(W_IN):
            OWNER[w] = "act" if kind in ("xin", "v", "g") else "dve"
        W_OUT0 = len(W_IN)
        for w in range(W_OUT0, W_OUT0 + 8):
            OWNER[w] = "act"
        MLP1 = W_OUT0 + 8

        def reads(w):
            who = OWNER[w]
            return (s_eva if who == "act" else s_evv), sum(OWNER[v] == who for v in range(w + 1))

        def w_bank(w):
            return 4 * (w % 2)


        GROUPS = DFF // 512

        class Counts:

            def __init__(self, w, act, dve, f32, hi, lo, nlo):
                self.w, self.act, self.dve, self.f32, self.hi, self.lo, self.nlo = w, act, dve, f32, hi, lo, nlo

        M1 = Counts(MLP1, sum(v == "act" for v in OWNER.values()), sum(v == "dve" for v in OWNER.values()),
                    2 * KC, 3 * KC, KC, 2 * KC)
        assert M1.w % 2 == 0

        def sq_buffer(n):
            return (RL if n // KC in SQUARES_IN_MLP else SQ)[n % 2]

        SQUARES_IN_MLP = (3, 5, 6)
        SQUARES_BY_POOL = (0, 2, 4)

        def added(n):
            by_pool = n // KC in SQUARES_BY_POOL
            return s_acc[by_pool], sum((v // KC in SQUARES_BY_POOL) == by_pool for v in range(n + 1))

        for g in range(GROUPS):
            for i in range(8):
                OWNER[MLP1 + 8 * g + i] = "act" if i < 4 else "dve"

        Z0 = MLP1 + 8 * GROUPS
        Z_TILES = [("iw", IW), ("iq", IQ), ("iq", IQ + P), ("akik", AK), ("avkr", AV)]
        Z_TILES += [("aq", AQ + P * i) for i in range(4)]
        Z_TILES += [("cq", CQ), ("cq", CQ + P), ("ckv", CKV)]
        Z_GATE = len(Z_TILES)
        LATENT_SUMS = Z_GATE + 5
        Z_TILES += [("gate", GT + P * i) for i in range(16)]
        BR0 = Z0 + len(Z_TILES)
        OUT0 = BR0 + 8
        MLP2 = OUT0 + 8
        for w in range(Z0, BR0):
            OWNER[w] = "act"
        for w in range(BR0, MLP2):
            OWNER[w] = "dve"
        DMAS = {Z0 + 3: 2, Z0 + 4: 4}

        def loads(w):
            return sum(DMAS.get(v, 1) for v in range(w % 2, w + 1, 2))

        M2 = Counts(MLP2, sum(v == "act" for v in OWNER.values()), sum(v == "dve" for v in OWNER.values()),
                    M1.f32 + 4 * GROUPS + KC, M1.hi + 4 * GROUPS + 4 * KC, M1.lo + 4 * GROUPS + 3 * KC, 0)
        assert M2.w % 2 == 0
        def half(t, k, e):
            return t[:, k * S + e * HALF:k * S + (e + 1) * HALF]

        Z_LO = M1.lo + 4 * GROUPS
        UPS = 17
        ATT = [(b, 2 * c + e) for c in range(4) for b in range(NB) for e in range(2)]
        ATT += [(b, r) for b in range(NB) for r in range(NB)]
        BACK = {16 * j + 15: j for j in range(4)}
        BACK.update({64 + 8 * j + 7: 4 + j for j in range(8)})
        GATED0 = sum(OWNER[v] == "dve" for v in range(BR0))

        @block.sync
        def _(sp):
            sp.dma_start(IDN[:, :], const[:, 0:P]).then_inc(s_const, 16)
            sp.dma_start(SC[:, 0:7], const[:, P:P + 7]).then_inc(s_const, 16)
            sp.dma_start(STG[0:NVA, 0:P], vec[0:NVA, :]).then_inc(s_const, 16)
            sp.dma_start(STG[0:NVB, P:2 * P], vec[NVA:NVA + NVB, :]).then_inc(s_const, 16)
            tri = CONST_AT["tri"][0]
            sp.dma_start(STG[:, 2 * P:3 * P], const[:, tri:tri + P]).then_inc(s_const, 16)
            sp.dma_start(ROT_S[:, :].bitcast(I32), positions.partition_broadcast(P)).then_inc(s_rot, 16)
            sp.dma_start(TAB[0:BUCKETS, :], rel_bias_2).then_inc(s_tab, 16)
            c = CONST_AT["rep"][0]
            sp.dma_start(REP[:, :], const[:, c:c + P]).then_inc(s_tab, 16)
            for j in range(2):
                sp.dma_start(XT[:, :].rearrange("p (b d) -> p b d", b=NB)[:, :, j * HALF:(j + 1) * HALF],
                             x.rearrange("(b p) d -> p b d", p=P)[:, :, j * HALF:(j + 1) * HALF]).then_inc(s_x[j], 16)
            def load_ada(n):
                sp.wait_ge(s_msum, n - 3)
                k, c = n % KC, D * ADA_GROUPS[n // KC]
                sp.dma_start(ADA[n % 4][:, :], w_ada[k * P:(k + 1) * P, c:c + D]).then_inc(s_ada_in[n % 4], 16)

            def load_w(w, src, kc, n):
                if w >= 2:
                    sp.wait_ge(s_w, w - 1)
                sp.dma_start(k_n(RAW[w % 2], kc, n), src).then_inc(s_raw[w % 2], 16)

            for j in range(4):
                to = [ADA_H[:, 0:4 * S], ADA_H[:, 4 * S:8 * S], ADA_L[:, :], WK[:, 0:4 * S]][j]
                sp.dma_start(to.rearrange("p (k n) -> p k n", k=4),
                             w_tile(w_ada, HALF * (j % 2), 4, D * ADA_GROUPS[j // 2], D)).then_inc(s_ada_first[j], 16)
                if j == 1:
                    load_w(0, w_tile(w_in, 0, KC, W_IN[0][2], P), KC, P)
            load_w(1, w_tile(w_in, 0, KC, W_IN[1][2], P), KC, P)
            sp.dma_start(DEC[:, :], const[:, CONST_AT["decay"][0]:CONST_AT["decay"][0] + 1028]).then_inc(s_dec, 16)
            sp.wait_ge(s_xc, KC)
            sp.dma_start(xs, X[:, :]).then_inc(s_xs, 16)
            n = ADA_EARLY
            for _ in range(4):
                load_ada(n)
                n += 1
            for w in range(2, len(W_IN)):
                load_w(w, w_tile(w_in, 0, KC, W_IN[w][2], P), KC, P)
                for _ in range(ADA_PER_TILE):
                    if w >= 3 and n < ADA_STEPS:
                        load_ada(n)
                        n += 1
            for i in range(8):
                load_w(W_OUT0 + i, w_tile(w_out, 0, KC, i * P, P), KC, P)
            sp.wait_ge(s_xs, 16)
            sp.wait_ge(s_ret_y, RET_HEADS)
            sp.dma_start(X[:, :], xs).then_inc(s_xr, 16)

            def mlp_loads(m, up, down):
                down_v = down.rearrange("(g k p) n -> g p k n", k=4, p=P)

                def group(g):
                    for i in range(8):
                        w = 8 * g + (m.w + i)
                        sp.wait_ge(s_w, w - 1)
                        if i < 4:
                            src = up.rearrange("(k p) n -> p k n", p=P)[:, :, bass.ds(512 * g + i * P, P)]
                            dst = k_n(RAW[i % 2], KC, P)
                        else:
                            src = down_v[bass.ds(g, 1), :, :, 256 * (i - 4):256 * (i - 3)].rearrange("o p k n -> (o p) k n")
                            dst = k_n(RAW[i % 2], 4, 256)
                        sp.dma_start(dst, src).then_inc(s_raw[i % 2], 16)

                with sp.Fori(0, GROUPS) as g:
                    group(g)

            mlp_loads(M1, w_fc1, w_fc2)

            for i, (kind, c0) in enumerate(Z_TILES):
                w = Z0 + i
                sp.wait_ge(s_w, w - 1)
                dst = k_n(RAW[w % 2], KC, P)
                if kind == "akik":
                    pieces = [(0, AK, 64), (64, IK, 64)]
                elif kind == "avkr":
                    pieces = [(0, AV, 64), (64, KR, 32), (96, KR + 16, 16), (112, KR, 16)]
                else:
                    pieces = [(0, c0, P)]
                for to, c, n in pieces:
                    sp.dma_start(dst[:, :, to:to + n], w_tile(w_in_2, 0, KC, c, n)).then_inc(s_raw[w % 2], 16)
                if i == 2:
                    sp.wait_ge(s_xr, 16)
                    sp.wait_ge(s_xn, 2 * KC)
                    sp.dma_start(xs, X[:, :]).then_inc(s_xs, 16)
                    sp.wait_ge(s_nlo, 3 * KC)
                    sp.dma_start(T2S[:, :].bitcast(I32), positions_2.partition_broadcast(P)).then_inc(s_pos2, 16)
                    q = WUQ[:, :].rearrange("p (k h n) -> p k h n", k=2, h=B_HEADS)
                    qd = w_uq_2.rearrange("(k p) (h n) -> p k h n", p=P, n=B_QK)
                    for k in range(2):
                        sp.dma_start(q[:, k, :, 0:B_QK], qd[:, k, :, :]).then_inc(s_wuq, 16)
                        sp.dma_start(q[:, k, :, 96:112], qd[:, k, :, 80:96]).then_inc(s_wuq, 16)
                        sp.dma_start(q[:, k, :, 112:128], qd[:, k, :, 64:80]).then_inc(s_wuq, 16)
                    kv = w_ukv_2.rearrange("p (h n) -> p h n", h=B_HEADS)
                    for e in range(2):
                        sp.dma_start(WUKV[:, e * HALF:(e + 1) * HALF].rearrange("p (h n) -> p h n", h=B_HEADS),
                                     kv[:, :, 64 * e:64 * (e + 1)]).then_inc(s_wuq, 16)

            def load_branch(m):
                w = BR0 + m
                sp.wait_ge(s_w, w - 1)
                src = w_branch_b_2 if m % 2 else w_branch_a_2
                sp.dma_start(k_n(RAW[w % 2], 4, 256), w_tile(src, 0, 4, 256 * (m // 2), 256)).then_inc(s_raw[w % 2], 16)

            load_branch(0)
            load_branch(1)
            sp.wait_ge(s_kr, 1)
            for h in range(1, B_HEADS):
                sp.dma_start(KM[64:96, h * S:(h + 1) * S], KM[64:96, 0:S]).then_inc(s_krd, 16)
            sp.wait_ge(s_mb, NB)
            sp.wait_ge(s_q, 8)
            sp.dma_start(POSB[:, :].bitcast(I32), positions_2.partition_broadcast(P)).then_inc(s_c4, 16)
            for dst, name in ((SEL, "sel"), (REACHED, "reach")):
                c, n = CONST_AT[name]
                sp.dma_start(dst[:, :], const[:, c:c + n]).then_inc(s_c4, 16)
            sp.wait_ge(s_pv, 128)
            for j in range(2):
                sp.wait_ge(s_gs[j], 128)

            def load_gates(m):
                if m >= 4:
                    sp.wait_ge(s_evv, GATED0 + m - 3)
                t = 8 * (m % 2) + 2 * (m // 2)
                sp.dma_start(GB[m % 4][:, :].rearrange("p (t s) -> p t s", t=2),
                             gs[t:t + 2].rearrange("t p s -> p t s")).then_inc(s_g[m % 4], 16)

            for m in range(8):
                load_gates(m)
                if m >= 2:
                    load_branch(m)
            for i in range(8):
                w = OUT0 + i
                if i == 2:
                    sp.wait_ge(s_lo, Z_LO + KC)
                    sp.wait_ge(s_xs, 32)
                    sp.dma_start(X[:, :], xs).then_inc(s_xr, 16)
                sp.wait_ge(s_w, w - 1)
                sp.dma_start(k_n(RAW[w % 2], KC, P), w_tile(w_out_2, 0, KC, i * P, P)).then_inc(s_raw[w % 2], 16)
            mlp_loads(M2, w_ff1_2, w_ff2_2)
            for t in range(NB):
                sp.wait_ge(s_fo[t % 2], t // 2 + 1)
                sp.dma_start(out[t * P:(t + 1) * P, :], OT[t % 4][:, :]).then_inc(s_out[t % 4], 16)
            for j in range(4):
                sp.wait_ge(s_out[j], 16 * NB // 4)

        @block.gpsimd
        def _(pool):
            def split(j, w, loads, n=1024, free=True):
                pool.wait_ge(s_raw[j], 16 * loads)
                if free:
                    pool.wait_ge(s_mm, w - 1)
                nc.gpsimd.tensor_add(WHI[j][:, 0:n], RAW[j][:, 0:n], ZERO[:, 0:1].to_broadcast([P, n])).then_inc(s_whi, 1)
                pool.wait_ge(s_whi, w + 1)
                nc.gpsimd.tensor_sub(WLO[j][:, 0:n], RAW[j][:, 0:n], WHI[j][:, 0:n].bitcast(F32)).then_inc(s_w, 1)

            nc.gpsimd.memset(ZERO[:, :], 0.0).then_inc(s_zero, 1)
            pool.wait_ge(s_zero, 1)

            def add_squares(first):
                for k in range(KC):
                    n = first + k
                    pool.wait_ge(s_sq, n + 1)
                    if n:
                        pool.wait_ge(*added(n - 1))
                    buf = sq_buffer(n)[:, :]
                    other = ZERO[:, 0:1].to_broadcast([P, S]) if k == 0 else ACC[:, :]
                    nc.gpsimd.tensor_add(ACC[:, :], buf, other).then_inc(s_acc[1], 1)

            def halves_added(u, first):
                for e in range(2):
                    for k in range(KC):
                        n = first + k
                        pool.wait_ge(*((a_sq, KC * u + k + 1) if e == 0 else (s_sq, n + 1)))
                        if e == 1 or k == 0:
                            pool.wait_ge(*added(n - 1))
                        if e == 0 and KC * u + k:
                            pool.wait_ge(a_acc, KC * u + k)
                        other = ZERO[:, 0:1].to_broadcast([P, HALF]) if k == 0 else half(ACC, 0, e)
                        nc.gpsimd.tensor_add(half(ACC, 0, e), half(SQ[k % 2], 0, e), other
                                             ).then_inc(a_acc if e == 0 else s_acc[1], 1)

            def halves_low(v, first):
                for e in range(2):
                    for k in range(KC):
                        pool.wait_ge(*((a_hi, KC * v + k + 1) if e == 0 else (s_hi, first + k + 1)))
                        nc.gpsimd.tensor_sub(half(L, k, e), half(SQ[k % 2], 0, e), half(H, k, e).bitcast(F32)
                                             ).then_inc(a_nlo if e == 0 else s_nlo, 1)

            for w in range(W_OUT0 + 8):
                if w == 0:
                    add_squares(0)
                split(w % 2, w, w // 2 + 1, free=w >= 2)
                if w == 1:
                    halves_low(0, 0)

            def mlp_splits(m, before):

                def group(g, first):
                    for i in range(8):
                        split(i % 2, 8 * g + (m.w + i), 4 * g + loads(m.w + i))
                        if first and i == 1 and before is not None:
                            before()

                group(0, True)
                with pool.Fori(1, GROUPS) as g:
                    group(g, False)

            def before_mlp():
                halves_added(0, 2 * KC)
                halves_low(1, M1.hi - KC)

            mlp_splits(M1, before_mlp)

            for i in range(len(Z_TILES)):
                w = Z0 + i
                split(w % 2, w, loads(w))
                if i == 1:
                    halves_added(1, 4 * KC)
                    halves_low(2, M1.hi + 4 * GROUPS)
                if i == 5:
                    for b in range(2, NB):
                        pool.wait_ge(s_idx, IDX_HEADS * (b - 1))
                        a = SCORE_AT[b] + P * b
                        nc.gpsimd.affine_select(out=SCO[:, a:a + P], in_=SCO[:, a:a + P], compare_op=ALU.is_ge,
                                                fill=HIDDEN, base=0, pattern=[[-1, P]],
                                                channel_multiplier=1).then_inc(s_diag, 1)
            for w in range(BR0, MLP2):
                split(w % 2, w, loads(w))
                if w == BR0 + 1:
                    pool.wait_ge(s_tpd, 1)
                    for c in range(4):
                        hi = chunk(AQH, c)
                        nc.gpsimd.tensor_add(hi, chunk(AQP, c), ZERO[:, 0:1].to_broadcast([P, S])).then_inc(s_aqh, 1)
                    pool.wait_ge(s_aqh, 4)
                    for tiles, i0, i1, moved in ((48, 0, 48, s_aq), (64, 48, 64, s_aq2)):
                        pool.wait_ge(s_lg, tiles)
                        piece = lambda t, e: t[64 * e:64 * e + 64, :].rearrange("p (i n) -> p i n", n=64)[:, i0:i1]
                        to = QS[:, :].rearrange("p (i e n) -> p i e n", e=2, n=64)[:, i0:i1]
                        for e in range(2):
                            nc.gpsimd.tensor_sub(to[64:P, :, e, :], piece(AQP, e), piece(AQH, e).bitcast(F32)).then_inc(moved, 1)
                        for e in range(2):
                            zero = ZERO[64 * e:64 * e + 64, 0:1].rearrange("p (o n) -> p o n", o=1)
                            zero = zero.broadcast_to([64, i1 - i0, 64])
                            nc.gpsimd.tensor_add(to[0:64, :, e, :], piece(AQH, e).bitcast(F32), zero).then_inc(moved, 1)
            mlp_splits(M2, None)

        @block.tensor
        def _(pe):
            mm = nc.tensor.matmul

            def transpose(dst, src, n=P):
                return nc.tensor.transpose(dst, src, ident[0:n, 0:n])

            def product(w, first_of=None):
                pe.wait_ge(s_w, w + 1)
                if w >= 2:
                    pe.wait_ge(*reads(w - 2))
                hi, lo = k_n(WHI[w % 2], KC, P), k_n(WLO[w % 2], KC, P)
                b = w_bank(w)
                for k in range(KC):
                    if first_of is not None:
                        pe.wait_ge(first_of[0], first_of[1] + k + 1)
                    for n, (wt, a) in enumerate(((hi, H), (hi, L), (lo, H))):
                        for t in range(2):
                            last = mm(bank(b + t), wt[:, k, :], a[:, k * S + t * HALF:k * S + (t + 1) * HALF],
                                      start=(k == 0 and n == 0), stop=(k == KC - 1 and n == 2))
                last.then_inc(s_mm, 1)

            def sums(r, acc, b):
                for t in range(NB):
                    last = mm(bank(b)[:, t:t + 1], acc[:, t * P:(t + 1) * P], ones, start=True, stop=True)
                last.then_inc(s_ss, 1)

            def spread(r, b):
                pe.wait_ge(s_rs, r + 1)
                for t in range(NB):
                    last = mm(bank(b, 2)[:, t * P:(t + 1) * P], RS[:, t:t + 1].to_broadcast([P, P]), ident,
                              start=True, stop=True)
                last.then_inc(s_bc, 1)

            pe.wait_ge(s_const, 80)
            transpose(bank(7)[:, 0:NVA], STG[0:NVA, 0:P], NVA)
            transpose(bank(7)[:, NVA:NVA + NVB], STG[0:NVB, P:2 * P], NVB).then_inc(s_vt, 1)
            pe.wait_ge(s_tab, 32)
            mm(bank(6)[:, 0:8], REP[0:BUCKETS, :], TAB[0:BUCKETS, :], start=True, stop=True).then_inc(s_tp, 1)
            for k in range(KC):
                if k % 4 == 0:
                    pe.wait_ge(s_x[k // 4], 16)
                if k >= 2:
                    pe.wait_ge(s_sq, k - 1)
                for t in range(NB):
                    last = transpose(bank(2 * (k % 2), 2)[:, t * P:(t + 1) * P], XT[:, t * D + k * P:t * D + (k + 1) * P])
                last.then_inc(s_xt, 1)
            pe.wait_ge(*added(KC - 1))
            pe.wait_ge(s_vec, 1)
            sums(0, ACC, 7)

            def ada(g):
                pe.wait_ge(s_msum, KC * (g + 1))
                for i in range(8):
                    last = mm(bank(6)[:, 8 * g + i:8 * g + i + 1], MSUM[g if g < 2 else 2 + g % 2][:, i * P:(i + 1) * P],
                              ones, start=True, stop=True)
                last.then_inc(s_ada, 1)

            spread(0, 2)
            ada(0)
            ada(1)

            def ret_a(h):
                pe.wait_ge(*reads(12 + 4 * h + 2))
                if h:
                    pe.wait_ge(s_r_og, h)
                for t in range(NB):
                    last = transpose(bank(2, 2)[:, t * P:(t + 1) * P], R_VT[:, t * P:(t + 1) * P])
                last.then_inc(s_r_vT, 1)
                pe.wait_ge(s_r_k, h + 1)
                if h:
                    pe.wait_ge(s_ret_y, h)
                else:
                    pe.wait_ge(s_mod, 1)
                for t in range(NB):
                    last = transpose(bank(6, 2)[:, t * P:(t + 1) * P], R_KR[:, t * P:(t + 1) * P])
                last.then_inc(s_r_kT, 1)
                pe.wait_ge(s_r_q, h + 1)
                pe.wait_ge(s_r_vtok, h + 1)
                for t in range(NB):
                    last = mm(bank(2, 2)[:, t * P:(t + 1) * P], R_KR[:, t * P:(t + 1) * P],
                              R_QR[:, t * P:(t + 1) * P], start=True, stop=True)
                last.then_inc(s_r_sc, 1)
                pe.wait_ge(s_r_ktok, h + 1)
                for t in range(NB - 1):
                    last = mm(bank(6, 2)[:, t * P:(t + 1) * P], R_KTOK[:, t * P:(t + 1) * P],
                              R_VTOK[:, t * P:(t + 1) * P], start=True, stop=True)
                last.then_inc(s_r_kv, 1)

            def ret_b(h):
                pe.wait_ge(s_r_sd, h + 1)
                pe.wait_ge(s_r_st, h + 1)
                pe.wait_ge(s_r_qd, h + 1)
                for t in range(NB):
                    o = bank(2, 2)[:, t * P:(t + 1) * P]
                    last = mm(o, R_VTOK[:, t * P:(t + 1) * P], R_SD[:, t * P:(t + 1) * P],
                              start=True, stop=(t == 0))
                    if t:
                        last = mm(o, R_ST[:, (t - 1) * P:t * P], R_QD[:, t * P:(t + 1) * P],
                                  start=False, stop=True)
                last.then_inc(s_r_o, 1)

            def ret_c(h):
                pe.wait_ge(s_r_sq, h + 1)
                sums(1 + h, R_SQ, 6)

            def first_pair(v, w, nlo):
                for e in range(2):
                    for j in range(2):
                        if e == 0:
                            pe.wait_ge(s_w, w + j + 1)
                        hi, lo = k_n(WHI[j], KC, P), k_n(WLO[j], KC, P)
                        for k in range(KC):
                            if j == 0:
                                pe.wait_ge(*((a_nlo, KC * v + k + 1) if e == 0 else (s_nlo, nlo + k + 1)))
                            for n, (wt, a) in enumerate(((hi, H), (hi, L), (lo, H))):
                                last = mm(bank(4 * j + e), wt[:, k, :], half(a, k, e),
                                          start=(k == 0 and n == 0), stop=(k == KC - 1 and n == 2))
                        if e == 1:
                            last.then_inc(s_mm, 1)

            for w, (kind, h, _) in enumerate(W_IN):
                if w == 0:
                    first_pair(0, 0, 0)
                elif w >= 2:
                    product(w)
                if w in ADA_SUMMED_AFTER:
                    ada(ADA_SUMMED_AFTER[w])
                if kind == "q" and h:
                    ret_b(h - 1)
                if kind == "k" and h:
                    ret_c(h - 1)
                if kind == "v" and h:
                    spread(h, 6)
                if kind == "g":
                    ret_a(h)
            ret_b(RET_HEADS - 1)
            ret_c(RET_HEADS - 1)
            spread(RET_HEADS, 6)
            for i in range(8):
                product(W_OUT0 + i, (s_lo, 0) if i == 0 else None)

            def norm_products(r, squares):
                pe.wait_ge(*added(squares - 1))
                sums(r, ACC, 6)
                spread(r, 2)

            def halves_norm(u, r, squares):
                for e in range(2):
                    pe.wait_ge(*((a_acc, KC * (u + 1)) if e == 0 else added(squares - 1)))
                    for t in range(4 * e, 4 * e + 4):
                        last = mm(bank(e)[:, t:t + 1], ACC[:, t * P:(t + 1) * P], ones, start=True, stop=True)
                    last.then_inc(a_ss if e == 0 else s_ss, 1)
                    pe.wait_ge(*((a_rs, u + 1) if e == 0 else (s_rs, r + 1)))
                    for t in range(4 * e, 4 * e + 4):
                        last = mm(bank(6, 2)[:, t * P:(t + 1) * P], RS[:, t:t + 1].to_broadcast([P, P]), ident,
                                  start=True, stop=True)
                    last.then_inc(a_bc if e == 0 else s_bc, 1)

            def mlp_products(m, acts, hidden, first_of, between=None):
                (act_hi, act_lo), (hid_hi, hid_lo) = acts, hidden
                pe.wait_ge(s_eva, m.act)
                pe.wait_ge(s_evv, m.dve)

                def group(g, first):
                    pair = first and first_of is None
                    if pair:
                        first_pair(1, m.w, m.nlo - KC)
                    for i in range(2 if pair else 0, 8):
                        w = 8 * g + (m.w + i)
                        pe.wait_ge(s_w, w + 1)
                        if i < 2:
                            if not first:
                                pe.wait_ge(s_evv, 4 * g + (m.dve + i - 1))
                        elif i < 6:
                            pe.wait_ge(s_eva, 4 * g + (m.act + i - 1))
                        else:
                            pe.wait_ge(s_evv, 4 * g + (m.dve + i - 5))
                        b = 4 * (i % 2)
                        if i < 4:
                            hi, lo = k_n(WHI[i % 2], KC, P), k_n(WLO[i % 2], KC, P)
                            for k in range(KC):
                                if first and i == 0:
                                    pe.wait_ge(first_of[0], first_of[1] + k + 1)
                                for n, (wt, a) in enumerate(((hi, act_hi), (hi, act_lo), (lo, act_hi))):
                                    for t in range(2):
                                        last = mm(bank(b + t), wt[:, k, :], a[:, k * S + t * HALF:k * S + (t + 1) * HALF],
                                                  start=(k == 0 and n == 0), stop=(k == KC - 1 and n == 2))
                        else:
                            hi, lo = k_n(WHI[i % 2], 4, 256), k_n(WLO[i % 2], 4, 256)
                            for k in range(4):
                                if i == 4:
                                    pe.wait_ge(s_lo, 4 * g + (m.lo + k + 1))
                                for c in range(2):
                                    for n, (wt, a) in enumerate(((hi, hid_hi), (hi, hid_lo), (lo, hid_hi))):
                                        for t in range(2):
                                            last = mm(bank(b + 2 * c + t), wt[:, k, c * P:(c + 1) * P],
                                                      a[:, k * S + t * HALF:k * S + (t + 1) * HALF],
                                                      start=(k == 0 and n == 0), stop=(k == 3 and n == 2))
                        last.then_inc(s_mm, 1)
                        if first and between is not None and i in between:
                            between[i]()

                group(0, True)
                with pe.Fori(1, GROUPS) as g:
                    group(g, False)

            norm_products(5, 2 * KC)
            halves_norm(0, 6, 3 * KC)
            mlp_products(M1, (H, L), (FH, FL), None)
            norm_products(7, 4 * KC)
            halves_norm(1, 8, 5 * KC)

            def index_scores():
                pe.wait_ge(*reads(Z0 + 3))
                for t in range(NB):
                    last = transpose(bank(7)[:, 4 * t:4 * t + 4], IWT[0:4, t * P:(t + 1) * P], 4)
                last.then_inc(s_iwt, 1)
                m = 0
                for b in range(2, NB):
                    w = P * (b + 1)
                    for h in range(IDX_HEADS):
                        if m >= 2:
                            pe.wait_ge(s_rel, m - 1)
                        if m == 1:
                            pe.wait_ge(s_iw, 1)
                        rows = slice(64 * (h % 2), 64 * (h % 2) + 64)
                        q0 = (h // 2) * S + b * P
                        for c in range(0, w, HALF):
                            n = min(HALF, w - c)
                            last = mm(bank(2 + 4 * (m % 2), 2)[:, c:c + n], IQB[rows, q0:q0 + P], IKB[rows, c:c + n],
                                      start=True, stop=True)
                        last.then_inc(s_ixp, 1)
                        m += 1

            for i in range(len(Z_TILES)):
                if i == 0:
                    first_pair(2, Z0, 2 * KC)
                elif i >= 2:
                    product(Z0 + i)
                if i == 3:
                    index_scores()
                if i == LATENT_SUMS:
                    for n in range(2):
                        pe.wait_ge(s_lacc, n + 1)
                        for t in range(NB):
                            last = mm(bank(6 + n)[:, t:t + 1], (RT[0] if n == 0 else IWT)[:, t * P:(t + 1) * P], ones,
                                      start=True, stop=True)
                        last.then_inc(s_ss, 1)
                if i == LATENT_SUMS + 2:
                    spread(9, 2)
                if i == LATENT_SUMS + 4:
                    spread(10, 6)

            pe.wait_ge(s_wuq, 8 * 16)
            pe.wait_ge(s_eva, M2.act)
            for u in range(UPS):
                if u == 0:
                    pe.wait_ge(s_lat, 3)
                if u >= 4:
                    pe.wait_ge(s_upa, u - 3)
                    pe.wait_ge(s_upd, min(u - 3, 8))
                b = bank(2 * (u % 4), 2)
                if u < 8:
                    for k in range(2):
                        wt = WUQ[:, k * S + u * P:k * S + (u + 1) * P]
                        for t in range(2):
                            last = mm(b[:, t * HALF:(t + 1) * HALF], wt, CQB[:, k * S + t * HALF:k * S + (t + 1) * HALF],
                                      start=(k == 0), stop=(k == 1))
                elif u < 12:
                    wt = WUKV[:, P * (u - 8):P * (u - 7)]
                    for t in range(2):
                        last = mm(b[:, t * HALF:(t + 1) * HALF], wt, CKVB[:, t * HALF:(t + 1) * HALF], start=True, stop=True)
                elif u < 16:
                    wt = WUKV[:, HALF:]
                    for t in range(2):
                        tok = (2 * (u - 12) + t) * P
                        last = mm(b[:, t * HALF:(t + 1) * HALF], CKVB[:, tok:tok + P], wt, start=True, stop=True)
                else:
                    for t in range(NB):
                        last = transpose(b[:, t * A_DIM:(t + 1) * A_DIM], AVKR[0:64, t * P:(t + 1) * P], 64)
                last.then_inc(s_up, 1)

            def logits(n):
                b = ATT[n][0]
                w = P * (b + 1)
                dst = bank(2 * (n % 2), 2)
                if n >= 2:
                    pe.wait_ge(s_exp, n - 1)
                if n < 64:
                    h = ATT[n][1]
                    for c in range(0, w, HALF):
                        cw = min(HALF, w - c)
                        end = c + cw == w
                        last = mm(dst[:, c:c + cw], QM[0:B_QK, h * S + b * P:h * S + (b + 1) * P],
                                  KM[0:B_QK, h * S + c:h * S + c + cw], start=True, stop=not end)
                        if end:
                            last = mm(dst[:, w - P:w], IDB[:, :], TRB[:, :], start=False, stop=True)
                else:
                    i = n - 64
                    pe.wait_ge(s_step, NSTEP * (i + 1))
                    if i == 0:
                        pe.wait_ge(s_tpd, 1)
                        pe.wait_ge(s_kparts, 3)
                        pe.wait_ge(s_aq, 4)
                    if i == 48:
                        pe.wait_ge(s_aq2, 4)
                    at = slice(i * P, (i + 1) * P)
                    for c in range(0, w, HALF):
                        cw = min(HALF, w - c)
                        mm(dst[:, c:c + cw], QS[:, at], KHH[:, c:c + cw], start=True, stop=False)
                        mm(dst[:, c:c + cw], QS[0:64, at], KLO[0:64, c:c + cw], start=False, stop=False)
                        mm(dst[:, c:c + cw], SELB[:, (i % NB) * P:(i % NB + 1) * P],
                           MB[:, MASK_AT[b] + c:MASK_AT[b] + c + cw], start=False, stop=False)
                        for g in range(NSTEP):
                            for part in (DHI, DLO):
                                last = mm(dst[:, c:c + cw], part[:, g * P:(g + 1) * P],
                                          STEP[i % 2][:, g * S + c:g * S + c + cw], start=False,
                                          stop=(g == NSTEP - 1 and part is DLO))
                last.then_inc(s_lg, 1)

            def probs_t(n):
                pe.wait_ge(s_exp, n + 1)
                if n:
                    pe.wait_ge(s_pte, n)
                backs = sum(m <= n - 3 for m in BACK)
                if backs:
                    pe.wait_ge(s_bte, backs)
                for t in range(ATT[n][0] + 1):
                    last = transpose(bank(4, 2)[:, t * P:(t + 1) * P], PB[n % 2][:, t * P:(t + 1) * P])
                last.then_inc(s_pt, 1)

            def attend(n):
                b = ATT[n][0]
                pe.wait_ge(s_pte, n + 1)
                if n >= 2:
                    pe.wait_ge(s_oe, n - 1)
                for t in range(b + 1):
                    if n < 64:
                        v = VM[:, t * HALF + ATT[n][1] * B_V:t * HALF + (ATT[n][1] + 1) * B_V]
                    else:
                        v = VA[:, t * A_DIM:(t + 1) * A_DIM]
                    last = mm(bank(6 + n % 2)[:, 0:64], PTS[n % 2][:, t * P:(t + 1) * P], v,
                              start=(t == 0), stop=(t == b))
                last.then_inc(s_pv, 1)

            def back(j):
                last_tile = 16 * j + 15 if j < 4 else 64 + 8 * (j - 4) + 7
                pe.wait_ge(s_oe, last_tile + 1)
                pe.wait_ge(s_pte, min(last_tile + 3, 128))
                for t in range(NB):
                    if j < 4:
                        last = transpose(bank(4, 2)[:, t * P:(t + 1) * P], OB[:, t * P:(t + 1) * P])
                    else:
                        last = transpose(bank(4, 2)[0:64, t * P:(t + 1) * P], OB[:, t * 64:(t + 1) * 64])
                last.then_inc(s_bt, 1)

            pe.wait_ge(s_upa, UPS)
            pe.wait_ge(s_upd, 8)
            pe.wait_ge(s_q, 8)
            pe.wait_ge(s_krd, 7 * 16)
            logits(0)
            for n in range(128 + 3):
                if n + 1 < 128:
                    logits(n + 1)
                if n - 3 in BACK:
                    back(BACK[n - 3])
                if 0 <= n - 2 < 128:
                    attend(n - 2)
                if n < 128:
                    probs_t(n)

            def wide(w, a0, first_of):
                pe.wait_ge(s_w, w + 1)
                pe.wait_ge(*reads(w - 2))
                hi, lo = k_n(WHI[w % 2], 4, 256), k_n(WLO[w % 2], 4, 256)
                for k in range(4):
                    if first_of is not None:
                        pe.wait_ge(s_lo, first_of + k + 1)
                    for c in range(2):
                        for n, (wt, a) in enumerate(((hi, H), (hi, L), (lo, H))):
                            for t in range(2):
                                last = mm(bank(w_bank(w) + 2 * c + t), wt[:, k, c * P:(c + 1) * P],
                                          a[:, (a0 + k) * S + t * HALF:(a0 + k) * S + (t + 1) * HALF],
                                          start=(k == 0 and n == 0), stop=(k == 3 and n == 2))
                last.then_inc(s_mm, 1)

            pe.wait_ge(s_bte, 12)
            pe.wait_ge(s_oe, 128)
            for m in range(8):
                wide(BR0 + m, 4 * (m % 2), Z_LO + 4 * (m % 2) if m < 2 else None)
            for i in range(8):
                product(OUT0 + i, (s_lo, Z_LO + KC) if i == 0 else None)
            def root_sums():
                pe.wait_ge(*added(6 * KC - 1))
                sums(11, ACC, 6)

            def root_spread():
                spread(11, 2)
                pe.wait_ge(s_rs2, 1)

            mlp_products(M2, (A2H, A2L), (F2H, F2L), (s_lo, M2.lo - KC), {1: root_sums, 3: root_spread})

            def final_t(t):
                if t >= 4:
                    pe.wait_ge(s_fo[t % 2], t // 2 - 1)
                for k in range(KC):
                    last = transpose(bank(2 * ((t + 3) % 4), 2)[:, k * P:(k + 1) * P], XG[:, k * S + t * P:k * S + (t + 1) * P])
                last.then_inc(s_ft, 1)

            pe.wait_ge(s_evv, reads(MLP2 - 1)[1] + 4 * GROUPS)
            pe.wait_ge(s_fin, KC)
            for t in range(NB):
                if t == 3:
                    pe.wait_ge(*added(7 * KC - 1))
                    sums(12, ACC, 4)
                    pe.wait_ge(s_std, 13)
                final_t(t)

        @block.scalar
        def _(act):
            A = nc.scalar.activation

            def copy_out(w, dst, fn=ACT.Copy, **kw):
                act.wait_ge(s_mm, w + 1)
                return A(dst, bank(w_bank(w), 2), fn, **kw).then_inc(s_eva, 1)

            def root(r, b, n=D):
                act.wait_ge(s_ss, r + 1)
                if r:
                    act.wait_ge(s_rs, r)
                A(SS[:, :], bank(b)[:, 0:NB], ACT.Sqrt, bias=eps, scale=1.0 / n).then_inc(s_std, 1)

            act.wait_ge(s_vt, 1)
            A(VEC[:, 0:NVA + NVB], bank(7)[:, 0:NVA + NVB], ACT.Copy).then_inc(s_vec, 1)
            act.wait_ge(s_vec, 1)
            A(SILC[:, :], VEC[:, 0:8], ACT.Silu).then_inc(s_silc, 1)
            for k in range(KC):
                act.wait_ge(s_xt, k + 1)
                A(chunk(X, k), bank(2 * (k % 2), 2), ACT.Copy).then_inc(s_xc, 1)
                if k >= 2:
                    act.wait_ge(*added(k - 2))
                A(SQ[k % 2][:, :], bank(2 * (k % 2), 2), ACT.Square).then_inc(s_sq, 1)
            act.wait_ge(s_red, 1)
            A(ROT_S[:, :], CT[:, :], ACT.Sin, scale=sgn1).then_inc(s_sin, 1)
            A(ROT_C[:, :], CT[:, :], ACT.Sin, scale=0.5).then_inc(s_sin, 1)
            root(0, 7)

            def high_halves(v, first, between=None):
                for e in range(2):
                    for k in range(KC):
                        act.wait_ge(*((a_h32, KC * v + k + 1) if e == 0 else (s_h32, first + k + 1)))
                        A(half(H, k, e), half(SQ[k % 2], 0, e), ACT.Copy).then_inc(a_hi if e == 0 else s_hi, 1)
                        if e == 0 and k == 3 and between is not None:
                            between()

            high_halves(0, 0)
            for w, (kind, h, _) in enumerate(W_IN):
                if kind == "xin":
                    if h:
                        act.wait_ge(*reads(w - 2))
                    copy_out(w, CX[:, :])
                elif kind == "v":
                    copy_out(w, R_VT[:, :])
                elif kind == "g":
                    if h:
                        act.wait_ge(s_r_og, h)
                    copy_out(w, R_G[:, :], ACT.Silu)
                    act.wait_ge(s_r_vT, h + 1)
                    A(R_VTOK[:, :], bank(2, 2), ACT.Copy).then_inc(s_r_vtok, 1)
                    act.wait_ge(s_r_kT, h + 1)
                    act.wait_ge(s_dec, 16)
                    A(R_KTOK[:, :], bank(6, 2), ACT.Copy, scale=DEC[:, 1024 + h:1025 + h]).then_inc(s_r_ktok, 1)
                    if h == RET_HEADS - 1:
                        act.wait_ge(s_mm, W_OUT0)
                        for k in range(4):
                            A(chunk(H, k), chunk(Y, k), ACT.Copy).then_inc(s_hi, 1)
                    act.wait_ge(s_r_o, h + 1)
                    A(R_SQ[:, :], bank(2, 2), ACT.Square).then_inc(s_r_sq, 1)
                    act.wait_ge(s_ss, 1 + h + 1)
                    A(SS[:, :], bank(6)[:, 0:NB], ACT.Sqrt, bias=eps, scale=1.0 / RET_DIM).then_inc(s_std, 1)
            for k in range(4, KC):
                if k == KC - 1:
                    act.wait_ge(s_ret_y, RET_HEADS)
                A(chunk(H, k), chunk(Y, k), ACT.Copy).then_inc(s_hi, 1)
            def square(n, src):
                act.wait_ge(*added(n - 2))
                A(sq_buffer(n)[:, :], src, ACT.Square).then_inc(s_sq, 1)

            for i in range(8):
                w = W_OUT0 + i
                if i == 0:
                    act.wait_ge(s_lo, KC)
                act.wait_ge(s_mm, w + 1)
                square(KC + i, bank(w_bank(w), 2))
                copy_out(w, chunk(Y, i))

            def halves(u, r, n, first_x, first):

                def squares(e, k):
                    act.wait_ge(*((a_xn, KC * u + k + 1) if e == 0 else (s_xn, first_x + k + 1)))
                    if k >= 2:
                        act.wait_ge(*((a_acc, KC * u + k - 1) if e == 0 else added(n + k - 2)))
                    A(half(SQ[k % 2], 0, e), half(X, k, e), ACT.Square).then_inc(a_sq if e == 0 else s_sq, 1)

                def half_root(e):
                    act.wait_ge(*((a_ss, u + 1) if e == 0 else (s_ss, r + 1)))
                    act.wait_ge(*((s_rs, r) if e == 0 else (a_rs, u + 1)))
                    at = slice(4 * e, 4 * e + 4)
                    A(SS[:, at], bank(e)[:, at], ACT.Sqrt, bias=eps, scale=1.0 / D).then_inc(a_std if e == 0 else s_std, 1)

                for k in range(KC):
                    squares(0, k)
                for k in range(KC):
                    squares(1, k)
                    if k == 3:
                        half_root(0)
                high_halves(u + 1, first, lambda: half_root(1))

            root(5, 6)
            halves(0, 6, 2 * KC, 0, KC)

            def mlp_act(m, hid_hi, between=None):

                def group(g, first):
                    for i in range(4):
                        act.wait_ge(s_mm, 8 * g + (m.w + i + 1))
                        if not (first and i < 2):
                            act.wait_ge(s_h32, 4 * g + (m.f32 + i - 1))
                        A(RL[i % 2][:, :], bank(4 * (i % 2), 2), ACT.Relu).then_inc(s_eva, 1)
                        act.wait_ge(s_eva, 4 * g + (m.act + i + 1))
                        A(chunk(hid_hi, i), RL[i % 2][:, :], ACT.Square).then_inc(s_hi, 1)
                        if first and between is not None and i in between:
                            between[i]()

                group(0, True)
                with act.Fori(1, GROUPS) as g:
                    group(g, False)

            mlp_act(M1, FH)
            for k in range(KC):
                act.wait_ge(s_evv, M1.dve + 4 * (GROUPS - 1) + k // 2 + 1)
                square(3 * KC + k, chunk(Y, k))
            root(7, 6)
            halves(1, 8, 4 * KC, KC, 2 * KC + 4 * GROUPS)

            def read_tile(w, pieces):
                act.wait_ge(s_mm, w + 1)
                for n, (dst, rows, kw) in enumerate(pieces):
                    src = bank(w_bank(w), 2, rows)
                    if "split" in kw:
                        src = src.rearrange("p (i q) -> p i q", q=kw.pop("split"))
                    ins = A(dst, src, kw.pop("fn", ACT.Copy), **kw)
                    ins.then_inc(s_eva if n == len(pieces) - 1 else s_act, 1)

            every = slice(0, P)
            top, low_rows = slice(0, 64), slice(64, P)
            act.wait_ge(s_xs, 32)
            for i, (kind, c0) in enumerate(Z_TILES):
                w = Z0 + i
                if kind == "iw":
                    read_tile(w, [(IWT[0:4, :], slice(0, 4), {})])
                elif kind == "iq":
                    read_tile(w, [(chunk(IQB, (c0 - IQ) // P), every, {})])
                elif kind == "akik":
                    read_tile(w, [(AKB[0:64, :], top, {}), (IKB[64:P, :], low_rows, {}), (IKB[0:64, :], low_rows, {})])
                    m = 0
                    for b in range(2, NB):
                        n = P * (b + 1)
                        for h in range(IDX_HEADS):
                            act.wait_ge(s_ixp, m + 1)
                            if m >= 2:
                                act.wait_ge(s_idx, m - 1)
                            A(RT[m % 2][:, 0:n], bank(2 + 4 * (m % 2), 2)[:, 0:n], ACT.Relu,
                              scale=float(A_DIM) ** -0.5).then_inc(s_rel, 1)
                            m += 1
                elif kind == "avkr":
                    read_tile(w, [(AVKR[:, :], every, {})])
                    act.wait_ge(s_red2, 1)
                    A(T2S[:, :], GST[0][:, :], ACT.Sin, scale=sgn2).then_inc(s_sin2, 1)
                    A(T2C[:, :], GST[0][:, :], ACT.Sin, scale=0.5).then_inc(s_sin2, 1)
                elif kind == "aq":
                    c = (c0 - AQ) // P
                    read_tile(w, [(AQP[:, :].rearrange("p (i c q) -> p c i q", c=4, q=QT)[:, c], every,
                                   {"scale": float(A_DIM) ** -0.5, "split": QT})])
                elif kind == "cq":
                    read_tile(w, [(chunk(CQB, (c0 - CQ) // P), every, {})])
                elif kind == "ckv":
                    read_tile(w, [(CKVB[:, :], every, {})])
                else:
                    g = i - Z_GATE
                    if g >= 2:
                        act.wait_ge(s_gs[g % 2], 16 * (g // 2))
                    else:
                        act.wait_ge(s_sin2, 3)
                    read_tile(w, [(GST[g % 2][:, :], every, {"fn": ACT.Sigmoid, "bias": vcol("b_gate_2", g)})])
                    act.wait_ge(*reads(w))
                    act.dma_start(gs[g], GST[g % 2][:, :]).then_inc(s_gs[g % 2], 16)
                    if i == LATENT_SUMS:
                        root(9, 6, 2 * P)
                        root(10, 7, P)
            for u in range(UPS):
                act.wait_ge(s_up, u + 1)
                b = bank(2 * (u % 4), 2)
                if u < 8:
                    A(chunk(QM, u, rows=top), b[0:64, :], ACT.Copy, scale=float(B_QK) ** -0.5).then_inc(s_upa, 1)
                elif u < 12:
                    k = 2 * (u - 8)
                    A(chunk(KM, k, rows=top), b[0:64, :], ACT.Copy).then_inc(s_act, 1)
                    A(chunk(KM, k + 1, rows=top), b[64:P, :], ACT.Copy).then_inc(s_upa, 1)
                elif u < 16:
                    if u == 15:
                        act.wait_ge(s_mb, NB)
                    A(chunk(VM, u - 12), b, ACT.Copy).then_inc(s_upa, 1)
                else:
                    A(VA[:, :], b[:, 0:HALF], ACT.Copy).then_inc(s_upa, 1)

            def probs_copied(n):
                act.wait_ge(s_pt, n + 1)
                if n >= 2:
                    act.wait_ge(s_pv, n - 1)
                if n < 2:
                    for j in range(2):
                        act.wait_ge(s_gs[j], 128)
                w = P * (ATT[n][0] + 1)
                A(PTS[n % 2][:, 0:w], bank(4, 2)[:, 0:w], ACT.Copy).then_inc(s_pte, 1)

            def back_copied(j):
                act.wait_ge(s_bt, j + 1)
                if j < 4:
                    A(chunk(YB, j), bank(4, 2), ACT.Copy).then_inc(s_bte, 1)
                else:
                    b = j - 4
                    if b == 0:
                        act.wait_ge(s_aq2, 4)
                    src = bank(4, 2)[0:64, :].rearrange("p (r e c q) -> p r e c q", r=NB, c=4, e=2)
                    for e in range(2):
                        dst = YA[64 * e:64 * e + 64, :].rearrange("p (c b r q) -> p b r c q", c=4, b=NB, r=NB)[:, b]
                        A(dst, src[:, :, e], ACT.Copy).then_inc(s_act if e == 0 else s_bte, 1)

            def scaled(n):
                act.wait_ge(s_pv, n + 1)
                act.wait_ge(s_ri, n + 1)
                at = ATT[n][0] * P + (n % 2) * 64 if n < 64 else (n % 8) * 64
                A(OB[:, at:at + 64], bank(6 + n % 2)[:, 0:64], ACT.Copy, scale=RINV[:, n % 4:n % 4 + 1]).then_inc(s_oe, 1)

            for n in range(128 + 4):
                if n < 128:
                    act.wait_ge(s_nm, n + 1)
                    if n >= 2:
                        act.wait_ge(s_pt, n - 1)
                    if n >= 4:
                        act.wait_ge(s_ri, n - 3)
                    w = P * (ATT[n][0] + 1)
                    A(PB[n % 2][:, 0:w], bank(2 * (n % 2), 2)[:, 0:w], ACT.Exp, bias=NMX[:, n % 2:n % 2 + 1],
                      accum_out=RSUM[:, n % 4:n % 4 + 1]).then_inc(s_exp, 1)
                if n - 4 in BACK:
                    back_copied(BACK[n - 4])
                if 0 <= n - 1 < 128:
                    probs_copied(n - 1)
                if 0 <= n - 3 < 128:
                    scaled(n - 3)
            act.wait_ge(s_bte, 12)
            for k in range(KC):
                A(chunk(H, k), chunk(YA, k) if k < 4 else chunk(YB, k - 4), ACT.Copy).then_inc(s_hi, 1)
            act.wait_ge(s_mm, OUT0)
            for k in range(KC):
                act.wait_ge(s_evv, reads(BR0 + 2 * (k // 2) + 1)[1])
                A(chunk(H, k), chunk(Y, k), ACT.Copy).then_inc(s_hi, 1)
            for i in range(8):
                act.wait_ge(*reads(OUT0 + i))
                square(5 * KC + i, chunk(X, i))
                A(chunk(A2H, i), chunk(X, i), ACT.Copy, scale=vcol("mlp_norm_g_2", i)).then_inc(s_hi, 1)
            act.wait_ge(*added(6 * KC - 1))

            def squared_roots():
                act.wait_ge(s_bc, 12)
                A(RS2[:, :], bank(2, 2), ACT.Square).then_inc(s_rs2, 1)

            mlp_act(M2, F2H, {1: lambda: root(11, 6), 3: squared_roots})
            for k in range(KC):
                act.wait_ge(s_x2, k // 2 + 1)
                square(6 * KC + k, chunk(X, k))
            root(12, 4)
            for t in range(0, NB, 2):
                act.wait_ge(s_ft, t + 1)
                act.wait_ge(s_rs, 13)
                if t >= 4:
                    act.wait_ge(s_out[t % 4], 16 * (t // 4))
                A(OT[t % 4][:, :], bank(2 * ((t + 3) % 4), 2), ACT.Copy, scale=RS[:, t:t + 1]).then_inc(s_fo[0], 1)


        @block.vector
        def _(dve):
            V = nc.vector
            own = [0]

            def link(ins):
                own[0] += 1
                ins.then_inc(s_dve, 1)
                dve.wait_ge(s_dve, own[0])

            def recip(r):
                dve.wait_ge(s_std, r + 1)
                V.reciprocal(RS[:, :], SS[:, :]).then_inc(s_rs, 1)

            def low(src, k, first):
                dve.wait_ge(s_hi, first + k + 1)
                V.tensor_sub(chunk(L, k), src, chunk(H, k).bitcast(F32)).then_inc(s_lo, 1)

            def reduce_angle(t, tmp, inv):
                link(V.tensor_scalar(t, t, inv, None, ALU.mult))
                link(V.tensor_scalar(tmp, t, 1.0 / (2 * np.pi), MAGIC, ALU.mult, ALU.add))
                link(V.tensor_scalar(tmp, tmp, MAGIC, None, ALU.subtract))
                for c in TWO_PI:
                    link(V.scalar_tensor_tensor(t, tmp, -c, t, ALU.mult, ALU.add))

            dve.wait_ge(s_tp, 1)
            link(V.tensor_copy(DLT[:, :], bank(6)[:, 0:8]))
            dve.wait_ge(s_rot, 16)
            link(V.tensor_copy(CT[:, :], ROT_S[:, :].bitcast(I32)))
            dve.wait_ge(s_const, 80)
            link(V.tensor_copy(IDB[:, :], ident))
            link(V.tensor_copy(TRB[:, :], STG[:, 2 * P:3 * P]))
            reduce_angle(CT[:, :], ROT_C[:, :], inv1)
            V.tensor_scalar(CT[:, :], CT[:, :], PI, -PI, ALU.min, ALU.max).then_inc(s_red, 1)

            def add_square(n):
                dve.wait_ge(s_sq, n + 1)
                dve.wait_ge(*added(n - 1))
                if n % KC == 0:
                    V.tensor_copy(ACC[:, :], sq_buffer(n)[:, :]).then_inc(s_acc[0], 1)
                else:
                    V.tensor_add(ACC[:, :], ACC[:, :], sq_buffer(n)[:, :]).then_inc(s_acc[0], 1)

            def weigh(n):
                g, k = n // KC, n % KC
                if n < ADA_EARLY:
                    dve.wait_ge(s_ada_first[n // 4], 16)
                    src = [ADA_H, ADA_H, ADA_L, WK][n // 4][:, (n % 8 if g == 0 else n % 4) * S:][:, 0:S]
                else:
                    dve.wait_ge(s_ada_in[n % 4], 16 * ((n - ADA_EARLY) // 4 + 1))
                    src = ADA[n % 4][:, :]
                if n:
                    dve.wait_ge(s_msum, n)
                to = MSUM[g if g < 2 else 2 + g % 2][:, :]
                if k == 0:
                    if g >= 4:
                        dve.wait_ge(s_ada, g - 1)
                    V.tensor_scalar(to, src, SILC[:, k:k + 1], None, ALU.mult).then_inc(s_msum, 1)
                else:
                    V.scalar_tensor_tensor(to, src, SILC[:, k:k + 1], to, ALU.mult, ALU.add).then_inc(s_msum, 1)

            dve.wait_ge(s_silc, 1)
            for n in range(ADA_EARLY):
                weigh(n)
                if n == 11:
                    recip(0)
            dve.wait_ge(s_sin, 2)
            link(V.scalar_tensor_tensor(CT[:, :], ROT_C[:, :], -2.0, ROT_C[:, :], ALU.mult, ALU.mult))
            link(V.tensor_scalar(ROT_C[:, :], CT[:, :], 1.0, None, ALU.add))
            link(V.memset(CU[:, 0:2], 0.0))

            def modulation(g):
                a = 8 * ADA_GROUPS[g]
                n = VCOL["b_ada"] + a
                link(V.tensor_tensor(MOD[:, 8 * g:8 * g + 8], bank(6)[:, 8 * g:8 * g + 8], VEC[:, n:n + 8], ALU.add))

            def gains(name):
                return VEC[:, VCOL[name]:VCOL[name] + 8]

            dve.wait_ge(s_vec, 1)
            dve.wait_ge(s_ada, 2)
            modulation(0)
            modulation(1)
            link(V.scalar_tensor_tensor(MODA[:, 0:8], MOD[:, 0:8], 1.0, gains("g_pre_mix"), ALU.add, ALU.mult))

            def norm_halves(v, ready, b, scale, shift, n32, first, i, between=None):
                for e in range(2):
                    scaled, high, low_part = ((a_h32, a_hi, a_nlo), (s_h32, s_hi, s_nlo))[e]
                    c32, chi, clo = (KC * v, KC * v, KC * v) if e == 0 else (n32, first, KC * i)
                    dve.wait_ge(*ready[e])
                    for k in range(KC):
                        if shift:
                            if k:
                                dve.wait_ge(scaled, c32 + k)
                            link(V.tensor_tensor(half(ACC, 0, e), half(X, k, e), bank(b + e), ALU.mult))
                        if k >= 2:
                            dve.wait_ge(high, chi + k - 1)
                            dve.wait_ge(low_part, clo + k - 1)
                        if shift:
                            V.tensor_scalar(half(SQ[k % 2], 0, e), half(ACC, 0, e), scale(k), shift(k), ALU.mult,
                                            ALU.add).then_inc(scaled, 1)
                        else:
                            V.scalar_tensor_tensor(half(SQ[k % 2], 0, e), half(X, k, e), scale(k), bank(b + e), ALU.mult,
                                                   ALU.mult).then_inc(scaled, 1)
                        if e == 0 and k == 5 and between is not None:
                            between()

            dve.wait_ge(s_xc, KC)
            norm_halves(0, ((s_bc, 1), (s_bc, 1)), 2, lambda k: MODA[:, k:k + 1], lambda k: MOD[:, 8 + k:9 + k], 0, 0, 0)

            def tap(j, i):
                return vcol("conv_w", 4 * i + j)

            def rotate(w, dst, scale, done):
                src = bank(w_bank(w), 2)
                dve.wait_ge(s_mm, w + 1)
                V.scalar_tensor_tensor(R_T[:, :], src, scale, ROT_C[:, :], ALU.mult, ALU.mult).then_inc(s_rt, 1)
                for lo in (0, 64):
                    hi = 64 - lo
                    ins = V.scalar_tensor_tensor(R_T2[lo:lo + 64, :], src[hi:hi + 64, :], scale,
                                                 ROT_S[hi:hi + 64, :], ALU.mult, ALU.mult)
                    ins.then_inc(s_rt if lo == 0 else s_evv, 1)
                dve.wait_ge(s_rt, 2 * rots[0] + 2)
                dve.wait_ge(*reads(w))
                rots[0] += 1
                V.tensor_add(dst[:, :], R_T[:, :], R_T2[:, :]).then_inc(done, 1)

            rots = [0]
            blocks3 = lambda t: t.rearrange("p (b n) -> p b n", b=NB)

            def repeated(t):
                return t.rearrange("p (o n) -> p o n", o=1).broadcast_to([P, NB, P])

            def ret_finish(h):
                dve.wait_ge(s_r_o, h + 1)
                dve.wait_ge(*reads(12 + 4 * h + 3))
                dve.wait_ge(s_r_sq, h + 1)
                V.tensor_tensor(R_OG[:, :], bank(2, 2), R_G[:, :], ALU.mult).then_inc(s_r_og, 1)
                recip(1 + h)

            def ret_out(h):
                dve.wait_ge(s_bc, h + 2)
                dve.wait_ge(s_r_og, h + 1)
                V.tensor_tensor(chunk(Y, CONV + h), R_OG[:, :], bank(6, 2), ALU.mult).then_inc(s_ret_y, 1)

            n_ada = ADA_EARLY
            for w, (kind, h, _) in enumerate(W_IN):
                if kind == "c":
                    dve.wait_ge(s_mm, w + 1)
                    dve.wait_ge(*reads(w - 1))
                    V.tensor_tensor(CU[:, 2:S + 2], bank(w_bank(w), 2), CX[:, :], ALU.mult).then_inc(s_evv, 1)
                    dve.wait_ge(*reads(w))
                    link(V.tensor_scalar(CT[:, :], CU[:, 0:S], tap(h, 0), None, ALU.mult))
                    for i in (1, 2):
                        link(V.scalar_tensor_tensor(CT[:, :], CU[:, i:i + S], tap(h, i), CT[:, :], ALU.mult, ALU.add))
                elif kind == "b":
                    dve.wait_ge(s_mm, w + 1)
                    V.tensor_tensor(chunk(Y, h), bank(w_bank(w), 2), CT[:, :], ALU.mult).then_inc(s_evv, 1)
                elif kind == "q":
                    rotate(w, R_QR, 1.0, s_r_q)
                    dve.wait_ge(s_r_q, h + 1)
                    dve.wait_ge(s_dec, 16)
                    if h:
                        dve.wait_ge(s_r_o, h)
                    V.tensor_tensor(blocks3(R_QD[:, :]), blocks3(R_QR[:, :]), repeated(DEC[:, 512 + h * P:512 + (h + 1) * P]),
                                    ALU.mult).then_inc(s_r_qd, 1)
                elif kind == "k":
                    rotate(w, R_KR, float(RET_DIM) ** -0.5, s_r_k)
                    if h:
                        ret_finish(h - 1)
                elif kind == "v":
                    if h:
                        ret_out(h - 1)
                elif kind == "g":
                    dve.wait_ge(s_r_sc, h + 1)
                    V.tensor_tensor(blocks3(R_SD[:, :]), blocks3(bank(2, 2)), repeated(DEC[:, h * P:(h + 1) * P]),
                                    ALU.mult).then_inc(s_r_sd, 1)
                    dve.wait_ge(s_r_kv, h + 1)
                    link(V.tensor_copy(R_ST[:, 0:P], bank(6)[:, 0:P]))
                    for t in range(1, NB - 1):
                        ins = V.scalar_tensor_tensor(R_ST[:, t * P:(t + 1) * P], R_ST[:, (t - 1) * P:t * P],
                                                     GAMMA_BLOCK[h], bank(6, 2)[:, t * P:(t + 1) * P], ALU.mult, ALU.add)
                        if t < NB - 2:
                            link(ins)
                    ins.then_inc(s_r_st, 1)
                for _ in range(ADA_PER_TILE):
                    if n_ada < ADA_STEPS:
                        weigh(n_ada)
                        n_ada += 1
                if kind == "k" and h == 0:
                    dve.wait_ge(s_ada, 6)
                    for g in range(2, 6):
                        modulation(g)
                    V.tensor_tensor(MODA[:, 8:16], MOD[:, 16:24], gains("g_post_mix"), ALU.mult)
                    V.scalar_tensor_tensor(MODA[:, 16:24], MOD[:, 32:40], 1.0, gains("g_pre_mlp"), ALU.add, ALU.mult)
                    V.tensor_tensor(MODA[:, 24:32], MOD[:, 40:48], gains("g_post_mlp"), ALU.mult).then_inc(s_mod, 1)
            h = RET_HEADS - 1
            for k in range(4):
                low(chunk(Y, k), k, KC)
            ret_finish(h)
            for k in range(4, KC - 1):
                low(chunk(Y, k), k, KC)
            ret_out(h)
            low(chunk(Y, KC - 1), KC - 1, KC)

            for k in range(KC):
                add_square(KC + k)

            def residual_and_norm(u, r, gain, first_x, scale, shift, n32, first, i):

                def half_recip(e):
                    dve.wait_ge(*((a_std, u + 1) if e == 0 else (s_std, r + 2)))
                    at = slice(4 * e, 4 * e + 4)
                    V.reciprocal(RS[:, at], SS[:, at]).then_inc(a_rs if e == 0 else s_rs, 1)

                recip(r)
                dve.wait_ge(s_bc, r + 1)
                for e in range(2):
                    normed, total = ((a_yn, a_xn), (s_yn, s_xn))[e]
                    n0 = KC * u if e == 0 else first_x
                    for k in range(KC + 1):
                        if k < KC:
                            if k >= 2:
                                dve.wait_ge(total, n0 + k - 1)
                            V.tensor_tensor(half([CT, FT][k % 2], 0, e), half(Y, k, e), bank(2 + e), ALU.mult).then_inc(normed, 1)
                        if k:
                            dve.wait_ge(normed, n0 + k)
                            x = half(X, k - 1, e)
                            V.scalar_tensor_tensor(x, half([CT, FT][(k - 1) % 2], 0, e), gain(k - 1), x,
                                                   ALU.mult, ALU.add).then_inc(total, 1)
                        if e == 1 and k == 5:
                            half_recip(0)
                norm_halves(u + 1, ((a_bc, u + 1), (s_bc, r + 2)), 6, scale, shift, n32, first, i, lambda: half_recip(1))

            dve.wait_ge(s_xr, 16)
            dve.wait_ge(s_mod, 1)
            residual_and_norm(0, 5, lambda k: MODA[:, 8 + k:9 + k], 0, lambda k: MODA[:, 16 + k:17 + k],
                              lambda k: MOD[:, 24 + k:25 + k], KC, 2 * KC, 1)

            def mlp_dve(m, acc, hid_hi, hid_lo, squares, between=None, at_last=None):

                def group(g, first, last):
                    for i in range(4):
                        dve.wait_ge(s_eva, 4 * g + (m.act + i + 1))
                        if not (first and i == 0):
                            dve.wait_ge(s_lo, 4 * g + (m.lo + i))
                        V.tensor_tensor(FT[:, :], RL[i % 2][:, :], RL[i % 2][:, :], ALU.mult).then_inc(s_h32, 1)
                        dve.wait_ge(s_h32, 4 * g + (m.f32 + i + 1))
                        dve.wait_ge(s_hi, 4 * g + (m.hi + i + 1))
                        V.tensor_sub(chunk(hid_lo, i), FT[:, :], chunk(hid_hi, i).bitcast(F32)).then_inc(s_lo, 1)
                        if first and between is not None and i in between:
                            between[i]()
                    for c in range(4):
                        dve.wait_ge(s_mm, 8 * g + (m.w + 4 + c + 1))
                        dst = chunk(acc, 2 * c, 2)
                        if first:
                            V.tensor_copy(dst, bank(4 * (c % 2), 4)).then_inc(s_evv, 1)
                        else:
                            dve.wait_ge(s_evv, 4 * g + (m.dve + c))
                            V.tensor_tensor(dst, dst, bank(4 * (c % 2), 4), ALU.add).then_inc(s_evv, 1)
                        if last:
                            if at_last is not None:
                                at_last(c)
                            for k in (2 * c - 1, 2 * c):
                                if k >= 0:
                                    add_square(squares + k)

                group(0, True, False)
                with dve.Fori(1, GROUPS - 1) as g:
                    group(g, False, False)
                group(GROUPS - 1, False, True)
                add_square(squares + KC - 1)

            mlp_dve(M1, Y, FH, FL, 3 * KC)
            residual_and_norm(1, 7, lambda k: MODA[:, 24 + k:25 + k], KC, lambda k: vcol("attn_norm_g_2", k), None,
                              2 * KC + 4 * GROUPS, M1.hi + 4 * GROUPS, 2)

            dve.wait_ge(s_pos2, 16)
            link(V.tensor_copy(GST[0][:, :], T2S[:, :].bitcast(I32)))
            reduce_angle(GST[0][:, :], GST[1][:, :], inv2)
            V.tensor_scalar(GST[0][:, :], GST[0][:, :], PI, -PI, ALU.min, ALU.max).then_inc(s_red2, 1)
            dve.wait_ge(s_iwt, 1)
            V.tensor_scalar(IWTOK[:, :], bank(7)[:, 0:32], float(IDX_HEADS) ** -0.5, None, ALU.mult).then_inc(s_iw, 1)
            dve.wait_ge(s_iw, 1)
            m = 0
            for b in range(2, NB):
                n = P * (b + 1)
                sc = SCO[:, SCORE_AT[b]:SCORE_AT[b] + n]
                for h in range(IDX_HEADS):
                    dve.wait_ge(s_rel, m + 1)
                    iw = IWTOK[:, 4 * b + h:4 * b + h + 1]
                    if h == 0:
                        V.tensor_scalar(sc, RT[m % 2][:, 0:n], iw, None, ALU.mult).then_inc(s_idx, 1)
                    else:
                        dve.wait_ge(s_idx, m)
                        V.scalar_tensor_tensor(sc, RT[m % 2][:, 0:n], iw, sc, ALU.mult, ALU.add).then_inc(s_idx, 1)
                    m += 1
            dve.wait_ge(s_sin2, 2)
            link(V.scalar_tensor_tensor(GST[1][:, :], T2C[:, :], -2.0, T2C[:, :], ALU.mult, ALU.mult))
            V.tensor_scalar(T2C[:, :], GST[1][:, :], 1.0, None, ALU.add).then_inc(s_sin2, 1)
            link(V.memset(MB[:, P:2 * P], 0.0))
            V.tensor_copy(MB[:, 0:P], TRB[:, :]).then_inc(s_mb, 1)
            V.tensor_copy(MB[:, 2 * P:3 * P], TRB[:, :]).then_inc(s_mb, 1)

            selecting = range(2, NB)
            every = slice(0, NB - 2)

            def scores(b):
                return SCO[:, SCORE_AT[b]:SCORE_AT[b] + P * (b + 1)]

            def mask(b):
                return MB[:, MASK_AT[b]:MASK_AT[b] + P * (b + 1)]

            def count(op):
                for b in selecting:
                    own[0] += 1
                    V.tensor_scalar(mask(b), scores(b), CAND[:, b - 2:b - 1].bitcast(F32), 0.0, op, ALU.add,
                                    accum_out=REACH[:, b - 2:b - 1]).then_inc(s_dve, 1)
                dve.wait_ge(s_dve, own[0])

            def latent_squares():
                dve.wait_ge(*reads(Z0 + Z_GATE - 1))
                link(V.tensor_mul(RT[0][:, :], chunk(CQB, 0), chunk(CQB, 0)))
                link(V.tensor_mul(RT[1][:, :], chunk(CQB, 1), chunk(CQB, 1)))
                V.tensor_add(RT[0][:, :], RT[0][:, :], RT[1][:, :]).then_inc(s_lacc, 1)
                V.tensor_mul(IWT[:, :], CKVB[:, :], CKVB[:, :]).then_inc(s_lacc, 1)

            def query_latents():
                dve.wait_ge(s_bc, 10)
                for k in range(2):
                    V.scalar_tensor_tensor(chunk(CQB, k), chunk(CQB, k), vcol("q_latent_norm_g_2", k), bank(2, 2), ALU.mult,
                                           ALU.mult).then_inc(s_lat, 1)

            def key_latents():
                dve.wait_ge(s_bc, 11)
                V.scalar_tensor_tensor(CKVB[:, :], CKVB[:, :], vcol("kv_latent_norm_g_2", 0), bank(6, 2), ALU.mult,
                                       ALU.mult).then_inc(s_lat, 1)

            dve.wait_ge(s_diag, NB - 2)
            link(V.memset(KEY[:, :], 0))
            link(V.memset(CAND[:, :], 0))
            count(ALU.is_ge)
            link(V.tensor_scalar(FLIP[:, every], REACH[:, every], TOPK - 0.5, -1.0, ALU.is_lt, ALU.mult))
            for bit in range(30, -1, -1):
                link(V.scalar_tensor_tensor(CAND[:, every], KEY[:, every], 1 << bit, FLIP[:, every], ALU.bitwise_or,
                                            ALU.bitwise_xor))
                count(ALU.is_ge)
                link(V.tensor_scalar(NEXT[:, every], REACH[:, every], TOPK - 0.5, float(1 << bit), ALU.is_ge, ALU.mult))
                link(V.tensor_tensor(KEY[:, every], KEY[:, every], NEXT[:, every], ALU.bitwise_or))
                if bit == 13:
                    latent_squares()
                if bit == 7:
                    recip(9)
                if bit == 4:
                    query_latents()
                    recip(10)
                if bit == 0:
                    key_latents()
            link(V.tensor_tensor(CAND[:, every], KEY[:, every], FLIP[:, every], ALU.bitwise_xor))
            count(ALU.is_gt)
            link(V.tensor_scalar(ROOM[:, every], REACH[:, every], -1.0, float(TOPK), ALU.mult, ALU.add))
            for b in selecting:
                n = P * (b + 1)
                least, room = CAND[:, b - 2:b - 1].bitcast(F32), ROOM[:, b - 2:b - 1]
                equal, chosen = RT[0][:, 0:n], RT[1][:, 0:n]
                link(V.tensor_scalar(equal, scores(b), least, None, ALU.is_equal))
                link(V.tensor_tensor_scan(chosen, ones.to_broadcast([P, n]), equal, 0.0, ALU.mult, ALU.add))
                link(V.scalar_tensor_tensor(chosen, chosen, room, equal, ALU.is_le, ALU.mult))
                link(V.scalar_tensor_tensor(chosen, scores(b), least, chosen, ALU.is_gt, ALU.add))
                V.tensor_scalar(mask(b), chosen, -1.0, -NEG, ALU.add, ALU.mult).then_inc(s_mb, 1)

            dve.wait_ge(s_mb, NB)
            dve.wait_ge(s_sin2, 3)
            V.tensor_mul(PB[0][64:96, :], AVKR[64:96, :], T2C[64:96, :]).then_inc(s_kt, 1)
            V.tensor_mul(PB[1][64:96, :], AVKR[96:P, :], T2S[96:P, :]).then_inc(s_kt, 1)
            dve.wait_ge(s_kt, 2)
            dve.wait_ge(s_mm, BR0)
            V.tensor_add(KM[64:96, 0:S], PB[0][64:96, :], PB[1][64:96, :]).then_inc(s_kr, 1)
            for h in range(B_HEADS):
                dve.wait_ge(s_up, h + 1)
                b = bank(2 * (h % 4), 2)
                dve.wait_ge(s_kr if h == 0 else s_q, 1 if h == 0 else h)
                scale = float(B_QK) ** -0.5
                V.scalar_tensor_tensor(PB[0][64:96, :], b[64:96, :], scale, T2C[64:96, :], ALU.mult, ALU.mult).then_inc(s_kt, 1)
                V.scalar_tensor_tensor(PB[1][64:96, :], b[96:P, :], scale, T2S[96:P, :], ALU.mult, ALU.mult).then_inc(s_upd, 1)
                dve.wait_ge(s_kt, 3 + h)
                dve.wait_ge(s_upd, h + 1)
                V.tensor_add(QM[64:96, h * S:(h + 1) * S], PB[0][64:96, :], PB[1][64:96, :]).then_inc(s_q, 1)

            def inverse_sum(n):
                dve.wait_ge(s_exp, n + 1)
                if n >= 4:
                    dve.wait_ge(s_oe, n - 3)
                V.reciprocal(RINV[:, n % 4:n % 4 + 1], RSUM[:, n % 4:n % 4 + 1]).then_inc(s_ri, 1)

            def steps_of(i):
                w = P * (i // NB + 1)
                if i == 1:
                    dve.wait_ge(s_aq2, 2)
                if i >= 2:
                    dve.wait_ge(s_lg, 64 + i - 1)
                for g in range(NSTEP):
                    V.tensor_scalar(STEP[i % 2][:, g * S:g * S + w], POSB[:, 0:w], THR[:, NSTEP * i + g:NSTEP * i + g + 1],
                                    None, ALU.is_le).then_inc(s_step, 1)

            TABLES_AT, KEYS_AT = 14, 52
            for n in range(128):
                if n == TABLES_AT:
                    dve.wait_ge(s_c4, 48)
                    link(V.tensor_copy(POSB[:, :], POSB[:, :].bitcast(I32)))
                    link(V.tensor_copy(SELB[:, :], SEL[:, :]))
                    for t in range(STEPQ):
                        rows = slice(BUCKETS * t, BUCKETS * (t + 1))
                        link(V.tensor_scalar(THR[rows, :], POSB[rows, t:S:STEPQ], steps[rows, :], None, ALU.subtract))
                    for g in range(NSTEP):
                        at = slice(g * P, (g + 1) * P)
                        view = lambda t: t.rearrange("p (e c q) -> p e c q", e=2, q=QT)
                        link(V.tensor_tensor(view(DF[:, at]), view(REACHED[:, at]),
                                             DLT[:, :].rearrange("p (c e o) -> p e c o", e=2, o=1).broadcast_to([P, 2, 4, QT]),
                                             ALU.mult))
                    link(V.tensor_copy(DHI[:, :], DF[:, :]))
                    V.tensor_sub(DLO[:, :], DF[:, :], DHI[:, :].bitcast(F32)).then_inc(s_tpd, 1)
                if n == KEYS_AT:
                    dve.wait_ge(s_lg, 48)
                    V.tensor_copy(KHH[0:64, :], AKB[0:64, :]).then_inc(s_kparts, 1)
                    V.tensor_copy(KHH[64:P, :], AKB[0:64, :]).then_inc(s_kparts, 1)
                    dve.wait_ge(s_kparts, 2)
                    V.tensor_sub(KLO[0:64, :], AKB[0:64, :], KHH[0:64, :].bitcast(F32)).then_inc(s_kparts, 1)
                    steps_of(0)
                if n >= 64 and n + 1 < 128:
                    steps_of(n + 1 - 64)
                dve.wait_ge(s_lg, n + 1)
                w = P * (ATT[n][0] + 1)
                if n >= 2:
                    dve.wait_ge(s_exp, n - 1)
                V.reduce_max(NMX[:, n % 2:n % 2 + 1], bank(2 * (n % 2), 2)[:, 0:w], AX, negate=True).then_inc(s_nm, 1)
                if n:
                    inverse_sum(n - 1)
            inverse_sum(127)
            for k in range(KC):
                low(chunk(YA, k) if k < 4 else chunk(YB, k - 4), k, M2.hi - 3 * KC)
            for m in range(8):
                w = BR0 + m
                dve.wait_ge(s_mm, w + 1)
                dve.wait_ge(s_g[m % 4], 16 * (m // 4 + 1))
                dst = chunk(Y, 2 * (m // 2), 2)
                psum = bank(w_bank(w), 4)
                if m % 2 == 0:
                    V.tensor_mul(dst, psum, GB[m % 4][:, :]).then_inc(s_evv, 1)
                else:
                    link(V.tensor_mul(MT[:, :], psum, GB[m % 4][:, :]))
                    dve.wait_ge(s_evv, reads(w - 1)[1])
                    V.tensor_add(dst, dst, MT[:, :]).then_inc(s_evv, 1)
            for k in range(KC):
                low(chunk(Y, k), k, M2.hi - 2 * KC)
            dve.wait_ge(s_xr, 32)
            for i in range(9):
                w = OUT0 + i
                if i < 8:
                    dve.wait_ge(s_mm, w + 1)
                    V.tensor_add(chunk(X, i), chunk(X, i), bank(w_bank(w), 2)).then_inc(s_evv, 1)
                if i:
                    dve.wait_ge(s_hi, M2.hi - KC + i)
                    V.scalar_tensor_tensor(chunk(A2L, i - 1), chunk(X, i - 1), vcol("mlp_norm_g_2", i - 1),
                                           chunk(A2H, i - 1).bitcast(F32), ALU.mult, ALU.subtract).then_inc(s_lo, 1)
                    add_square(5 * KC + i - 1)

            def last_sum(c):
                dst = chunk(F2SUM, 2 * c, 2)
                dve.wait_ge(s_evv, M2.dve + 4 * (GROUPS - 1) + c + 1)
                if c == 0:
                    dve.wait_ge(s_mm, M2.w + 8 * GROUPS - 4)
                    dve.wait_ge(s_rs2, 1)
                for k in (2 * c, 2 * c + 1):
                    V.tensor_tensor(chunk(F2SUM, k), chunk(F2SUM, k), RS2[:, :], ALU.mult).then_inc(s_f2, 1)
                dve.wait_ge(s_f2, 2 * c + 2)
                V.tensor_add(chunk(X, 2 * c, 2), chunk(X, 2 * c, 2), dst).then_inc(s_x2, 1)
                dve.wait_ge(s_x2, c + 1)
                for k in (2 * c, 2 * c + 1):
                    V.tensor_scalar(chunk(XG, k), chunk(X, k), vcol("final_norm_g_2", k), None, ALU.mult).then_inc(s_fin, 1)

            mlp_dve(M2, F2SUM, F2H, F2L, 6 * KC, {1: lambda: recip(11)}, last_sum)
            recip(12)
            dve.wait_ge(s_rs, 13)
            for t in range(1, NB, 2):
                dve.wait_ge(s_ft, t + 1)
                if t >= 4:
                    dve.wait_ge(s_out[t % 4], 16 * (t // 4))
                V.tensor_scalar(OT[t % 4][:, :], bank(2 * ((t + 3) % 4), 2), RS[:, t:t + 1], None, ALU.mult).then_inc(s_fo[1], 1)


_MATRICES = ["w_ada", "w_in", "w_out", "w_fc1", "w_fc2", "w_in_2", "w_uq_2", "w_ukv_2", "w_branch_a_2", "w_branch_b_2",
             "w_out_2", "w_ff1_2", "w_ff2_2"]


def kernel(**inputs):
    import numpy as _np
    import concourse.bacc as _bacc
    from concourse import mybir as _mybir
    from concourse.bass_utils import run_bass_kernel_spmd as _run

    given = {name: _np.ascontiguousarray(a) for name, a in inputs.items()}
    arrays = {"x": given["x"].reshape(S, D), "positions": given["positions"].reshape(1, S)}
    for name in _MATRICES:
        arrays[name] = given[name].reshape(given[name].shape[-2:])
    arrays["positions_2"] = given["positions_2"].reshape(1, S)
    arrays["rel_bias_2"] = given["rel_bias_2"]
    arrays["vec"] = _np.concatenate([given[name].reshape(-1, P) for name, _ in VEC_A + VEC_B])
    arrays["const"] = CONST

    nc = _bacc.Bacc("TRN2", target_bir_lowering=False, num_devices=1)
    args = {n: nc.dram_tensor(n, a.shape, _mybir.dt.from_np(a.dtype), kind="ExternalInput").ap()
            for n, a in arrays.items()}
    args["out"] = nc.dram_tensor("out", (S, D), _mybir.dt.float32, kind="ExternalOutput").ap()
    build(nc, **args)
    result = _run(nc, [arrays], core_ids=[0])
    return result.results[0]["out"].reshape(1, S, D)
```
